# Optimizing a Trainium2 kernel written in Bass

```python
import jax, jax.numpy as jnp
from jax import lax
import numpy as np

D_MODEL = 1024
BATCH = 1
SEQ = 256
DEPTH = 2

HEAD_DIM = 64
N_MIXERS = 4
GROUP_WIDTH = D_MODEL // N_MIXERS
N_GROUP_HEADS = GROUP_WIDTH // HEAD_DIM
MIX_WIDTH = N_MIXERS * GROUP_WIDTH
CMP_LEN = 32
CMP_STRIDE = 16
CMP_HIDDEN = 2 * HEAD_DIM
SEL_BLOCK = 64
SEL_TOPK = 16
WINDOW = 512
Q_BLOCK = 128
N_BRANCH = 3
ROPE_THETA = 500000.0
ROPE_DIM = HEAD_DIM // 4
SGU_CHUNK = 128
POOL_WINDOWS = (2, 4, 8, 16)
POOL_GROUP = GROUP_WIDTH // len(POOL_WINDOWS)
CONV_WIDTH = 3
D_FF = 3584
N_EXPERTS = 8
TOP_K = 2
N_DENSE = (DEPTH + 1) // 2
N_MOE = DEPTH // 2
EPS = 1e-6
NEG_INF = -1e30
IN_SIZES = (GROUP_WIDTH,) + (HEAD_DIM,) * 6 + (N_BRANCH * N_GROUP_HEADS,) + (GROUP_WIDTH,) * 6
D_IN = sum(IN_SIZES)

kernel_name = "hybrid_nsa_sgu_pool_conv_moe"

def rms_norm(x, g):
    xf = x.astype(jnp.float32)
    y = xf * lax.rsqrt(jnp.mean(xf * xf, axis=-1, keepdims=True) + EPS)
    return (y * g.astype(jnp.float32)).astype(x.dtype)

def apply_partial_rope(x, pos):
    half = ROPE_DIM // 2
    inv_freq = ROPE_THETA ** (-jnp.arange(half, dtype=jnp.float32) / half)
    ang = pos.astype(jnp.float32)[..., None] * inv_freq
    cos, sin = jnp.cos(ang), jnp.sin(ang)
    xr = x[..., :ROPE_DIM].astype(jnp.float32)
    x1, x2 = xr[..., :half], xr[..., half:]
    rot = jnp.concatenate([x1 * cos - x2 * sin, x1 * sin + x2 * cos], axis=-1).astype(x.dtype)
    return jnp.concatenate([rot, x[..., ROPE_DIM:]], axis=-1)

def compress_blocks(t, pe, w1, w2):
    b, s, d = t.shape
    c = t.reshape(b, s // CMP_STRIDE, CMP_STRIDE, d)
    blocks = jnp.concatenate([c[:, :-1], c[:, 1:]], axis=2) + pe
    hid = jax.nn.gelu(blocks.reshape(b, -1, CMP_LEN * d) @ w1)
    return hid @ w2

def nsa_mixer(q, k_cmp, v_cmp, k_sel, v_sel, k_win, v_win, gates, q_g, k_g, cmp_pe, cmp_w1, cmp_w2):
    b, s, _ = q.shape
    h, d = N_GROUP_HEADS, HEAD_DIM
    scale = d ** -0.5
    pos = jnp.arange(s)
    q = apply_partial_rope(rms_norm(q.reshape(b, s, h, d), q_g), pos[:, None])

    nc = s // CMP_STRIDE - 1
    cmp_end = jnp.arange(nc) * CMP_STRIDE + CMP_LEN - 1
    kc = apply_partial_rope(rms_norm(compress_blocks(k_cmp, cmp_pe[0], cmp_w1[0], cmp_w2[0]), k_g[0]), cmp_end)
    vc = compress_blocks(v_cmp, cmp_pe[1], cmp_w1[1], cmp_w2[1])
    s_c = jnp.einsum("bshd,bnd->bhsn", q, kc, preferred_element_type=jnp.float32) * scale
    valid_c = cmp_end[None, :] <= pos[:, None]
    p_c = jax.nn.softmax(jnp.where(valid_c, s_c, NEG_INF), axis=-1) * valid_c
    o_c = jnp.einsum("bhsn,bnd->bshd", p_c.astype(vc.dtype), vc)

    nb = s // SEL_BLOCK
    cs = jnp.arange(nc) * CMP_STRIDE
    bs = jnp.arange(nb) * SEL_BLOCK
    overlap = jnp.clip(jnp.minimum(cs[:, None] + CMP_LEN, bs[None, :] + SEL_BLOCK)
                       - jnp.maximum(cs[:, None], bs[None, :]), 0, None).astype(jnp.float32) / CMP_LEN
    imp = jnp.einsum("bhsn,nj->bsj", p_c, overlap)
    cur = pos // SEL_BLOCK
    blk = jnp.arange(nb)
    valid_b = blk[None, :] <= cur[:, None]
    forced = (blk[None, :] == 0) | (blk[None, :] == cur[:, None]) | (blk[None, :] == cur[:, None] - 1)
    score = jnp.where(valid_b & forced, 1e4, jnp.where(valid_b, imp, -1.0))
    n_sel = min(SEL_TOPK, nb)
    top_val, sel_idx = lax.top_k(score, n_sel)
    sel_ok = top_val >= 0.0

    k_sel = apply_partial_rope(rms_norm(k_sel, k_g[1]), pos)
    k_win = apply_partial_rope(rms_norm(k_win, k_g[2]), pos)
    kb_sel = k_sel.reshape(b, nb, SEL_BLOCK, d)
    vb_sel = v_sel.reshape(b, nb, SEL_BLOCK, d)
    kpad = jnp.pad(k_win, ((0, 0), (WINDOW, 0), (0, 0)))
    vpad = jnp.pad(v_win, ((0, 0), (WINDOW, 0), (0, 0)))
    nq = s // Q_BLOCK

    def to_blocks(a):
        return a.reshape((b, nq, Q_BLOCK) + a.shape[2:]).swapaxes(0, 1)

    def block_fn(args):
        qb, idx, ok, qi = args
        s0 = qi * Q_BLOCK
        tq = s0 + jnp.arange(Q_BLOCK)
        ks = jax.vmap(lambda kb, ix: kb[ix])(kb_sel, idx).reshape(b, Q_BLOCK, n_sel * SEL_BLOCK, d)
        vs = jax.vmap(lambda vb, ix: vb[ix])(vb_sel, idx).reshape(b, Q_BLOCK, n_sel * SEL_BLOCK, d)
        kpos = idx[..., None] * SEL_BLOCK + jnp.arange(SEL_BLOCK)
        m_s = ((kpos <= tq[None, :, None, None]) & ok[..., None]).reshape(b, Q_BLOCK, n_sel * SEL_BLOCK)
        ss = jnp.einsum("bqhd,bqkd->bhqk", qb, ks, preferred_element_type=jnp.float32) * scale
        ps = jax.nn.softmax(jnp.where(m_s[:, None], ss, NEG_INF), axis=-1)
        o_s = jnp.einsum("bhqk,bqkd->bqhd", ps.astype(vs.dtype), vs)
        kw = lax.dynamic_slice_in_dim(kpad, s0, WINDOW + Q_BLOCK, axis=1)
        vw = lax.dynamic_slice_in_dim(vpad, s0, WINDOW + Q_BLOCK, axis=1)
        kp = s0 - WINDOW + jnp.arange(WINDOW + Q_BLOCK)
        m_w = (kp[None, :] <= tq[:, None]) & (kp[None, :] > tq[:, None] - WINDOW) & (kp[None, :] >= 0)
        sw = jnp.einsum("bqhd,bkd->bhqk", qb, kw, preferred_element_type=jnp.float32) * scale
        pw = jax.nn.softmax(jnp.where(m_w, sw, NEG_INF), axis=-1)
        o_w = jnp.einsum("bhqk,bkd->bqhd", pw.astype(vw.dtype), vw)
        return o_s, o_w

    o_s, o_w = lax.map(block_fn, (to_blocks(q), to_blocks(sel_idx), to_blocks(sel_ok), jnp.arange(nq)))
    o_s = o_s.swapaxes(0, 1).reshape(b, s, h, d)
    o_w = o_w.swapaxes(0, 1).reshape(b, s, h, d)
    o = gates[..., 0:1] * o_c + gates[..., 1:2] * o_s + gates[..., 2:3] * o_w
    return o.reshape(b, s, GROUP_WIDTH)

def sgu_mixer(u, v, g, w_s, b_s):
    b, s, _ = u.shape
    vn = rms_norm(v, g).reshape(b, s // SGU_CHUNK, SGU_CHUNK, N_GROUP_HEADS, HEAD_DIM)
    w_m = w_s * jnp.tril(jnp.ones((SGU_CHUNK, SGU_CHUNK), w_s.dtype))
    mixed = jnp.einsum("gts,bcsgd->bctgd", w_m, vn) + b_s.T[:, :, None]
    return u * mixed.reshape(b, s, GROUP_WIDTH)

def pool_mixer(p, w, scale):
    b, s, _ = p.shape
    pf = p.astype(jnp.float32)
    csum = jnp.pad(jnp.cumsum(pf, axis=1), ((0, 0), (1, 0), (0, 0)))
    t = jnp.arange(s)
    outs = []
    for gi, win in enumerate(POOL_WINDOWS):
        c0, c1 = gi * POOL_GROUP, (gi + 1) * POOL_GROUP
        lo = jnp.maximum(t + 1 - win, 0)
        cnt = jnp.minimum(t + 1, win).astype(jnp.float32)
        mean = (csum[:, 1:, c0:c1] - csum[:, lo, c0:c1]) / cnt[None, :, None]
        outs.append(mean - pf[..., c0:c1])
    dlt = jnp.stack(outs, axis=2).astype(p.dtype)
    y = jnp.einsum("bsgc,gcd->bsgd", dlt, w).reshape(b, s, GROUP_WIDTH)
    return y * scale

def shortconv_mixer(bg, cg, hin, w):
    z = cg * hin
    y = lax.conv_general_dilated(z, w[:, None, :].astype(z.dtype), window_strides=(1,),
                                 padding=[(CONV_WIDTH - 1, 0)],
                                 dimension_numbers=("NWC", "WIO", "NWC"),
                                 feature_group_count=z.shape[-1])
    return bg * y

def hybrid_mixer(hn, w_in, q_g, k_g, cmp_pe, cmp_w1, cmp_w2, sgu_g, sgu_w, sgu_b,
                 pool_w, pool_s, conv_w, out_g, w_out):
    b, s, _ = hn.shape
    offs, acc = [], 0
    for sz in IN_SIZES[:-1]:
        acc += sz
        offs.append(acc)
    proj = hn @ w_in
    (q, kc, vc, ks, vs, kw, vw, gt, u, v, pin, bg, cg, hin) = jnp.split(proj, offs, axis=-1)
    gates = jax.nn.sigmoid(gt.astype(jnp.float32)).reshape(b, s, N_GROUP_HEADS, N_BRANCH, 1).astype(hn.dtype)
    gates = gates[..., 0]
    ya = nsa_mixer(q, kc, vc, ks, vs, kw, vw, gates, q_g, k_g, cmp_pe, cmp_w1, cmp_w2)
    yb = sgu_mixer(u, v, sgu_g, sgu_w, sgu_b)
    yc = pool_mixer(pin, pool_w, pool_s)
    yd = shortconv_mixer(bg, cg, hin, conv_w)
    ys = jnp.stack([ya, yb, yc, yd], axis=2)
    y = rms_norm(ys, out_g.reshape(N_MIXERS, GROUP_WIDTH)).reshape(b, s, MIX_WIDTH)
    return y @ w_out

def swiglu(x, w1, w3, w2):
    return (jax.nn.silu(x @ w1) * (x @ w3)) @ w2

def moe_swiglu(x, router, w1, w3, w2):
    logits = (x @ router).astype(jnp.float32)
    top_v, top_i = lax.top_k(logits, TOP_K)
    top_w = jax.nn.softmax(top_v, axis=-1)
    gate = jnp.sum(jax.nn.one_hot(top_i, N_EXPERTS, dtype=jnp.float32) * top_w[..., None], axis=-2).astype(x.dtype)
    out = jnp.zeros_like(x)
    for e in range(N_EXPERTS):
        out = out + gate[..., e:e + 1] * swiglu(x, w1[e], w3[e], w2[e])
    return out

def setup_inputs(seed: int = 0) -> dict:
    key = jax.random.key(seed)
    ks = jax.random.split(key, 32)
    f32 = jnp.float32
    nrm = lambda k, shape, sc: jax.random.normal(k, shape, f32) * sc
    gain = lambda k, shape: 1.0 + 0.05 * jax.random.normal(k, shape, f32)
    return {
        "x": jax.random.normal(ks[0], (BATCH, SEQ, D_MODEL), f32),
        "attn_norm_g": gain(ks[1], (DEPTH, D_MODEL)),
        "w_in": nrm(ks[2], (DEPTH, D_MODEL, D_IN), D_MODEL ** -0.5),
        "q_norm_g": gain(ks[3], (DEPTH, HEAD_DIM)),
        "k_norm_g": gain(ks[4], (DEPTH, N_BRANCH, HEAD_DIM)),
        "cmp_pe": nrm(ks[5], (DEPTH, 2, CMP_LEN, HEAD_DIM), 0.1),
        "cmp_w1": nrm(ks[6], (DEPTH, 2, CMP_LEN * HEAD_DIM, CMP_HIDDEN), (CMP_LEN * HEAD_DIM) ** -0.5),
        "cmp_w2": nrm(ks[7], (DEPTH, 2, CMP_HIDDEN, HEAD_DIM), CMP_HIDDEN ** -0.5),
        "sgu_norm_g": gain(ks[8], (DEPTH, GROUP_WIDTH)),
        "sgu_w": nrm(ks[9], (DEPTH, N_GROUP_HEADS, SGU_CHUNK, SGU_CHUNK), 0.5 * SGU_CHUNK ** -0.5),
        "sgu_b": gain(ks[10], (DEPTH, N_GROUP_HEADS, SGU_CHUNK)),
        "pool_w": nrm(ks[11], (DEPTH, len(POOL_WINDOWS), POOL_GROUP, POOL_GROUP), POOL_GROUP ** -0.5),
        "pool_scale": 1.0 + 0.1 * jax.random.normal(ks[12], (DEPTH, GROUP_WIDTH), f32),
        "conv_w": nrm(ks[13], (DEPTH, CONV_WIDTH, GROUP_WIDTH), CONV_WIDTH ** -0.5),
        "mix_out_norm_g": gain(ks[14], (DEPTH, MIX_WIDTH)),
        "w_out": nrm(ks[15], (DEPTH, MIX_WIDTH, D_MODEL), MIX_WIDTH ** -0.5),
        "ffn_norm_g": gain(ks[16], (DEPTH, D_MODEL)),
        "ffn_w1": nrm(ks[17], (N_DENSE, D_MODEL, D_FF), D_MODEL ** -0.5),
        "ffn_w3": nrm(ks[18], (N_DENSE, D_MODEL, D_FF), D_MODEL ** -0.5),
        "ffn_w2": nrm(ks[19], (N_DENSE, D_FF, D_MODEL), D_FF ** -0.5),
        "router_w": nrm(ks[20], (N_MOE, D_MODEL, N_EXPERTS), D_MODEL ** -0.5),
        "expert_w1": nrm(ks[21], (N_MOE, N_EXPERTS, D_MODEL, D_FF), D_MODEL ** -0.5),
        "expert_w3": nrm(ks[22], (N_MOE, N_EXPERTS, D_MODEL, D_FF), D_MODEL ** -0.5),
        "expert_w2": nrm(ks[23], (N_MOE, N_EXPERTS, D_FF, D_MODEL), D_FF ** -0.5),
    }

def reference(x, attn_norm_g, w_in, q_norm_g, k_norm_g, cmp_pe, cmp_w1, cmp_w2, sgu_norm_g, sgu_w,
              sgu_b, pool_w, pool_scale, conv_w, mix_out_norm_g, w_out, ffn_norm_g, ffn_w1, ffn_w3,
              ffn_w2, router_w, expert_w1, expert_w3, expert_w2):
    for layer in range(DEPTH):
        hn = rms_norm(x, attn_norm_g[layer])
        x = x + hybrid_mixer(hn, w_in[layer], q_norm_g[layer], k_norm_g[layer], cmp_pe[layer],
                             cmp_w1[layer], cmp_w2[layer], sgu_norm_g[layer], sgu_w[layer],
                             sgu_b[layer], pool_w[layer], pool_scale[layer], conv_w[layer],
                             mix_out_norm_g[layer], w_out[layer])
        hn = rms_norm(x, ffn_norm_g[layer])
        i = layer // 2
        if layer % 2 == 0:
            x = x + swiglu(hn, ffn_w1[i], ffn_w3[i], ffn_w2[i])
        else:
            x = x + moe_swiglu(hn, router_w[i], expert_w1[i], expert_w3[i], expert_w2[i])
    return x


_drawn_inputs = setup_inputs


def setup_inputs(seed=0):
    import zlib

    import numpy as np

    out = dict(_drawn_inputs(seed))
    spreads = {}
    factors = {'sgu_norm_g': 3.888}
    for name, (base, spread) in spreads.items():
        noise = np.random.default_rng([zlib.crc32(name.encode()), seed]).standard_normal(out[name].shape)
        drawn = base * np.exp(spread * noise) if base else spread * noise
        out[name] = __import__('jax').numpy.asarray(drawn.astype(out[name].dtype))
    for name, factor in factors.items():
        out[name] = (out[name] * factor).astype(out[name].dtype)
    return out
```

```python
from contextlib import ExitStack

import numpy as np

import concourse.bass as bass
from concourse import mybir

F32 = mybir.dt.float32
F32R = mybir.dt.float32r
I32 = mybir.dt.int32
ALU = mybir.AluOpType
ACT = mybir.ActivationFunctionType
AX_X = mybir.AxisListType.X
ds = bass.ds

P = 128
D = 1024
KC = D // P
S = 256
NT = S // P
HD = 64
NH = 4
GW = 256
DEPTH = 2
D_IN = 2188
FF = 3584
NE = 8
EPS = 1e-6
NEG = -1e30
NCMP = S // 16 - 1
CP = 32
THETA = 500000.0
POOLS = (2, 4, 8, 16)
Q0, KCM, KS, VS, KW, VW, GT, U0, V0, PIN, BG, CG, HIN = 0, 256, 384, 448, 512, 576, 640, 652, 908, 1164, 1420, 1676, 1932
FB = 512
NFB = FF // FB
UW = 2048
RAW = 6
SPL = 3
W_IN_UNITS = 9
W_OUT_UNITS = 4
FFN_UNITS = 6 * NFB
SLOTS = 128
GELU_C = 0.7978845608028654


def const_layout():
    at, out = 0, {}
    for name, n in (("ident", P), ("band", 12 * P), ("shift", 4 * P), ("causal", P), ("triu", P),
                    ("before", P), ("ones", P), ("iota", P), ("cos", NT * 8), ("sin", NT * 8),
                    ("ccos", 8), ("csin", 8), ("cmask", NT * CP), ("cvalid", NT * CP), ("blk", NH),
                    ("mhalf", 8)):
        out[name] = (at, n)
        at += n
    return out, at


def const_table():
    lay, width = const_layout()
    c = np.zeros((P, width), np.float32)

    def put(name, a):
        at, n = lay[name]
        a = np.asarray(a, np.float32).reshape(a.shape[0], -1)
        c[:a.shape[0], at:at + n] = a

    r = np.arange(P)
    put("ident", np.eye(P))
    t = np.arange(S)
    bands = []
    for win in POOLS:
        b = ((t[:, None] <= t[None, :]) & (t[:, None] > t[None, :] - win)) / np.minimum(t + 1, win)[None, :].astype(np.float32)
        bands.append(b.astype(np.float32) - np.eye(S, dtype=np.float32))
    bands = np.stack(bands, 1)
    put("band", np.stack([bands[:P, :, :P], bands[:P, :, P:], bands[P:, :, P:]], 1))
    put("shift", np.stack([r[None, :] == r[:, None] + 1, r[None, :] == r[:, None] + 2,
                           r[None, :] + P == r[:, None] + 1, r[None, :] + P == r[:, None] + 2], 1))
    put("causal", np.where(r[None, :] <= r[:, None], 0.0, NEG))
    put("triu", r[:, None] <= r[None, :])
    put("before", r[:, None] < r[None, :])
    put("ones", np.ones((P, P)))
    put("iota", np.tile(r[None, :], (P, 1)))
    inv = (THETA ** (-np.arange(8, dtype=np.float32) / 8)).astype(np.float32)
    ang = (t.astype(np.float32)[:, None] * inv).reshape(NT, P, 8).transpose(1, 0, 2)
    put("cos", np.cos(ang))
    put("sin", np.sin(ang))
    end = (np.arange(CP) * 16 + 31).astype(np.float32)
    put("ccos", np.cos(end[:, None] * inv))
    put("csin", np.sin(end[:, None] * inv))
    ok = (end[None, :] <= t[:, None]) & (np.arange(CP) < NCMP)[None, :]
    ok = ok.reshape(NT, P, CP).transpose(1, 0, 2)
    put("cmask", np.where(ok, 0.0, NEG))
    put("cvalid", ok)
    put("blk", r[:, None] // CP == np.arange(NH)[None, :])
    put("mhalf", np.full((P, 8), -0.5))
    return c


def spread(ap, axis, n):
    shape = list(ap.shape)
    shape[axis] = n
    return ap.broadcast_to(shape)


def bc(ap, axis, n):
    return spread(ap.unsqueeze(axis), axis, n)


def build(nc, x_in, attn_norm_g, w_in, q_norm_g, k_norm_g, cmp_pe, cmp_w1, cmp_w2, sgu_norm_g, sgu_w, sgu_b,
          pool_w, pool_scale, conv_w, mix_out_norm_g, w_out, ffn_norm_g, ffn_w1, ffn_w3, ffn_w2,
          router_w, expert_w1, expert_w3, expert_w2, consts, out):
    lay, cwidth = const_layout()
    ctx = ExitStack()
    with ctx:
        def sb(name, shape, dt=F32):
            return ctx.enter_context(nc.sbuf_tensor(name, shape, dt))

        def sem(name):
            return ctx.enter_context(nc.semaphore(name))

        raw = [sb(f"raw{i}", [P, UW]) for i in range(RAW)]
        whi = [sb(f"whi{i}", [P, UW], F32R) for i in range(SPL)]
        wlo = [sb(f"wlo{i}", [P, UW], F32R) for i in range(SPL)]
        ct = sb("ct", [P, cwidth])
        x = sb("x", [P, NT, D])
        xn = sb("xn", [P, NT, D])
        xTh = sb("xTh", [P, KC, S], F32R)
        xTl = sb("xTl", [P, KC, S], F32R)
        pr = sb("pr", [P, NT, D_IN])
        gains = sb("gains", [P, 6, KC])
        g6 = sb("g6", [P, 6, HD])
        gkc = sb("gkc", [P, HD])
        gsgu = sb("gsgu", [P, GW])
        psc = sb("psc", [P, GW])
        cw = sb("cw", [P, 3, GW])
        sgb = sb("sgb", [P, NH])
        sgw = pr[:, 0, 0:NH * P].rearrange("p (g s) -> p g s", g=NH)
        sgT = sb("sgT", [P, NH, P])
        pw = sb("pw", [P, NH, HD])
        big = sb("big", [P, 4096])
        w1c = big[:, :].rearrange("p (k a n) -> p k a n", k=2, a=16)
        w2c = sb("w2c", [P, 2, HD])
        peT = sb("peT", [P, 2, 16])
        rt = sb("rt", [P, KC, NE])
        ssx = sb("ssx", [P, NT])
        rsx = sb("rsx", [P, NT])
        ss = sb("ss", [P, NT, 8])
        rs = sb("rs", [P, NT, 8])
        ssc = sb("ssc", [CP, 1])
        rsc = sb("rsc", [CP, 1])
        ssy = sb("ssy", [P, NT, NH])
        rsy = sb("rsy", [P, NT, NH])
        kd = xn[:, :, 2 * GW:3 * GW].rearrange("p t (j a d) -> p t j a d", j=2, a=2)
        zk = [xn[:, :, 0:GW], xn[:, :, GW:2 * GW], xn[:, :, 3 * GW:4 * GW]]
        tmp = sb("tmp", [P, NT, 6, HD])
        qk = sb("qk", [P, NT, 6, HD])
        rp = [xn[:, :, 2 * GW + 48 * i:2 * GW + 48 * (i + 1)].rearrange("p t (h f) -> p t h f", h=6) for i in range(4)]
        qT = pr[0:HD, :, CG:CG + 2 * GW].rearrange("p t (i s) -> p t i s", i=2)
        dlt = pr[HD:P, :, CG:CG + 2 * GW].rearrange("p t (i s) -> p t i s", i=2)
        kT = sb("kT", [HD, 2, S])
        vn = tmp[:].rearrange("p t h d -> p t (h d)")[:, :, 0:GW]
        kvb = sb("kvb", [P, 2, 16, 16])
        hx = sb("hx", [P, 2, NCMP])
        hy = sb("hy", [P, 2, NCMP])
        hz = sb("hz", [P, 2, NCMP])
        hidp = sb("hidp", [P, 2, NH, CP])
        kcs = sb("kcs", [CP, 3, HD])
        krp = sb("krp", [CP, 4, 8])
        kcT = sb("kcT", [HD, CP])
        vbd = sb("vbd", [P, NH, HD])
        gates = sb("gates", [P, NT, NH, 3])
        sc = big[:, 0:2048].rearrange("p (i h s) -> p i h s", i=2, h=NH)
        scc = big[:, 3072:3328].rearrange("p (t h n) -> p t h n", t=NT, h=NH)
        mx = sb("mx", [P, 4, NH])
        sm = sb("sm", [P, 4, NH])
        cf = sb("cf", [P, 4, NH])
        mxc = sb("mxc", [P, NT, NH])
        smc = sb("smc", [P, NT, NH])
        pT = big[:, 2048:3072].rearrange("p (k h q) -> p k h q", k=2, h=NH)
        pcT = big[:, 3328:3584].rearrange("p (t q) -> p t q", t=NT)
        ot = big[:, 3584:3840]
        junk = qk[:, 0].rearrange("p h d -> p (h d)")[:, 0:GW]
        sg = pr[:, 1, 1024:2048].rearrange("p (t n) -> p t n", t=NT)
        gTh = sb("gTh", [P, NT, 4, P], F32R)
        gTl = sb("gTl", [P, NT, 4, P], F32R)
        gbc = pr[:, 0, 0:D]
        rhl = sb("rhl", [P, 2, KC, NE], F32R)
        lg = sb("lg", [P, NT, NE])
        top = sb("top", [P, NT, 8])
        sel = sb("sel", [P, NT, NE])
        ra = sb("ra", [P, NT, NE])
        rb = sb("rb", [P, NT, NE])
        rsc1 = sb("rsc1", [P, NT])
        gate = sb("gate", [P, NT, NE])
        posm = sb("posm", [P, NT, NE])
        cnt = sb("cnt", [P, 2])
        flag = sb("flag", [P, 1], I32)
        yg = pr[:, 0, 0:D]
        onehot = pr[:, 1, 0:NT * SLOTS].rearrange("p (t s) -> p t s", t=NT)
        onehotT = pr[:, 1, 256:512]
        xgh = xTh[:, :, 0:SLOTS]
        xgl = xTl[:, :, 0:SLOTS]
        zero = sb("zero", [P, P], F32R)

        bank = [ctx.enter_context(nc.psum_tensor(f"bank{i}", [P, 512], F32)) for i in range(8)]

        def C(name, rows=P):
            at, n = lay[name]
            return ct[0:rows, at:at + n]

        ident = C("ident")

        s_const, s_x, s_small, s_lay = sem("const_in"), sem("x_in"), sem("small_in"), [sem("layer_in0"), sem("layer_in1")]
        s_gbc, s_rt = sem("ffn_gain_in"), sem("router_in")
        landed = [sem(f"landed{i}") for i in range(RAW)]
        s_hi, s_lo, used = sem("unit_hi"), sem("unit_lo"), sem("unit_used")
        x_sq, x_rstd, xn_ready = sem("x_sq"), sem("x_rstd"), sem("xn_ready")
        xT_psum, xTh_ready, xTl_ready = sem("xT_psum"), sem("xTh_ready"), sem("xTl_ready")
        pr_ready = sem("proj_ready")
        sguT_psum, sguT_ready = sem("sguT_psum"), sem("sguT_ready")
        kd_ready, kdT_psum, kvb_ready = sem("kd_ready"), sem("kdT_psum"), sem("kvb_ready")
        hid_psum, gelu_in, gelu_e, hid_ready = sem("hid_psum"), sem("gelu_in"), sem("gelu_exp"), sem("hid_ready")
        kcvc_psum, kc_ss, kc_rstd, kc_ready = sem("kcvc_psum"), sem("kc_ss"), sem("kc_rstd"), sem("kc_ready")
        kcT_psum, kcT_ready, vbd_ready = sem("kcT_psum"), sem("kcT_ready"), sem("vbd_ready")
        z_ready, qk_ss, v_ss, qk_rstd = sem("z_ready"), sem("qk_ss"), sem("v_ss"), sem("qk_rstd")
        qk_ready, vn_ready = sem("qk_ready"), sem("vn_ready")
        qkT_psum, qkT_ready = sem("qkT_psum"), sem("qkT_ready")
        dlt_psum, dlt_ready, poolY_psum = sem("dlt_psum"), sem("dlt_ready"), sem("poolY_psum")
        conv_psum, sgu_psum, mix_done = sem("conv_psum"), sem("sgu_psum"), sem("mix_evacuated")
        gate_e = sem("gate_exp")
        cs_psum, cs_in, cs_exp, cs_ready = sem("cmp_scores"), sem("cmp_masked"), sem("cmp_exp"), sem("cmp_probs")
        cT_psum, cT_ready, co_psum, co_done = sem("cmpT_psum"), sem("cmpT_ready"), sem("cmp_out"), sem("cmp_out_used")
        a_s, a_max, a_exp = sem("scores"), sem("score_max"), sem("probs")
        a_T, a_Tr, a_o, a_done = sem("probsT"), sem("probsT_copied"), sem("attn_out"), sem("attn_out_used")
        y_sq, y_rstd, yn_ready = sem("y_sq"), sem("y_rstd"), sem("yn_ready")
        x_mid = sem("x_plus_mixer")
        silu_done, g_ready, gT_psum, gTh_ready, gTl_ready = (sem("silu_done"), sem("g_ready"), sem("gT_psum"),
                                                             sem("gTh_ready"), sem("gTl_ready"))
        y_added, x_ffn = sem("dense_y_added"), sem("x_plus_dense")
        rh_ready, lg_psum, lg_ready, lg_exp = sem("router_split"), sem("logits_psum"), sem("top2_in"), sem("top2_exp")
        sel_ready, pos_psum, route_ready = sem("sel_ready"), sem("pos_psum"), sem("route_ready")
        zero_ready, hp_ready, g6_ready = sem("zero_ready"), sem("hidp_zeroed"), sem("g6_scaled")
        oh_ready, xg_psum, xgh_ready, xgl_ready = sem("onehot"), sem("gathered"), sem("xgh_ready"), sem("xgl_ready")
        ohT_psum, ohT_ready, yg_ready, sc_psum, sc_done = (sem("onehotT_psum"), sem("onehotT"), sem("yg_ready"),
                                                           sem("scattered"), sem("scatter_added"))
        dve_order, pool_order = sem("dve_order"), sem("pool_order")
        s_done, s_out = sem("x_final"), sem("out_stored")

        WIN = [0, W_IN_UNITS + W_OUT_UNITS + FFN_UNITS]
        WOUT = [n + W_IN_UNITS for n in WIN]
        DENSE = WOUT[0] + W_OUT_UNITS
        MOE = WOUT[1] + W_OUT_UNITS
        MOE2 = MOE + NE * FFN_UNITS
        LAY_LOADED = 16 * 17

        class Unit:

            def __init__(self, base, rounds=0, slots_ahead=0):
                self.base, self.rounds, self.ahead = base, rounds, slots_ahead
                self.raw = raw[base % RAW]
                self.landed = landed[base % RAW]
                self.hi, self.lo = whi[base % SPL], wlo[base % SPL]
                self.n = base + rounds
                self.turn = base // RAW + slots_ahead

        def load_unit(sp, u, src, words):
            if u.base >= RAW:
                sp.wait_ge(s_lo, u.n - RAW + 1)
            sp.dma_start(words(u.raw), src).then_inc(u.landed, 16)

        def round_unit(act, u, n=UW):
            act.wait_ge(u.landed, 16 * (u.turn + 1))
            if u.base >= SPL:
                act.wait_ge(used, u.n - SPL + 1)
            nc.scalar.activation(u.hi[:, 0:n], u.raw[:, 0:n], ACT.Copy).then_inc(s_hi, 1)

        def rest_unit(dve, u, n=UW):
            dve.wait_ge(s_hi, u.n + 1)
            nc.vector.tensor_tensor(u.lo[:, 0:n], u.raw[:, 0:n], u.hi[:, 0:n].bitcast(F32), ALU.subtract).then_inc(s_lo, 1)

        def in_words(n):
            return (4 * FB) if n < W_IN_UNITS - 1 else KC * (D_IN - 4 * FB)

        def three_passes(o, xh, xl, wh, wl, start, stop):
            nc.tensor.matmul(o, xh, wh, start=start, stop=False)
            nc.tensor.matmul(o, xh, wl, start=False, stop=False)
            return nc.tensor.matmul(o, xl, wh, start=False, stop=stop)

        block = ctx.enter_context(nc.Block())

        @block.sync
        def _(sp):
            sp.dma_start(x[:], x_in.rearrange("(t p) d -> p t d", p=P)).then_inc(s_x, 16)
            sp.dma_start(ct[:], consts).then_inc(s_const, 16)

            def mixer_weights(L):
                for n in range(W_IN_UNITS):
                    src = w_in[L].rearrange("(c p) n -> p c n", p=P)
                    if n < W_IN_UNITS - 1:
                        b, h = n // 2, n % 2
                        src = src[:, 4 * h:4 * h + 4, b * FB:(b + 1) * FB]
                        load_unit(sp, Unit(WIN[L] + n), src, lambda r: r[:, :].rearrange("p (c n) -> p c n", c=4))
                    else:
                        src = src[:, :, 4 * FB:D_IN]
                        load_unit(sp, Unit(WIN[L] + n), src,
                                  lambda r: r[:, 0:in_words(8)].rearrange("p (c n) -> p c n", c=KC))
                for n in range(W_OUT_UNITS):
                    b, h = n // 2, n % 2
                    src = w_out[L].rearrange("(c p) n -> p c n", p=P)[:, 4 * h:4 * h + 4, b * FB:(b + 1) * FB]
                    load_unit(sp, Unit(WOUT[L] + n), src, lambda r: r[:, :].rearrange("p (c n) -> p c n", c=4))

            def in_block(u0, rounds, turns, w1, w3, f):
                j = 0
                for w in (w1, w3):
                    for h in range(2):
                        src = w.rearrange("(c p) n -> p c n", p=P)[:, 4 * h:4 * h + 4, ds(f * FB, FB)]
                        load_unit(sp, Unit(u0 + j, rounds, turns), src,
                                  lambda r: r[:, :].rearrange("p (c n) -> p c n", c=4))
                        j += 1

            def out_block(u0, rounds, turns, w2, f):
                for h in range(2):
                    src = w2[ds(f * FB, FB), h * FB:(h + 1) * FB].rearrange("(c p) n -> p c n", p=P)
                    load_unit(sp, Unit(u0 + h, rounds, turns), src,
                              lambda r: r[:, :].rearrange("p (c n) -> p c n", c=4))

            def ffn_weights(base, rounds, turns, w1, w3, w2):
                in_block(base, rounds, turns, w1, w3, 0)
                with sp.Fori(1, NFB) as f:
                    in_block(base + 4, rounds + (f - 1) * 6, turns + (f - 1), w1, w3, f)
                    out_block(base + 8, rounds + (f - 1) * 6, turns + (f - 1), w2, f - 1)
                out_block(base + FFN_UNITS - 2, rounds, turns, w2, NFB - 1)

            def expert(w, e):
                return w[0, ds(e, 1)].rearrange("a k n -> (a k) n")

            mixer_weights(0)
            ffn_weights(DENSE, 0, 0, ffn_w1[0], ffn_w3[0], ffn_w2[0])
            mixer_weights(1)

            def experts(base):
                with sp.Fori(0, NE) as e:
                    ffn_weights(base, e * FFN_UNITS, e * (FFN_UNITS // RAW),
                                expert(expert_w1, e), expert(expert_w3, e), expert(expert_w2, e))

            experts(MOE)
            sp.wait_ge(route_ready, 1)
            more = sp.value_load(flag[0:1, 0:1], min_val=0, max_val=1)
            with sp.If(more > 0):
                experts(MOE2)
            sp.wait_ge(s_done, 1)
            sp.dma_start(out.rearrange("(t p) d -> p t d", p=P), x[:]).then_inc(s_out, 16)
            sp.wait_ge(s_out, 16)

        @block.gpsimd
        def _(pool):
            count = [0]

            def small(dst, src, s):
                pool.dma_start(dst, src, allow_slow_non_contiguous=True).then_inc(s, 16)

            def layer_weights(L):
                for k in range(2):
                    small(w1c[:, k], cmp_w1[L, k].rearrange("(a p) n -> p a n", p=P), s_lay[L])
                    small(w2c[:, k], cmp_w2[L, k], s_lay[L])
                    for h in range(2):
                        small(peT[h * HD:(h + 1) * HD, k, :], cmp_pe[L, k].rearrange("(a two) d -> two d a", two=2)[h],
                              s_lay[L])
                small(sgw[:], sgu_w[L].rearrange("g t s -> t g s"), s_lay[L])
                small(cw[:], spread(conv_w[L:L + 1], 0, P), s_lay[L])
                small(g6[:, 0:NH, :], spread(bc(q_norm_g[L:L + 1], 1, NH), 0, P), s_lay[L])
                small(g6[:, NH:NH + 2, :], spread(k_norm_g[L:L + 1, 1:3], 0, P), s_lay[L])
                small(gkc[:], spread(k_norm_g[L, 0:1], 0, P), s_lay[L])
                small(gsgu[:], spread(sgu_norm_g[L:L + 1], 0, P), s_lay[L])
                small(psc[:], spread(pool_scale[L:L + 1], 0, P), s_lay[L])
                small(sgb[:], sgu_b[L].rearrange("g t -> t g"), s_lay[L])
                small(pw[HD:P], pool_w[L].rearrange("g c d -> c g d"), s_lay[L])

            def rsqrt(outp, inp, n, wait, value, done):
                pool.wait_ge(wait, value)
                nc.gpsimd.tensor_scalar(inp, inp, 1.0 / n, EPS, ALU.mult, ALU.add).then_inc(pool_order, 1)
                count[0] += 1
                pool.wait_ge(pool_order, count[0])
                w = inp.shape[-1]
                nc.gpsimd.tensor_tensor(outp, inp, C("mhalf", inp.shape[0])[:, 0:w], ALU.pow).then_inc(done, 1)

            for L in range(DEPTH):
                for j, g in enumerate((attn_norm_g, mix_out_norm_g, ffn_norm_g)):
                    small(gains[:, 3 * L + j, :], g[L].rearrange("(c p) -> p c", p=P), s_small)
            layer_weights(0)
            small(rt[:], router_w[0].rearrange("(c p) e -> p c e", p=P), s_rt)
            pool.wait_ge(s_const, 16)
            for L in range(DEPTH):
                rsqrt(rsx[:], ssx[:], D, x_sq, 4 * L + 2, x_rstd)
                pool.wait_ge(v_ss, 2 * (L + 1))
                pool.wait_ge(qk_ss, L + 1)
                nc.gpsimd.tensor_scalar(ss[:, :, 0:6], ss[:, :, 0:6], 1.0 / HD, EPS, ALU.mult, ALU.add).then_inc(pool_order, 1)
                nc.gpsimd.tensor_scalar(ss[:, :, 6:7], ss[:, :, 6:7], 1.0 / GW, EPS, ALU.mult, ALU.add).then_inc(pool_order, 1)
                count[0] += 2
                pool.wait_ge(pool_order, count[0])
                for t in range(NT):
                    nc.gpsimd.tensor_tensor(rs[:, t, 0:7], ss[:, t, 0:7], C("mhalf")[:, 0:7], ALU.pow).then_inc(qk_rstd, 1)
                rsqrt(rsc[:], ssc[:], HD, kc_ss, L + 1, kc_rstd)
                rsqrt(rsy[:, 0, :], ssy[:, 0, :], GW, y_sq, 8 * L + 4, y_rstd)
                rsqrt(rsy[:, 1, :], ssy[:, 1, :], GW, y_sq, 8 * L + 8, y_rstd)
                if L == 0:
                    pool.wait_ge(yn_ready, 2)
                    layer_weights(1)
                rsqrt(rsx[:], ssx[:], D, x_sq, 4 * L + 4, x_rstd)
            pool.wait_ge(y_sq, 16)
            small(gbc, spread(ffn_norm_g[1:2], 0, P), s_gbc)

        @block.scalar
        def _(act):
            def square_x(k):
                if k == 0:
                    act.wait_ge(s_x, 16)
                elif k == 2:
                    act.wait_ge(x_ffn, 4)
                else:
                    act.wait_ge(x_mid, 4 * (k // 2 + 1))
                if k:
                    act.wait_ge(x_rstd, k)
                for t in range(NT):
                    if k:
                        act.wait_ge(xTh_ready, 8 * {1: 2, 2: 3, 3: 5}[k])
                        act.wait_ge(xTl_ready, 8 * {1: 2, 2: 3, 3: 5}[k])
                    nc.scalar.activation(xn[:, t, :], x[:, t, :], ACT.Square, accum_out=ssx[:, t:t + 1]).then_inc(x_sq, 1)

            def split_hi(k, gain):
                for c in range(KC):
                    act.wait_ge(xT_psum, 8 * k + c // 2 * 2 + 2)
                    nc.scalar.activation(xTh[:, c, :], bank[4 + c // 2][:, (c % 2) * S:(c % 2 + 1) * S], ACT.Copy,
                                         scale=gains[:, gain, c:c + 1] if gain is not None else 1.0).then_inc(xTh_ready, 1)

            def mixer(L):
                units = [Unit(WIN[L] + n) for n in range(W_IN_UNITS)]
                for n in range(SPL):
                    round_unit(act, units[n], in_words(n))
                square_x(2 * L)
                if L == 0:
                    act.wait_ge(s_small, 16 * 6)
                split_hi(3 * L, 3 * L)
                for c in range(5):
                    for n in (2 * c + 3, 2 * c + 4):
                        if n < W_IN_UNITS:
                            round_unit(act, units[n], in_words(n))
                    act.wait_ge(used, WIN[L] + min(2 * c + 2, W_IN_UNITS))
                    n = min(FB, D_IN - c * FB)
                    for t in range(NT):
                        nc.scalar.copy(pr[:, t, c * FB:c * FB + n], bank[2 * (c % 2) + t][:, 0:n]).then_inc(pr_ready, 1)
                act.wait_ge(pr_ready, 10 * (L + 1))
                nc.scalar.activation(gates[:].rearrange("p t h b -> p t (h b)"), pr[:, :, GT:GT + 12], ACT.Exp,
                                     scale=-1.0).then_inc(gate_e, 1)
                for t in range(NT):
                    nc.scalar.activation(junk[:, :], pr[:, t, V0:V0 + GW], ACT.Square,
                                         accum_out=ss[:, t, 6:7]).then_inc(v_ss, 1)
                    act.wait_ge(v_ss, 2 * L + t + 1)
                wout = [Unit(WOUT[L] + n) for n in range(W_OUT_UNITS)]
                for n in range(SPL):
                    round_unit(act, wout[n])
                act.wait_ge(z_ready, 3 * (L + 1))
                for j in range(2):
                    act.wait_ge(dlt_psum, 2 * L + j + 1)
                    nc.scalar.copy(dlt[:, j], bank[j][0:HD, :].rearrange("p (g s) -> p g s", g=2)).then_inc(dlt_ready, 1)
                act.wait_ge(gelu_in, L + 1)
                nc.scalar.activation(hz[:], hy[:], ACT.Exp, scale=-2.0 * GELU_C).then_inc(gelu_e, 1)
                for j in range(3):
                    act.wait_ge(qkT_psum, 3 * L + j + 1)
                    nc.scalar.copy(qT[:, j] if j < 2 else kT[:],
                                   bank[[6, 7, 4][j]][0:HD, :].rearrange("p (h s) -> p h s", h=2)).then_inc(qkT_ready, 1)
                act.wait_ge(cs_in, L + 1)
                nc.scalar.activation(scc[:], scc[:], ACT.Exp).then_inc(cs_exp, 1)
                act.wait_ge(cT_psum, L + 1)
                nc.scalar.copy(pcT[:].rearrange("p t q -> p (t q)"), bank[7][:, 0:NT * P]).then_inc(cT_ready, 1)
                for i in range(4):
                    t, k = i % 2, 4 * L + i
                    act.wait_ge(a_max, k + 1)
                    for h in range(NH):
                        nc.scalar.activation(sc[:, i % 2, h, 0:P * (t + 1)], sc[:, i % 2, h, 0:P * (t + 1)], ACT.Exp,
                                             bias=mx[:, i, h:h + 1], accum_out=sm[:, i, h:h + 1]).then_inc(a_exp, 1)
                    for kt in range(t + 1):
                        act.wait_ge(a_T, 6 * L + [0, 1, 3, 4][i] + kt + 1)
                        if k:
                            act.wait_ge(a_o, k)
                        nc.scalar.copy(pT[:, kt], bank[4 + kt][:, :].rearrange("p (h q) -> p h q", h=NH)).then_inc(a_Tr, 1)
                act.wait_ge(mix_done, 6 * (L + 1))
                act.wait_ge(a_done, 4 * (L + 1))
                for t in range(NT):
                    for m in range(4):
                        nc.scalar.activation(junk[:, :], xn[:, t, m * GW:(m + 1) * GW], ACT.Square,
                                             accum_out=ssy[:, t, m:m + 1]).then_inc(y_sq, 1)
                        act.wait_ge(y_sq, 8 * L + 4 * t + m + 1)
                split_hi(3 * L + 1, 3 * L + 1)
                round_unit(act, wout[3])

            def silu(value, k, tiles):
                act.wait_ge(used, value)
                act.wait_ge(gT_psum, k * tiles)
                for t in range(tiles):
                    nc.scalar.activation(sg[:, t, :], bank[t][:, :], ACT.Silu).then_inc(silu_done, 1)

            def split_g(k, tiles):
                for t in range(tiles):
                    act.wait_ge(gT_psum, k * tiles + t + 1)
                    nc.scalar.copy(gTh[:, t], bank[4 + t][:, :].rearrange("p (c s) -> p c s", c=4)).then_inc(gTh_ready, 1)

            def ffn(base, rounds, turns, k0, tiles, first):
                for n in range(first, 4):
                    round_unit(act, Unit(base + n, rounds, turns))
                silu(base + rounds + 2, k0, tiles)
                with act.Fori(1, NFB) as f:
                    r, tn = rounds + (f - 1) * 6, turns + (f - 1)
                    for n in range(4, 8):
                        round_unit(act, Unit(base + n, r, tn))
                    silu(base + r + 6, k0 + f, tiles)
                    split_g(k0 + f - 1, tiles)
                    for n in range(8, 10):
                        round_unit(act, Unit(base + n, r, tn))
                for n in range(FFN_UNITS - 2, FFN_UNITS):
                    round_unit(act, Unit(base + n, rounds, turns))
                split_g(k0 + NFB - 1, tiles)

            mixer(0)
            for n in range(SPL):
                round_unit(act, Unit(DENSE + n))
            square_x(1)
            split_hi(2, 2)
            ffn(DENSE, 0, 0, 0, NT, SPL)
            mixer(1)
            square_x(3)
            split_hi(5, None)
            act.wait_ge(lg_ready, 1)
            nc.scalar.activation(ra[:], ra[:], ACT.Exp).then_inc(lg_exp, 1)

            def experts(base, e0):
                with act.Fori(0, NE) as e:
                    rounds, turns, k = e * FFN_UNITS, e * (FFN_UNITS // RAW), e + e0
                    for n in range(2):
                        round_unit(act, Unit(base + n, rounds, turns))
                    for j in range(2):
                        act.wait_ge(xg_psum, 2 * k + j + 1)
                        nc.scalar.copy(xgh[:, 4 * j:4 * j + 4, :],
                                       bank[1 + 2 * j][:, :].rearrange("p (c s) -> p c s", c=4)).then_inc(xgh_ready, 1)
                    act.wait_ge(ohT_psum, k + 1)
                    nc.scalar.copy(onehotT, bank[5][:, 0:NT * P]).then_inc(ohT_ready, 1)
                    round_unit(act, Unit(base + 2, rounds, turns))
                    ffn(base, rounds, turns, k * NFB + NT * NFB, 1, SPL)
                    act.wait_ge(used, base + rounds + FFN_UNITS)
                    for j in range(2):
                        nc.scalar.copy(yg[:, j * FB:(j + 1) * FB], bank[6 + j][:, :]).then_inc(yg_ready, 1)

            experts(MOE, 0)
            act.wait_ge(route_ready, 1)
            more = act.value_load(flag[0:1, 0:1], min_val=0, max_val=1)
            with act.If(more > 0):
                experts(MOE2, NE)

        @block.vector
        def _(dve):
            V = nc.vector
            count = [0]

            def link(ins):
                count[0] += 1
                ins.then_inc(dve_order, 1)
                dve.wait_ge(dve_order, count[0])

            def settle(*ins):
                for i in ins:
                    count[0] += 1
                    i.then_inc(dve_order, 1)
                dve.wait_ge(dve_order, count[0])

            def tt(o, a, b, op):
                return V.tensor_tensor(o, a, b, op)

            def split_lo(k, gain):
                for c in range(KC):
                    dve.wait_ge(xTh_ready, 8 * k + c // 2 * 2 + 2)
                    src = bank[4 + c // 2][:, (c % 2) * S:(c % 2 + 1) * S]
                    hi = xTh[:, c, :].bitcast(F32)
                    if gain is None:
                        tt(xTl[:, c, :], src, hi, ALU.subtract).then_inc(xTl_ready, 1)
                    else:
                        V.scalar_tensor_tensor(xTl[:, c, :], src, gains[:, gain, c:c + 1], hi, ALU.mult,
                                               ALU.subtract).then_inc(xTl_ready, 1)

            def scale_x(k):
                dve.wait_ge(x_rstd, k + 1)
                for t in range(NT):
                    V.tensor_scalar(xn[:, t, :], x[:, t, :], rsx[:, t:t + 1], None, ALU.mult).then_inc(xn_ready, 1)

            def rope(q, cos, sin, scr):
                a, b = q[..., 0:8] if len(q.shape) == 2 else q[:, :, :, 0:8], q[..., 8:16] if len(q.shape) == 2 else q[:, :, :, 8:16]
                settle(tt(scr[0], a, cos, ALU.mult), tt(scr[1], b, sin, ALU.mult),
                       tt(scr[2], a, sin, ALU.mult), tt(scr[3], b, cos, ALU.mult))
                return tt(a, scr[0], scr[1], ALU.subtract), tt(b, scr[2], scr[3], ALU.add)

            def mixer(L):
                units = [Unit(WIN[L] + n) for n in range(W_IN_UNITS)]
                for n in range(SPL):
                    rest_unit(dve, units[n], in_words(n))
                scale_x(2 * L)
                dve.wait_ge(sguT_psum, L + 1)
                tt(sgT[:], bank[0][:, :].rearrange("p (g t) -> p g t", g=NH), bc(C("triu"), 1, NH), ALU.mult).then_inc(sguT_ready, 1)
                split_lo(3 * L, 3 * L)
                for n in range(SPL, W_IN_UNITS):
                    rest_unit(dve, units[n], in_words(n))
                wout = [Unit(WOUT[L] + n) for n in range(W_OUT_UNITS)]
                dve.wait_ge(pr_ready, 10 * (L + 1))
                for t in range(NT):
                    V.tensor_copy(kd[:, t], bc(pr[:, t, KCM:KCM + 2 * HD].rearrange("p (j d) -> p j d", j=2), 2, 2)).then_inc(kd_ready, 1)
                a = tt(tmp[:, :, 0:4, :].rearrange("p t h d -> p t (h d)"), pr[:, :, 0:GW], pr[:, :, 0:GW], ALU.mult)
                b = tt(tmp[:, :, 4, :], pr[:, :, KS:KS + HD], pr[:, :, KS:KS + HD], ALU.mult)
                c = tt(tmp[:, :, 5, :], pr[:, :, KW:KW + HD], pr[:, :, KW:KW + HD], ALU.mult)
                settle(a, b, c)
                V.tensor_reduce(ss[:, :, 0:6], tmp[:], AX_X, ALU.add).then_inc(qk_ss, 1)
                if L == 0:
                    dve.wait_ge(s_small, 16 * 6)
                dve.wait_ge(s_lay[L], LAY_LOADED)
                link(V.tensor_scalar(g6[:, 0:NH, :], g6[:, 0:NH, :], HD ** -0.5, None, ALU.mult))
                z = tmp[:, :, :, :].rearrange("p t h d -> p t (h d)")[:, :, 0:GW]
                dve.wait_ge(qk_ss, L + 1)
                link(tt(z, pr[:, :, CG:CG + GW], pr[:, :, HIN:HIN + GW], ALU.mult))
                for k in range(3):
                    tt(zk[k], z, bc(cw[:, k, :], 1, NT), ALU.mult).then_inc(z_ready, 1)
                dve.wait_ge(kdT_psum, L + 1)
                for s in range(2):
                    rows = slice(s * HD, (s + 1) * HD)
                    for hi in range(2):
                        src = bank[4][rows, :].rearrange("p (j n a two) -> p j n a two", j=2, n=16, two=2)[:, :, hi:hi + NCMP, :, s]
                        dst = kvb[rows, :, 8 * hi:8 * hi + 8, 0:NCMP].rearrange("p j a n -> p j n a")
                        for j in range(2):
                            tt(dst[:, j], src[:, j], bc(peT[rows, j, 8 * hi:8 * hi + 8], 1, NCMP), ALU.add).then_inc(kvb_ready, 1)
                dve.wait_ge(qk_rstd, 2 * (L + 1))
                a = tt(qk[:, :, 0:4, :], pr[:, :, 0:GW].rearrange("p t (h d) -> p t h d", h=NH), bc(rs[:, :, 0:4], 3, HD), ALU.mult)
                b = tt(qk[:, :, 4, :], pr[:, :, KS:KS + HD], bc(rs[:, :, 4], 2, HD), ALU.mult)
                c = tt(qk[:, :, 5, :], pr[:, :, KW:KW + HD], bc(rs[:, :, 5], 2, HD), ALU.mult)
                settle(a, b, c)
                qf = qk[:].rearrange("p t h d -> p t (h d)")
                link(tt(qf, qf, bc(g6[:].rearrange("p h d -> p (h d)"), 1, NT), ALU.mult))
                cos = bc(C("cos").rearrange("p (t f) -> p t f", t=NT), 2, 6)
                sin = bc(C("sin").rearrange("p (t f) -> p t f", t=NT), 2, 6)
                for i in rope(qk, cos, sin, rp):
                    i.then_inc(qk_ready, 1)
                for t in range(NT):
                    V.scalar_tensor_tensor(vn[:, t, :], pr[:, t, V0:V0 + GW], rs[:, t, 6:7], gsgu[:, :], ALU.mult,
                                           ALU.mult).then_inc(vn_ready, 1)
                dve.wait_ge(gate_e, L + 1)
                gf = gates[:].rearrange("p t h b -> p (t h b)")
                link(V.tensor_scalar(gf, gf, 1.0, None, ALU.add))
                link(V.reciprocal(gf, gf))
                dve.wait_ge(hid_psum, L + 1)
                link(V.tensor_copy(hx[:], bank[5][:, 0:2 * CP].rearrange("p (j n) -> p j n", j=2)[:, :, 0:NCMP]))
                link(tt(hy[:], hx[:], hx[:], ALU.mult))
                link(V.tensor_scalar(hy[:], hy[:], 0.044715, 1.0, ALU.mult, ALU.add))
                link(tt(hz[:], hy[:], hx[:], ALU.mult))
                V.tensor_copy(hy[:], hz[:]).then_inc(gelu_in, 1)
                dve.wait_ge(poolY_psum, L + 1)
                tt(xn[:, :, 2 * GW:3 * GW], bank[2][:, :].rearrange("p (t d) -> p t d", t=NT), bc(psc[:, :], 1, NT),
                   ALU.mult).then_inc(mix_done, 1)
                dve.wait_ge(conv_psum, L + 1)
                tt(xn[:, :, 3 * GW:4 * GW], bank[3][:, :].rearrange("p (t d) -> p t d", t=NT), pr[:, :, BG:BG + GW],
                   ALU.mult).then_inc(mix_done, 1)
                dve.wait_ge(sgu_psum, L + 1)
                for g in range(NH):
                    V.scalar_tensor_tensor(xn[:, :, GW + g * HD:GW + (g + 1) * HD],
                                           bank[0][:, :].rearrange("p (t d) -> p t d", t=NT)[:, :, g * HD:(g + 1) * HD],
                                           sgb[:, g:g + 1], pr[:, :, U0 + g * HD:U0 + (g + 1) * HD], ALU.add,
                                           ALU.mult).then_inc(mix_done, 1)
                dve.wait_ge(gelu_e, L + 1)
                link(V.tensor_scalar(hy[:], hz[:], 1.0, None, ALU.add))
                link(V.reciprocal(hz[:], hy[:]))
                for j in range(2):
                    tt(hidp[:, j, :, 0:NCMP], bc(hx[:, j], 1, NH), bc(hz[:, j], 1, NH), ALU.mult).then_inc(hid_ready, 1)
                dve.wait_ge(kcvc_psum, L + 1)
                link(V.tensor_copy(kcs[:, 0, :], bank[5][0:CP, 128:192]))
                link(tt(kcs[:, 1, :], kcs[:, 0, :], kcs[:, 0, :], ALU.mult))
                V.tensor_reduce(ssc[:], kcs[:, 1, :], AX_X, ALU.add).then_inc(kc_ss, 1)
                tt(vbd[:], bc(bank[5][:, 192:256], 1, NH), bc(C("blk"), 2, HD), ALU.mult).then_inc(vbd_ready, 1)
                for n in range(SPL):
                    rest_unit(dve, wout[n])
                dve.wait_ge(kc_rstd, L + 1)
                link(V.scalar_tensor_tensor(kcs[:, 2, :], kcs[:, 0, :], rsc[:, 0:1], gkc[0:CP, :], ALU.mult, ALU.mult))
                for i in rope(kcs[:, 2, :], C("ccos", CP), C("csin", CP), [krp[:, i, :] for i in range(4)]):
                    i.then_inc(kc_ready, 1)
                dve.wait_ge(kcT_psum, L + 1)
                V.tensor_copy(kcT[:], bank[5][0:HD, 256:256 + CP]).then_inc(kcT_ready, 1)
                dve.wait_ge(cs_psum, L + 1)
                for t in range(NT):
                    i = tt(scc[:, t], bank[6][:, t * P:(t + 1) * P].rearrange("p (h n) -> p h n", h=NH),
                           bc(C("cmask")[:, t * CP:(t + 1) * CP], 1, NH), ALU.add)
                    count[0] += 1
                    i.then_inc(dve_order, 1)
                dve.wait_ge(dve_order, count[0])
                link(V.tensor_reduce(mxc[:], scc[:], AX_X, ALU.max))
                tt(scc[:], scc[:], bc(mxc[:], 3, CP), ALU.subtract).then_inc(cs_in, 1)

                def scores(i):
                    t = i % 2
                    dve.wait_ge(a_s, 4 * L + i + 1)
                    if 4 * L + i >= 2:
                        dve.wait_ge(a_T, 6 * (L if i >= 2 else L - 1) + [4, 6, 1, 3][i])
                    b0 = 2 * (i % 2)
                    if t == 0:
                        link(tt(sc[:, 0, :, 0:P], bank[b0][:, :].rearrange("p (h k) -> p h k", h=NH), bc(C("causal"), 1, NH), ALU.add))
                    else:
                        done = []
                        for j in range(2):
                            src = bank[b0 + j][:, :].rearrange("p (h k) -> p h k", h=2)
                            done.append(V.tensor_copy(sc[:, 1, 2 * j:2 * j + 2, 0:P], src[:, :, 0:P]))
                            done.append(tt(sc[:, 1, 2 * j:2 * j + 2, P:S], src[:, :, P:S], bc(C("causal"), 1, 2), ALU.add))
                        settle(*done)
                    V.tensor_reduce(mx[:, i, :], sc[:, i % 2, :, 0:P * (t + 1)], AX_X, ALU.max, negate=True).then_inc(a_max, 1)

                scores(0)
                dve.wait_ge(cs_exp, L + 1)
                link(V.tensor_reduce(smc[:], scc[:], AX_X, ALU.add))
                a = V.reciprocal(smc[:], smc[:])
                b = tt(scc[:], scc[:], bc(C("cvalid").rearrange("p (t n) -> p t n", t=NT), 2, NH), ALU.mult)
                b.then_inc(cs_ready, 1)
                link(a)
                link(tt(smc[:], smc[:], gates[:, :, :, 0], ALU.mult))
                scores(1)
                dve.wait_ge(co_psum, L + 1)
                for t in range(NT):
                    tt(xn[:, t, 0:GW].rearrange("p (h d) -> p h d", h=NH),
                       bank[7][:, t * GW:(t + 1) * GW].rearrange("p (h d) -> p h d", h=NH), bc(smc[:, t, :], 2, HD),
                       ALU.mult).then_inc(co_done, 1)
                for i in range(4):
                    t, br = i % 2, i // 2
                    if i + 2 < 4:
                        nxt = i + 2
                    else:
                        nxt = None
                    dve.wait_ge(a_exp, 4 * (4 * L + i + 1))
                    link(V.reciprocal(cf[:, i, :], sm[:, i, :]))
                    link(tt(cf[:, i, :], cf[:, i, :], gates[:, t, :, 1 + br], ALU.mult))
                    if nxt is not None:
                        scores(nxt)
                    dve.wait_ge(a_o, 4 * L + i + 1)
                    dve.wait_ge(co_done, 2 * L + 2)
                    o = bank[6 + i % 2][:, 0:GW]
                    link(tt(ot[:, :].rearrange("p (h d) -> p h d", h=NH), o.rearrange("p (h d) -> p h d", h=NH),
                            bc(cf[:, i, :], 2, HD), ALU.mult))
                    if i >= 1:
                        dve.wait_ge(a_done, 4 * L + i)
                    tt(xn[:, t, 0:GW], xn[:, t, 0:GW], ot[:, :], ALU.add).then_inc(a_done, 1)
                for t in range(NT):
                    dve.wait_ge(y_rstd, 2 * L + t + 1)
                    y = xn[:, t, :].rearrange("p (m d) -> p m d", m=4)
                    tt(y, y, bc(rsy[:, t, :], 2, GW), ALU.mult).then_inc(yn_ready, 1)
                split_lo(3 * L + 1, 3 * L + 1)
                rest_unit(dve, wout[3])
                for b in range(2):
                    dve.wait_ge(used, WOUT[L] + 2 * b + 2)
                    for t in range(NT):
                        tt(x[:, t, b * FB:(b + 1) * FB], x[:, t, b * FB:(b + 1) * FB], bank[2 * b + t][:, :], ALU.add).then_inc(x_mid, 1)

            def times_h3(value, k, tiles):
                dve.wait_ge(used, value)
                for t in range(tiles):
                    dve.wait_ge(silu_done, k * tiles + t + 1)
                    tt(sg[:, t, :], sg[:, t, :], bank[2 + t][:, :], ALU.mult).then_inc(g_ready, 1)

            def split_g(k, tiles):
                for t in range(tiles):
                    dve.wait_ge(gTh_ready, k * tiles + t + 1)
                    tt(gTl[:, t], bank[4 + t][:, :].rearrange("p (c s) -> p c s", c=4), gTh[:, t].bitcast(F32),
                       ALU.subtract).then_inc(gTl_ready, 1)

            def add_y(value, half):
                dve.wait_ge(used, value)
                for t in range(NT):
                    xs = x[:, t, half * FB:(half + 1) * FB]
                    tt(xs, xs, bank[(6 if half == 0 else 4) + t][:, :], ALU.add).then_inc(y_added, 1)

            def ffn(base, rounds, k0, tiles, first, dense):
                for n in range(first, 4):
                    rest_unit(dve, Unit(base + n, rounds))

                def step(f, add):
                    r = rounds + (f - 1) * 6
                    rest_unit(dve, Unit(base + 4, r))
                    times_h3(base + r + 2, k0 + f - 1, tiles)
                    rest_unit(dve, Unit(base + 5, r))
                    if add:
                        add_y(base + r + 3, 0)
                    rest_unit(dve, Unit(base + 6, r))
                    if add:
                        add_y(base + r + 4, 1)
                    rest_unit(dve, Unit(base + 7, r))
                    split_g(k0 + f - 1, tiles)
                    rest_unit(dve, Unit(base + 8, r))
                    rest_unit(dve, Unit(base + 9, r))

                rest_unit(dve, Unit(base + 4, rounds))
                times_h3(base + rounds + 4, k0, tiles)
                for n in (5, 6, 7):
                    rest_unit(dve, Unit(base + n, rounds))
                split_g(k0, tiles)
                for n in (8, 9):
                    rest_unit(dve, Unit(base + n, rounds))
                with dve.Fori(2, NFB) as f:
                    step(f, dense)
                r = rounds + (NFB - 1) * 6
                rest_unit(dve, Unit(base + 4, r))
                times_h3(base + r + 2, k0 + NFB - 1, tiles)
                rest_unit(dve, Unit(base + 5, r))
                if dense:
                    add_y(base + r + 3, 0)
                    add_y(base + r + 4, 1)
                split_g(k0 + NFB - 1, tiles)
                if dense:
                    add_y(base + r + 5, 0)
                    add_y(base + r + 6, 1)

            V.memset(hidp[:].rearrange("p j h n -> p (j h n)"), 0.0).then_inc(hp_ready, 1)
            V.memset(zero[:].bitcast(F32), 0.0).then_inc(zero_ready, 1)
            dve.wait_ge(hp_ready, 1)
            dve.wait_ge(s_const, 16)
            mixer(0)
            for n in range(SPL):
                rest_unit(dve, Unit(DENSE + n))
            scale_x(1)
            split_lo(2, 2)
            ffn(DENSE, 0, 0, NT, SPL, True)
            dve.wait_ge(y_added, 4 * NFB)
            V.tensor_copy(cnt[:, 0:1], rsx[:, 0:1]).then_inc(x_ffn, 4)
            mixer(1)
            scale_x(3)
            dve.wait_ge(s_gbc, 16)
            dve.wait_ge(xn_ready, 8)
            for t in range(NT):
                tt(xn[:, t, :], xn[:, t, :], gbc, ALU.mult).then_inc(xn_ready, 1)
            dve.wait_ge(s_rt, 16)
            link(V.tensor_copy(rhl[:, 0], rt[:]))
            tt(rhl[:, 1], rt[:], rhl[:, 0].bitcast(F32), ALU.subtract).then_inc(rh_ready, 1)
            split_lo(5, None)
            dve.wait_ge(lg_psum, 1)
            link(V.tensor_copy(lg[:], bank[0][:, 0:NT * NE].rearrange("p (t e) -> p t e", t=NT)))
            settle(*[V.max(top[:, t, :], lg[:, t, :]) for t in range(NT)])
            m1, m2 = bc(top[:, :, 0], 2, NE), bc(top[:, :, 1], 2, NE)
            tt(ra[:], lg[:], m1, ALU.subtract).then_inc(lg_ready, 1)
            settle(tt(sel[:], lg[:], m2, ALU.is_gt), tt(rb[:], lg[:], m2, ALU.is_equal))
            link(V.tensor_reduce(rsc1[:], sel[:], AX_X, ALU.add))
            link(tt(posm[:, :, 0], rsc1[:], rb[:, :, 0], ALU.add))
            for e in range(1, NE):
                link(tt(posm[:, :, e], posm[:, :, e - 1], rb[:, :, e], ALU.add))
            link(V.tensor_scalar(posm[:], posm[:], 2.0, None, ALU.is_le))
            link(tt(rb[:], rb[:], posm[:], ALU.mult))
            tt(sel[:], sel[:], rb[:], ALU.add).then_inc(sel_ready, 1)
            dve.wait_ge(sel_ready, 1)
            dve.wait_ge(lg_exp, 1)
            link(tt(ra[:], ra[:], sel[:], ALU.mult))
            link(V.tensor_reduce(rsc1[:], ra[:], AX_X, ALU.add))
            link(V.reciprocal(rsc1[:], rsc1[:]))
            link(tt(gate[:], ra[:], bc(rsc1[:], 2, NE), ALU.mult))
            dve.wait_ge(pos_psum, 1)
            link(V.scalar_tensor_tensor(posm[:], bank[1][:, 0:NT * NE].rearrange("p (t e) -> p t e", t=NT), 1.0, sel[:],
                                        ALU.add, ALU.mult))
            link(V.tensor_scalar(posm[:], posm[:], -1.0, None, ALU.add))
            link(V.tensor_reduce(cnt[:, 0:1], bank[1][:, NT * NE:(NT + 1) * NE], AX_X, ALU.max))
            V.tensor_scalar(flag[:], cnt[:, 0:1], float(SLOTS), None, ALU.is_gt).then_inc(route_ready, 1)

            def experts(base, e0, first_slot):
                with dve.Fori(0, NE) as e:
                    rounds, k = e * FFN_UNITS, e + e0
                    dve.wait_ge(used, base + rounds)
                    for t in range(NT):
                        V.tensor_scalar(onehot[:, t, :], C("iota"), float(first_slot), posm[:, t, ds(e, 1)], ALU.add,
                                        ALU.is_equal).then_inc(oh_ready, 1)
                    for n in range(2):
                        rest_unit(dve, Unit(base + n, rounds))
                    for j in range(2):
                        dve.wait_ge(xgh_ready, 2 * k + j + 1)
                        tt(xgl[:, 4 * j:4 * j + 4, :], bank[1 + 2 * j][:, :].rearrange("p (c s) -> p c s", c=4),
                           xgh[:, 4 * j:4 * j + 4, :].bitcast(F32), ALU.subtract).then_inc(xgl_ready, 1)
                    rest_unit(dve, Unit(base + 2, rounds))
                    ffn(base, rounds, k * NFB + NT * NFB, 1, SPL, False)
                    for t in range(NT):
                        for j in range(2):
                            dve.wait_ge(sc_psum, 4 * k + 2 * t + j + 1)
                            xs = x[:, t, j * FB:(j + 1) * FB]
                            b = bank[[1, 3, 4, 5][2 * t + j]]
                            V.scalar_tensor_tensor(xs, b[:, :], gate[:, t, ds(e, 1)], xs, ALU.mult, ALU.add).then_inc(sc_done, 1)

            dve.wait_ge(route_ready, 1)
            experts(MOE, 0, 0)
            more = dve.value_load(flag[0:1, 0:1], min_val=0, max_val=1)
            with dve.If(more > 0):
                experts(MOE2, NE, SLOTS)
            V.tensor_copy(cnt[:, 1:2], rsx[:, 0:1]).then_inc(s_done, 1)

        @block.tensor
        def _(pe):
            T = nc.tensor

            def transpose_x(k, wait, value):
                for c in range(KC):
                    for t in range(NT):
                        if c == 0:
                            pe.wait_ge(wait, value - NT + t + 1)
                        i = T.transpose(bank[4 + c // 2][:, (c % 2) * S + t * P:(c % 2) * S + (t + 1) * P],
                                        xn[:, t, c * P:(c + 1) * P], ident)
                    i.then_inc(xT_psum, 1)

            def product(L0, n_units, k, bank_of, width_of):
                for n in range(n_units):
                    u = Unit(L0 + n)
                    whole = width_of(n) != FB
                    w = width_of(n)
                    chunks = range(KC) if whole else range(4 * (n % 2), 4 * (n % 2) + 4)
                    pe.wait_ge(s_lo, u.n + 1)
                    wh = u.hi[:, 0:len(chunks) * w].rearrange("p (c n) -> p c n", n=w)
                    wl = u.lo[:, 0:len(chunks) * w].rearrange("p (c n) -> p c n", n=w)
                    for j, c in enumerate(chunks):
                        if n < 2 or whole:
                            pe.wait_ge(xTl_ready, 8 * k + c + 1)
                        for t in range(NT):
                            i = three_passes(bank_of(n, t)[:, 0:w], xTh[:, c, t * P:(t + 1) * P], xTl[:, c, t * P:(t + 1) * P],
                                             wh[:, j, :], wl[:, j, :], c == 0, c == KC - 1)
                    i.then_inc(used, 1)
                    yield n

            def mixer(L):
                pe.wait_ge(s_lay[L], LAY_LOADED)
                pe.wait_ge(s_const, 16)
                if L:
                    pe.wait_ge(silu_done, NT * NFB)
                for g in range(NH):
                    i = T.transpose(bank[0][:, g * P:(g + 1) * P], sgw[:, g, :], ident)
                i.then_inc(sguT_psum, 1)
                transpose_x(3 * L, xn_ready, 4 * L + 2)
                pe.wait_ge(sguT_ready, L + 1)
                if L:
                    pe.wait_ge(g_ready, NT * NFB)
                for n in product(WIN[L], W_IN_UNITS, 3 * L, lambda n, t: bank[2 * ((n // 2) % 2) + t],
                                 lambda n: FB if n < W_IN_UNITS - 1 else D_IN - 4 * FB):
                    if n % 2 and n >= 3:
                        pe.wait_ge(pr_ready, 10 * L + n - 1)
                for t in range(NT):
                    pe.wait_ge(kd_ready, 2 * L + t + 1)
                    for j in range(2):
                        i = T.transpose(bank[4][:, j * S + t * P:j * S + (t + 1) * P], kd[:, t, j].rearrange("p a d -> p (a d)"), ident)
                i.then_inc(kdT_psum, 1)
                pe.wait_ge(pr_ready, 10 * (L + 1))
                band = C("band").rearrange("p (m g t) -> p m g t", m=3, g=4)
                for g in range(4):
                    o = bank[g // 2][0:HD, (g % 2) * S:(g % 2 + 1) * S]
                    w = [pr[:, t, PIN + g * HD:PIN + (g + 1) * HD] for t in range(NT)]
                    T.matmul(o[:, 0:P], w[0], band[:, 0, g, :], start=True, stop=True)
                    T.matmul(o[:, P:S], w[0], band[:, 1, g, :], start=True, stop=False)
                    i = T.matmul(o[:, P:S], w[1], band[:, 2, g, :], start=False, stop=True)
                    if g % 2:
                        i.then_inc(dlt_psum, 1)
                pe.wait_ge(z_ready, 3 * (L + 1))
                sh = C("shift").rearrange("p (k t) -> p k t", k=4)
                for t in range(NT):
                    o = bank[3][:, t * GW:(t + 1) * GW]
                    T.matmul(o, ident, zk[2][:, t, :], start=True, stop=False)
                    T.matmul(o, sh[:, 0, :], zk[1][:, t, :], start=False, stop=False)
                    i = T.matmul(o, sh[:, 1, :], zk[0][:, t, :], start=False, stop=(t == 0))
                    if t:
                        T.matmul(o, sh[:, 2, :], zk[1][:, 0, :], start=False, stop=False)
                        i = T.matmul(o, sh[:, 3, :], zk[0][:, 0, :], start=False, stop=True)
                i.then_inc(conv_psum, 1)
                pe.wait_ge(kvb_ready, 8 * (L + 1))
                for j in range(2):
                    for a in range(16):
                        i = T.matmul(bank[5][:, j * CP:j * CP + NCMP], w1c[:, j, a, :], kvb[:, j, a, 0:NCMP],
                                     start=(a == 0), stop=(a == 15))
                i.then_inc(hid_psum, 1)
                pe.wait_ge(dlt_ready, 2 * (L + 1))
                for t in range(NT):
                    for g in range(4):
                        i = T.matmul(bank[2][:, t * GW + g * HD:t * GW + (g + 1) * HD], dlt[:, g // 2, g % 2, t * P:(t + 1) * P], pw[HD:P, g, :],
                                     start=True, stop=True)
                i.then_inc(poolY_psum, 1)
                pe.wait_ge(vn_ready, 2 * (L + 1))
                for t in range(NT):
                    for g in range(NH):
                        i = T.matmul(bank[0][:, t * GW + g * HD:t * GW + (g + 1) * HD], sgT[:, g, :], vn[:, t, g * HD:(g + 1) * HD],
                                     start=True, stop=True)
                i.then_inc(sgu_psum, 1)
                pe.wait_ge(qk_ready, 2 * (L + 1))
                for h in range(6):
                    for t in range(NT):
                        i = T.transpose(bank[[6, 7, 4][h // 2]][0:HD, (h % 2) * S + t * P:(h % 2) * S + (t + 1) * P],
                                        qk[:, t, h, :], ident)
                    if h % 2:
                        i.then_inc(qkT_psum, 1)
                pe.wait_ge(hid_ready, 2 * (L + 1))
                T.matmul(bank[5][0:CP, 128:192], hidp[:, 0, 0, :], w2c[:, 0, :], start=True, stop=True)
                T.matmul(bank[5][:, 192:256], hidp[:, 1].rearrange("p h n -> p (h n)"), w2c[:, 1, :], start=True,
                         stop=True).then_inc(kcvc_psum, 1)

                def scores(i):
                    t, b0 = i % 2, 2 * (i % 2)
                    if i >= 2:
                        pe.wait_ge(a_max, 4 * L + i - 1)
                    for h in range(NH):
                        n = P * (t + 1)
                        b = bank[b0 + h * n // 512]
                        mm = T.matmul(b[:, h * n % 512:h * n % 512 + n], qT[:, h // 2, h % 2, t * P:(t + 1) * P],
                                      kT[:, i // 2, 0:n], start=True, stop=True)
                    mm.then_inc(a_s, 1)

                pe.wait_ge(qkT_ready, 3 * (L + 1))
                pe.wait_ge(mix_done, 6 * L + 6)
                scores(0)
                pe.wait_ge(kc_ready, 2 * (L + 1))
                T.transpose(bank[5][0:HD, 256:256 + CP], kcs[:, 2, :], ident[0:CP, 0:CP]).then_inc(kcT_psum, 1)
                pe.wait_ge(kcT_ready, L + 1)
                for t in range(NT):
                    for h in range(NH):
                        i = T.matmul(bank[6][:, (t * NH + h) * CP:(t * NH + h + 1) * CP], qT[:, h // 2, h % 2, t * P:(t + 1) * P], kcT[:, :],
                                     start=True, stop=True)
                i.then_inc(cs_psum, 1)
                scores(1)
                pe.wait_ge(cs_ready, L + 1)
                for t in range(NT):
                    i = T.transpose(bank[7][:, t * P:(t + 1) * P], scc[:, t].rearrange("p h n -> p (h n)"), ident)
                i.then_inc(cT_psum, 1)
                pe.wait_ge(cT_ready, L + 1)
                pe.wait_ge(vbd_ready, L + 1)
                for t in range(NT):
                    i = T.matmul(bank[7][:, t * GW:(t + 1) * GW], pcT[:, t, :], vbd[:].rearrange("p h d -> p (h d)"),
                                 start=True, stop=True)
                i.then_inc(co_psum, 1)
                for i in range(4):
                    t, v0 = i % 2, (VS, VW)[i // 2]
                    pe.wait_ge(a_exp, 4 * (4 * L + i + 1))
                    if i >= 1:
                        pe.wait_ge(a_Tr, 6 * L + [0, 1, 3, 4][i])
                    for kt in range(t + 1):
                        for h in range(NH):
                            mm = T.transpose(bank[4 + kt][:, h * P:(h + 1) * P], sc[:, i % 2, h, kt * P:(kt + 1) * P], ident)
                        mm.then_inc(a_T, 1)
                    if i + 2 < 4:
                        scores(i + 2)
                    pe.wait_ge(a_Tr, 6 * L + [0, 1, 3, 4][i] + t + 1)
                    if i >= 2:
                        pe.wait_ge(a_done, 4 * L + i - 1)
                    elif i == 1:
                        pe.wait_ge(co_done, 2 * L + 2)
                    for h in range(NH):
                        for kt in range(t + 1):
                            mm = T.matmul(bank[6 + i % 2][:, h * HD:(h + 1) * HD], pT[:, kt, h, :],
                                          pr[:, kt, v0:v0 + HD], start=(kt == 0), stop=(kt == t))
                    mm.then_inc(a_o, 1)
                transpose_x(3 * L + 1, yn_ready, 2 * L + 2)
                for n in product(WOUT[L], W_OUT_UNITS, 3 * L + 1, lambda n, t: bank[2 * (n // 2) + t], lambda n: FB):
                    pass

            def up(base, rounds, w, tiles, xh, xl, first=False):
                for h in range(2):
                    u = Unit(base + 2 * w + h, rounds)
                    pe.wait_ge(s_lo, u.n + 1)
                    wh = u.hi[:, :].rearrange("p (c n) -> p c n", c=4)
                    wl = u.lo[:, :].rearrange("p (c n) -> p c n", c=4)
                    for j in range(4):
                        c = 4 * h + j
                        for t in range(tiles):
                            i = three_passes(bank[2 * w + t][:, :], xh[:, c, t * P:(t + 1) * P], xl[:, c, t * P:(t + 1) * P],
                                             wh[:, j, :], wl[:, j, :], c == 0, c == KC - 1)
                    i.then_inc(used, 1)

            def turn(k, tiles):
                for t in range(tiles):
                    pe.wait_ge(g_ready, k * tiles + t + 1)
                    for c in range(4):
                        i = T.transpose(bank[4 + t][:, c * P:(c + 1) * P], sg[:, t, c * P:(c + 1) * P], ident)
                    i.then_inc(gT_psum, 1)

            def down(base, rounds, k, tiles, dense, last=True):
                for h in range(2):
                    u = Unit(base + h, rounds)
                    pe.wait_ge(s_lo, u.n + 1)
                    if h == 0:
                        pe.wait_ge(gTl_ready, (k + 1) * tiles)
                    wh = u.hi[:, :].rearrange("p (c n) -> p c n", c=4)
                    wl = u.lo[:, :].rearrange("p (c n) -> p c n", c=4)
                    for j in range(4):
                        for t in range(tiles):
                            o = bank[(6 if h == 0 else 4) + t] if dense else bank[6 + h]
                            i = three_passes(o[:, :], gTh[:, t, j, :], gTl[:, t, j, :], wh[:, j, :], wl[:, j, :],
                                             dense and j == 0, last and j == 3)
                    i.then_inc(used, 1)

            mixer(0)
            transpose_x(2, xn_ready, 4)
            pe.wait_ge(xTl_ready, 24)
            pe.wait_ge(x_mid, 4)
            up(DENSE, 0, 0, NT, xTh, xTl)
            up(DENSE, 0, 1, NT, xTh, xTl)

            def dense_step(f, r, peeled):
                pe.wait_ge(silu_done, NT * f)
                up(DENSE + 4, r, 0, NT, xTh, xTl)
                if not peeled:
                    pe.wait_ge(y_added, 4 * (f - 1))
                turn(f - 1, NT)
                up(DENSE + 4, r, 1, NT, xTh, xTl)
                down(DENSE + 8, r, f - 1, NT, True)

            dense_step(1, 0, True)
            with pe.Fori(2, NFB) as f:
                dense_step(f, (f - 1) * 6, False)
            pe.wait_ge(y_added, 4 * (NFB - 1))
            turn(NFB - 1, NT)
            down(DENSE + FFN_UNITS - 2, 0, NFB - 1, NT, True)
            mixer(1)
            transpose_x(5, xn_ready, 10)
            pe.wait_ge(rh_ready, 1)
            pe.wait_ge(xTl_ready, 48)
            pe.wait_ge(x_mid, 8)
            for t in range(NT):
                for c in range(KC):
                    for n, (a, b) in enumerate(((xTh, 0), (xTh, 1), (xTl, 0), (xTl, 1))):
                        i = T.matmul(bank[0][:, t * NE:(t + 1) * NE], a[:, c, t * P:(t + 1) * P], rhl[:, b, c, :],
                                     start=(c == 0 and n == 0), stop=(c == KC - 1 and n == 3))
            i.then_inc(lg_psum, 1)
            pe.wait_ge(sel_ready, 1)
            T.matmul(bank[1][:, 0:NE], C("before"), sel[:, 0, :], start=True, stop=True)
            T.matmul(bank[1][:, NE:2 * NE], C("ones"), sel[:, 0, :], start=True, stop=False)
            T.matmul(bank[1][:, NE:2 * NE], C("before"), sel[:, 1, :], start=False, stop=True)
            T.matmul(bank[1][:, 2 * NE:3 * NE], C("ones"), sel[:, 0, :], start=True, stop=False)
            T.matmul(bank[1][:, 2 * NE:3 * NE], C("ones"), sel[:, 1, :], start=False, stop=True).then_inc(pos_psum, 1)
            pe.wait_ge(route_ready, 1)
            pe.wait_ge(zero_ready, 1)

            def experts(base, e0):
                with pe.Fori(0, NE) as e:
                    rounds, k = e * FFN_UNITS, e + e0
                    kb = k * NFB + NT * NFB
                    pe.wait_ge(oh_ready, 2 * (k + 1))
                    for c in range(KC):
                        for t in range(NT):
                            i = T.matmul(bank[1 + 2 * (c // 4)][:, (c % 4) * P:(c % 4 + 1) * P], xn[:, t, c * P:(c + 1) * P],
                                         onehot[:, t, :], start=(t == 0), stop=(t == NT - 1))
                        if c % 4 == 3:
                            i.then_inc(xg_psum, 1)
                    for t in range(NT):
                        i = T.transpose(bank[5][:, t * P:(t + 1) * P], onehot[:, t, :], ident)
                    i.then_inc(ohT_psum, 1)
                    pe.wait_ge(xgl_ready, 2 * (k + 1))
                    for h in range(2):
                        T.matmul(bank[6 + h][:, :], zero[:, :], bc(zero[:, :], 1, 4), start=True, stop=False)
                    up(base, rounds, 0, 1, xgh, xgl)
                    up(base, rounds, 1, 1, xgh, xgl)
                    with pe.Fori(1, NFB) as f:
                        r = rounds + (f - 1) * 6
                        pe.wait_ge(silu_done, kb + f)
                        up(base + 4, r, 0, 1, xgh, xgl)
                        turn(kb + f - 1, 1)
                        up(base + 4, r, 1, 1, xgh, xgl)
                        down(base + 8, r, kb + f - 1, 1, False, last=False)
                    turn(kb + NFB - 1, 1)
                    down(base + FFN_UNITS - 2, rounds, kb + NFB - 1, 1, False)
                    pe.wait_ge(ohT_ready, k + 1)
                    pe.wait_ge(gTl_ready, kb + NFB)
                    for t in range(NT):
                        for j in range(2):
                            pe.wait_ge(yg_ready, 2 * k + j + 1)
                            T.matmul(bank[[1, 3, 4, 5][2 * t + j]][:, :], onehotT[:, t * P:(t + 1) * P], yg[:, j * FB:(j + 1) * FB],
                                     start=True, stop=True).then_inc(sc_psum, 1)

            experts(MOE, 0)
            more = pe.value_load(flag[0:1, 0:1], min_val=0, max_val=1)
            with pe.If(more > 0):
                experts(MOE2, NE)


_INS = ["x", "attn_norm_g", "w_in", "q_norm_g", "k_norm_g", "cmp_pe", "cmp_w1", "cmp_w2", "sgu_norm_g", "sgu_w",
        "sgu_b", "pool_w", "pool_scale", "conv_w", "mix_out_norm_g", "w_out", "ffn_norm_g", "ffn_w1", "ffn_w3",
        "ffn_w2", "router_w", "expert_w1", "expert_w3", "expert_w2"]


def kernel(**inputs):
    import concourse.bacc as bacc
    from concourse.bass_utils import run_bass_kernel_spmd

    nc = bacc.Bacc("TRN2", target_bir_lowering=False, num_devices=1)
    arrays, args = {}, []
    for name in _INS:
        a = np.ascontiguousarray(inputs[name])
        arrays[f"in_{name}"] = a
        args.append(nc.dram_tensor(f"in_{name}", a.shape, mybir.dt.from_np(a.dtype), kind="ExternalInput").ap())
    args[0] = args[0].rearrange("b s d -> (b s) d")
    arrays["in_consts"] = const_table()
    args.append(nc.dram_tensor("in_consts", arrays["in_consts"].shape, F32, kind="ExternalInput").ap())
    o = nc.dram_tensor("out_0", (1, S, D), F32, kind="ExternalOutput").ap()
    build(nc, *args, o.rearrange("b s d -> (b s) d"))
    r = run_bass_kernel_spmd(nc, [arrays], core_ids=[0])
    return r.results[0]["out_0"]
```

```python
from contextlib import ExitStack

import numpy as np

import concourse.bass as bass
from concourse import mybir

F32 = mybir.dt.float32
F32R = mybir.dt.float32r
I32 = mybir.dt.int32
ALU = mybir.AluOpType
ACT = mybir.ActivationFunctionType
AX_X = mybir.AxisListType.X
ds = bass.ds

P = 128
D = 1024
KC = D // P
S = 256
NT = S // P
HD = 64
NH = 4
GW = 256
DEPTH = 2
D_IN = 2188
FF = 3584
NE = 8
EPS = 1e-6
NEG = -1e30
NCMP = S // 16 - 1
CP = 32
THETA = 500000.0
POOLS = (2, 4, 8, 16)
Q0, KCM, KS, VS, KW, VW, GT, U0, V0, PIN, BG, CG, HIN = 0, 256, 384, 448, 512, 576, 640, 652, 908, 1164, 1420, 1676, 1932
FB = 512
NFB = FF // FB
UW = 2048
RAW = 6
SPL = 3
W_IN_UNITS = 9
W_OUT_UNITS = 4
FFN_UNITS = 6 * NFB
SLOTS = 128
PE_ROW = 3 * DEPTH * KC
SGB_ROW = PE_ROW + DEPTH * 2 * 16
N_ROWS = SGB_ROW + DEPTH * NH
GELU_C = 0.7978845608028654


def const_layout():
    at, out = 0, {}
    for name, n in (("ident", P), ("triu", P), ("mhalf", 8),
                    ("band", 12 * P), ("shift", 4 * P), ("causal", P),
                    ("before", P), ("ones", P), ("iota", P), ("cos", NT * 8), ("sin", NT * 8),
                    ("ccos", 8), ("csin", 8), ("cmask", NT * CP), ("cvalid", NT * CP), ("blk", NH)):
        out[name] = (at, n)
        at += n
    return out, at


def const_table():
    lay, width = const_layout()
    c = np.zeros((P, width), np.float32)

    def put(name, a):
        at, n = lay[name]
        a = np.asarray(a, np.float32).reshape(a.shape[0], -1)
        c[:a.shape[0], at:at + n] = a

    r = np.arange(P)
    put("ident", np.eye(P))
    t = np.arange(S)
    bands = []
    for win in POOLS:
        b = ((t[:, None] <= t[None, :]) & (t[:, None] > t[None, :] - win)) / np.minimum(t + 1, win)[None, :].astype(np.float32)
        bands.append(b.astype(np.float32) - np.eye(S, dtype=np.float32))
    bands = np.stack(bands, 1)
    put("band", np.stack([bands[:P, :, :P], bands[:P, :, P:], bands[P:, :, P:]], 1))
    put("shift", np.stack([r[None, :] == r[:, None] + 1, r[None, :] == r[:, None] + 2,
                           r[None, :] + P == r[:, None] + 1, r[None, :] + P == r[:, None] + 2], 1))
    put("causal", np.where(r[None, :] <= r[:, None], 0.0, NEG))
    put("triu", r[:, None] <= r[None, :])
    put("before", r[:, None] < r[None, :])
    put("ones", np.ones((P, P)))
    put("iota", np.tile(r[None, :], (P, 1)))
    inv = (THETA ** (-np.arange(8, dtype=np.float32) / 8)).astype(np.float32)
    ang = (t.astype(np.float32)[:, None] * inv).reshape(NT, P, 8).transpose(1, 0, 2)
    put("cos", np.cos(ang))
    put("sin", np.sin(ang))
    end = (np.arange(CP) * 16 + 31).astype(np.float32)
    put("ccos", np.cos(end[:, None] * inv))
    put("csin", np.sin(end[:, None] * inv))
    ok = (end[None, :] <= t[:, None]) & (np.arange(CP) < NCMP)[None, :]
    ok = ok.reshape(NT, P, CP).transpose(1, 0, 2)
    put("cmask", np.where(ok, 0.0, NEG))
    put("cvalid", ok)
    put("blk", r[:, None] // CP == np.arange(NH)[None, :])
    put("mhalf", np.full((P, 8), -0.5))
    return c


def spread(ap, axis, n):
    shape = list(ap.shape)
    shape[axis] = n
    return ap.broadcast_to(shape)


def bc(ap, axis, n):
    return spread(ap.unsqueeze(axis), axis, n)


def build(nc, x_in, attn_norm_g, w_in, q_norm_g, k_norm_g, cmp_pe, cmp_w1, cmp_w2, sgu_norm_g, sgu_w, sgu_b,
          pool_w, pool_scale, conv_w, mix_out_norm_g, w_out, ffn_norm_g, ffn_w1, ffn_w3, ffn_w2,
          router_w, expert_w1, expert_w3, expert_w2, consts, out):
    lay, cwidth = const_layout()
    ctx = ExitStack()
    with ctx:
        def sb(name, shape, dt=F32):
            return ctx.enter_context(nc.sbuf_tensor(name, shape, dt))

        def sem(name):
            return ctx.enter_context(nc.semaphore(name))

        raw = [sb(f"raw{i}", [P, UW]) for i in range(RAW)]
        whi = [sb(f"whi{i}", [P, UW], F32R) for i in range(SPL)]
        wlo = [sb(f"wlo{i}", [P, UW], F32R) for i in range(SPL)]
        ct = sb("ct", [P, cwidth])
        x = sb("x", [P, NT, D])
        xn = sb("xn", [P, NT, D])
        xTh = sb("xTh", [P, KC, S], F32R)
        xTl = sb("xTl", [P, KC, S], F32R)
        pr = sb("pr", [P, NT, D_IN])
        rows = pr[0:N_ROWS, 1, 0:P]
        cols = sb("cols", [P, N_ROWS])
        g6 = sb("g6", [P, 6, HD])
        gkc = sb("gkc", [P, HD])
        gsgu = sb("gsgu", [P, GW])
        psc = sb("psc", [P, GW])
        cw = sb("cw", [P, 3, GW])
        sgT = sb("sgT", [P, NH, P])
        pw = sb("pw", [P, NH, HD])
        big = sb("big", [P, 4096])
        w1c = big[:, :].rearrange("p (k a n) -> p k a n", k=2, a=16)
        w2c = sb("w2c", [P, 2, HD])
        rt = sb("rt", [P, KC, NE])
        ssx = sb("ssx", [P, NT, 2])
        rsx = sb("rsx", [P, NT])
        ss = sb("ss", [P, NT, 8])
        rs = sb("rs", [P, NT, 8])
        ssc = sb("ssc", [CP, 1])
        rsc = sb("rsc", [CP, 1])
        ssy = sb("ssy", [P, NT, NH])
        rsy = sb("rsy", [P, NT, NH])
        kd = xn[:, :, 2 * GW:3 * GW].rearrange("p t (j a d) -> p t j a d", j=2, a=2)
        zk = [xn[:, :, 0:GW], xn[:, :, GW:2 * GW], xn[:, :, 3 * GW:4 * GW]]
        tmp = sb("tmp", [P, NT, 6, HD])
        qk = sb("qk", [P, NT, 6, HD])
        rp = [xn[:, :, 2 * GW + 48 * i:2 * GW + 48 * (i + 1)].rearrange("p t (h f) -> p t h f", h=6) for i in range(4)]
        qT = pr[0:HD, :, CG:CG + 2 * GW].rearrange("p t (i s) -> p t i s", i=2)
        dlt = pr[HD:P, :, CG:CG + 2 * GW].rearrange("p t (i s) -> p t i s", i=2)
        sgw = qk[:].rearrange("p t h d -> p (t h d)")[:, 0:NH * P].rearrange("p (g s) -> p g s", g=NH)
        kT = sb("kT", [HD, 2, S])
        vn = tmp[:].rearrange("p t h d -> p t (h d)")[:, :, 0:GW]
        kvb = sb("kvb", [P, 2, 16, 16])
        hx = big[:, 3840:3840+2 * NCMP].rearrange("p (j n) -> p j n", j=2)
        hy = big[:, 3872:3872+2 * NCMP].rearrange("p (j n) -> p j n", j=2)
        hz = big[:, 3904:3904+2 * NCMP].rearrange("p (j n) -> p j n", j=2)
        hidp = sb("hidp", [P, 2, NH, CP])
        kcs = sb("kcs", [CP, 3, HD])
        krp = sb("krp", [CP, 4, 8])
        kcT = sb("kcT", [HD, CP])
        vbd = sb("vbd", [P, NH, HD])
        gates = sb("gates", [P, NT, NH, 3])
        sc = big[:, 0:2048].rearrange("p (i h s) -> p i h s", i=2, h=NH)
        scc = big[:, 3072:3328].rearrange("p (t h n) -> p t h n", t=NT, h=NH)
        mx = sb("mx", [P, 4, NH])
        sm = sb("sm", [P, 4, NH])
        cf = sb("cf", [P, 4, NH])
        mxc = sb("mxc", [P, NT, NH])
        smc = sb("smc", [P, NT, NH])
        pT = big[:, 2048:3072].rearrange("p (k h q) -> p k h q", k=2, h=NH)
        pcT = big[:, 3328:3584].rearrange("p (t q) -> p t q", t=NT)
        ot = big[:, 3584:3840]
        junk = qk[:, 0].rearrange("p h d -> p (h d)")[:, 0:GW]
        sg = pr[:, 1, 1024:2048].rearrange("p (t n) -> p t n", t=NT)
        gTh = sb("gTh", [P, NT, 4, P], F32R)
        gTl = sb("gTl", [P, NT, 4, P], F32R)
        gbc = pr[:, 0, 0:D]
        lg = sb("lg", [P, NT, NE])
        top = sb("top", [P, NT, 8])
        sel = sb("sel", [P, NT, NE])
        ra = sb("ra", [P, NT, NE])
        rb = sb("rb", [P, NT, NE])
        rsc1 = sb("rsc1", [P, NT])
        gate = sb("gate", [P, NT, NE])
        posm = sb("posm", [P, NT, NE])
        cnt = sb("cnt", [P, 2])
        flag = sb("flag", [P, 1], I32)
        ygh = xTh[:, :, SLOTS:2 * SLOTS]
        ygl = xTl[:, :, SLOTS:2 * SLOTS]
        onehot = pr[:, 1, 0:NT * SLOTS].rearrange("p (t s) -> p t s", t=NT)
        onehotT = sb("onehotT", [P, S], F32R)
        xgh = xTh[:, :, 0:SLOTS]
        xgl = xTl[:, :, 0:SLOTS]
        zero = sb("zero", [P, P], F32R)

        bank = [ctx.enter_context(nc.psum_tensor(f"bank{i}", [P, 512], F32)) for i in range(8)]

        def C(name, rows=P):
            at, n = lay[name]
            return ct[0:rows, at:at + n]

        ident = C("ident")

        def gain_col(gain, c):
            i = (gain % 3) * DEPTH * KC + gain // 3 * KC + c
            return cols[:, i:i + 1]

        s_const, s_tables, s_x, s_rows, s_sgw, s_lay = sem("const_in"), sem("tables_in"), sem("x_in"), sem("rows_in"), sem("sgu_w_in"), [sem("layer_in0"), sem("layer_in1")]
        s_gbc, s_rt = sem("ffn_gain_in"), sem("router_in")
        landed = [sem(f"landed{i}") for i in range(RAW)]
        s_hi, s_lo, used = sem("unit_hi"), sem("unit_lo"), sem("unit_used")
        x_sq, x_rstd, xn_ready = sem("x_sq"), sem("x_rstd"), sem("xn_ready")
        xT_psum, xTh_ready, xTl_ready = sem("xT_psum"), sem("xTh_ready"), sem("xTl_ready")
        pr_ready = sem("proj_ready")
        rowsT_psum, cols_ready = sem("rowsT_psum"), sem("cols_ready")
        sguT_psum, sguT_ready = sem("sguT_psum"), sem("sguT_ready")
        kd_ready, kdT_psum, kvb_ready = sem("kd_ready"), sem("kdT_psum"), sem("kvb_ready")
        hid_psum, gelu_in, gelu_e, hid_ready = sem("hid_psum"), sem("gelu_in"), sem("gelu_exp"), sem("hid_ready")
        kcvc_psum, kc_ss, kc_rstd, kc_ready = sem("kcvc_psum"), sem("kc_ss"), sem("kc_rstd"), sem("kc_ready")
        kcT_psum, kcT_ready, vbd_ready = sem("kcT_psum"), sem("kcT_ready"), sem("vbd_ready")
        z_ready, qk_ss, v_ss, qk_rstd = sem("z_ready"), sem("qk_ss"), sem("v_ss"), sem("qk_rstd")
        qk_ready, vn_ready = sem("qk_ready"), sem("vn_ready")
        qkT_psum, qkT_ready = sem("qkT_psum"), sem("qkT_ready")
        dlt_psum, dlt_ready, poolY_psum = sem("dlt_psum"), sem("dlt_ready"), sem("poolY_psum")
        conv_psum, sgu_psum, mix_done = sem("conv_psum"), sem("sgu_psum"), sem("mix_evacuated")
        gate_e = sem("gate_exp")
        cs_psum, cs_in, cs_exp, cs_ready = sem("cmp_scores"), sem("cmp_masked"), sem("cmp_exp"), sem("cmp_probs")
        cT_psum, cT_ready, co_psum, co_done = sem("cmpT_psum"), sem("cmpT_ready"), sem("cmp_out"), sem("cmp_out_used")
        a_s, a_max, a_exp = sem("scores"), sem("score_max"), sem("probs")
        a_T, a_Tr, a_o, a_done = sem("probsT"), sem("probsT_copied"), sem("attn_out"), sem("attn_out_used")
        y_sq, y_rstd, yn_ready = sem("y_sq"), sem("y_rstd"), sem("yn_ready")
        x_mid = sem("x_plus_mixer")
        silu_done, g_ready, gT_psum, gTh_ready, gTl_ready = (sem("silu_done"), sem("g_ready"), sem("gT_psum"),
                                                             sem("gTh_ready"), sem("gTl_ready"))
        y_added = sem("dense_y_added")
        lg_psum, lg_ready, lg_exp = sem("logits_psum"), sem("top2_in"), sem("top2_exp")
        sel_ready, pos_psum, route_ready = sem("sel_ready"), sem("pos_psum"), sem("route_ready")
        zero_ready, hp_ready, g6_ready = sem("zero_ready"), sem("hidp_zeroed"), sem("g6_scaled")
        oh_ready, xg_psum, xgh_ready, xgl_ready = sem("onehot"), sem("gathered"), sem("xgh_ready"), sem("xgl_ready")
        ohT_psum, ohT_ready, ygh_ready, ygl_ready, sc_psum, sc_done = (sem("onehotT_psum"), sem("onehotT"), sem("ygh_ready"), sem("ygl_ready"),
                                                           sem("scattered"), sem("scatter_added"))
        dve_order, pool_order = sem("dve_order"), sem("pool_order")
        s_done, s_out = sem("x_final"), sem("out_stored")

        WIN = [0, W_IN_UNITS + W_OUT_UNITS + FFN_UNITS]
        WOUT = [n + W_IN_UNITS for n in WIN]
        DENSE = WOUT[0] + W_OUT_UNITS
        MOE = WOUT[1] + W_OUT_UNITS
        MOE2 = MOE + NE * FFN_UNITS
        HEAD = lay["band"][0]
        LAY_LOADED = 16 * 11

        class Unit:

            def __init__(self, base, rounds=0, slots_ahead=0):
                self.base, self.rounds, self.ahead = base, rounds, slots_ahead
                self.raw = raw[base % RAW]
                self.landed = landed[base % RAW]
                self.hi, self.lo = whi[base % SPL], wlo[base % SPL]
                self.n = base + rounds
                self.turn = base // RAW + slots_ahead

        def load_unit(sp, u, src, words):
            if u.base >= RAW:
                sp.wait_ge(s_lo, u.n - RAW + 1)
            sp.dma_start(words(u.raw), src).then_inc(u.landed, 16)

        def round_unit(act, u, n=UW):
            act.wait_ge(u.landed, 16 * (u.turn + 1))
            if u.base >= SPL:
                act.wait_ge(used, u.n - SPL + 1)
            nc.scalar.activation(u.hi[:, 0:n], u.raw[:, 0:n], ACT.Copy).then_inc(s_hi, 1)

        def rest_unit(dve, u, n=UW):
            dve.wait_ge(s_hi, u.n + 1)
            nc.vector.tensor_tensor(u.lo[:, 0:n], u.raw[:, 0:n], u.hi[:, 0:n].bitcast(F32), ALU.subtract).then_inc(s_lo, 1)

        def in_words(n):
            return (4 * FB) if n < W_IN_UNITS - 1 else KC * (D_IN - 4 * FB)

        def xT_bank(k, c):
            return bank[(2 if k == 3 and c < 4 else 4) + c // 2][:, (c % 2) * S:(c % 2 + 1) * S]

        def x_half(k, h):
            if k == 0:
                return s_x, 16
            if k == 3:
                return y_added, 4 * NFB - 2 + 2 * h
            return x_mid, 4 * (k // 3) + 2 * (h + 1)

        def three_passes(o, xh, xl, wh, wl, start, stop):
            nc.tensor.matmul(o, xh, wh, start=start, stop=False)
            nc.tensor.matmul(o, xh, wl, start=False, stop=False)
            return nc.tensor.matmul(o, xl, wh, start=False, stop=stop)

        block = ctx.enter_context(nc.Block())

        @block.sync
        def _(sp):
            sp.dma_start(x[:], x_in.rearrange("(t p) d -> p t d", p=P)).then_inc(s_x, 16)
            sp.dma_start(ct[:, 0:HEAD], consts[:, 0:HEAD]).then_inc(s_const, 16)
            for j, g in enumerate((attn_norm_g, mix_out_norm_g, ffn_norm_g)):
                sp.dma_start(rows[j * DEPTH * KC:(j + 1) * DEPTH * KC, :], g.rearrange("l (c p) -> (l c) p", p=P)).then_inc(s_rows, 16)
            sp.dma_start(rows[PE_ROW:SGB_ROW, :], cmp_pe.rearrange("l k (a two) d -> (l k a) (two d)", two=2)).then_inc(s_rows, 16)
            sp.dma_start(rows[SGB_ROW:N_ROWS, :], sgu_b.rearrange("l g t -> (l g) t")).then_inc(s_rows, 16)

            def mixer_weights(L):
                for n in range(W_IN_UNITS):
                    if L == 0 and n == RAW:
                        sp.dma_start(ct[:, HEAD:], consts[:, HEAD:]).then_inc(s_tables, 16)
                    src = w_in[L].rearrange("(c p) n -> p c n", p=P)
                    if n < W_IN_UNITS - 1:
                        b, h = n // 2, n % 2
                        src = src[:, 4 * h:4 * h + 4, b * FB:(b + 1) * FB]
                        load_unit(sp, Unit(WIN[L] + n), src, lambda r: r[:, :].rearrange("p (c n) -> p c n", c=4))
                    else:
                        src = src[:, :, 4 * FB:D_IN]
                        load_unit(sp, Unit(WIN[L] + n), src,
                                  lambda r: r[:, 0:in_words(8)].rearrange("p (c n) -> p c n", c=KC))
                for n in range(W_OUT_UNITS):
                    b, h = n // 2, n % 2
                    src = w_out[L].rearrange("(c p) n -> p c n", p=P)[:, 4 * h:4 * h + 4, b * FB:(b + 1) * FB]
                    load_unit(sp, Unit(WOUT[L] + n), src, lambda r: r[:, :].rearrange("p (c n) -> p c n", c=4))

            def in_block(u0, rounds, turns, w1, w3, f):
                j = 0
                for w in (w1, w3):
                    for h in range(2):
                        src = w.rearrange("(c p) n -> p c n", p=P)[:, 4 * h:4 * h + 4, ds(f * FB, FB)]
                        load_unit(sp, Unit(u0 + j, rounds, turns), src,
                                  lambda r: r[:, :].rearrange("p (c n) -> p c n", c=4))
                        j += 1

            def out_block(u0, rounds, turns, w2, f):
                for h in range(2):
                    src = w2[ds(f * FB, FB), h * FB:(h + 1) * FB].rearrange("(c p) n -> p c n", p=P)
                    load_unit(sp, Unit(u0 + h, rounds, turns), src,
                              lambda r: r[:, :].rearrange("p (c n) -> p c n", c=4))

            def ffn_weights(base, rounds, turns, w1, w3, w2):
                in_block(base, rounds, turns, w1, w3, 0)
                with sp.Fori(1, NFB) as f:
                    in_block(base + 4, rounds + (f - 1) * 6, turns + (f - 1), w1, w3, f)
                    out_block(base + 8, rounds + (f - 1) * 6, turns + (f - 1), w2, f - 1)
                out_block(base + FFN_UNITS - 2, rounds, turns, w2, NFB - 1)

            def expert(w, e):
                return w[0, ds(e, 1)].rearrange("a k n -> (a k) n")

            mixer_weights(0)
            ffn_weights(DENSE, 0, 0, ffn_w1[0], ffn_w3[0], ffn_w2[0])
            mixer_weights(1)

            def experts(base):
                with sp.Fori(0, NE) as e:
                    ffn_weights(base, e * FFN_UNITS, e * (FFN_UNITS // RAW),
                                expert(expert_w1, e), expert(expert_w3, e), expert(expert_w2, e))

            experts(MOE)
            sp.wait_ge(route_ready, 1)
            more = sp.value_load(flag[0:1, 0:1], min_val=0, max_val=1)
            with sp.If(more > 0):
                experts(MOE2)
            sp.wait_ge(s_done, 1)
            sp.dma_start(out.rearrange("(t p) d -> p t d", p=P), x[:]).then_inc(s_out, 16)
            sp.wait_ge(s_out, 16)

        @block.gpsimd
        def _(pool):
            count = [0]

            def small(dst, src, s):
                pool.dma_start(dst, src, allow_slow_non_contiguous=True).then_inc(s, 16)

            def layer_weights(L):
                small(sgw[:], sgu_w[L].rearrange("g t s -> t g s"), s_sgw)
                for k in range(2):
                    small(w1c[:, k], cmp_w1[L, k].rearrange("(a p) n -> p a n", p=P), s_lay[L])
                    small(w2c[:, k], cmp_w2[L, k], s_lay[L])
                small(cw[:], spread(conv_w[L:L + 1], 0, P), s_lay[L])
                small(g6[:, 0:NH, :], spread(bc(q_norm_g[L:L + 1], 1, NH), 0, P), s_lay[L])
                small(g6[:, NH:NH + 2, :], spread(k_norm_g[L:L + 1, 1:3], 0, P), s_lay[L])
                small(gkc[:], spread(k_norm_g[L, 0:1], 0, P), s_lay[L])
                small(gsgu[:], spread(sgu_norm_g[L:L + 1], 0, P), s_lay[L])
                small(psc[:], spread(pool_scale[L:L + 1], 0, P), s_lay[L])
                small(pw[HD:P], pool_w[L].rearrange("g c d -> c g d"), s_lay[L])

            def rsqrt(outp, inp, n, wait, value, done):
                pool.wait_ge(wait, value)
                nc.gpsimd.tensor_scalar(inp, inp, 1.0 / n, EPS, ALU.mult, ALU.add).then_inc(pool_order, 1)
                count[0] += 1
                pool.wait_ge(pool_order, count[0])
                w = inp.shape[-1]
                nc.gpsimd.tensor_tensor(outp, inp, C("mhalf", inp.shape[0])[:, 0:w], ALU.pow).then_inc(done, 1)

            def x_statistics(n):
                pool.wait_ge(x_sq, 4 * (n + 1))
                nc.gpsimd.tensor_tensor(ssx[:, :, 0], ssx[:, :, 0], ssx[:, :, 1], ALU.add).then_inc(pool_order, 1)
                count[0] += 1
                rsqrt(rsx[:], ssx[:, :, 0], D, pool_order, count[0], x_rstd)

            pool.wait_ge(s_const, 16)
            for L in range(DEPTH):
                x_statistics(2 * L)
                if L == 0:
                    layer_weights(0)
                    small(rt[:], router_w[0].rearrange("(c p) e -> p c e", p=P), s_rt)
                pool.wait_ge(v_ss, 2 * (L + 1))
                pool.wait_ge(qk_ss, L + 1)
                nc.gpsimd.tensor_scalar(ss[:, :, 0:6], ss[:, :, 0:6], 1.0 / HD, EPS, ALU.mult, ALU.add).then_inc(pool_order, 1)
                nc.gpsimd.tensor_scalar(ss[:, :, 6:7], ss[:, :, 6:7], 1.0 / GW, EPS, ALU.mult, ALU.add).then_inc(pool_order, 1)
                count[0] += 2
                pool.wait_ge(pool_order, count[0])
                for t in range(NT):
                    nc.gpsimd.tensor_tensor(rs[:, t, 0:7], ss[:, t, 0:7], C("mhalf")[:, 0:7], ALU.pow).then_inc(qk_rstd, 1)
                rsqrt(rsc[:], ssc[:], HD, kc_ss, L + 1, kc_rstd)
                rsqrt(rsy[:, 0, :], ssy[:, 0, :], GW, y_sq, 8 * L + 4, y_rstd)
                rsqrt(rsy[:, 1, :], ssy[:, 1, :], GW, y_sq, 8 * L + 8, y_rstd)
                if L == 0:
                    pool.wait_ge(yn_ready, 2)
                    layer_weights(1)
                x_statistics(2 * L + 1)
            pool.wait_ge(y_sq, 16)
            small(gbc, spread(ffn_norm_g[1:2], 0, P), s_gbc)

        @block.scalar
        def _(act):
            def square_x(n, k, h):
                act.wait_ge(*x_half(k, h))
                if n:
                    act.wait_ge(x_rstd, n)
                for t in range(NT):
                    nc.scalar.activation(xn[:, t, h * FB:(h + 1) * FB], x[:, t, h * FB:(h + 1) * FB], ACT.Square,
                                         accum_out=ssx[:, t, h:h + 1]).then_inc(x_sq, 1)

            def split_hi(k, gain, chunks=range(KC)):
                for c in chunks:
                    act.wait_ge(xT_psum, 8 * k + c // 2 * 2 + 2)
                    nc.scalar.activation(xTh[:, c, :], xT_bank(k, c), ACT.Copy, scale=gain_col(gain, c)).then_inc(xTh_ready, 1)

            def next_operand(n, k, base, ahead):
                for i in range(ahead):
                    round_unit(act, Unit(base + i))
                square_x(n, k, 0)
                split_hi(k, k, range(0, 4))
                for i in range(ahead, SPL):
                    round_unit(act, Unit(base + i))
                square_x(n, k, 1)
                split_hi(k, k, range(4, 8))

            def mixer(L):
                units = [Unit(WIN[L] + n) for n in range(W_IN_UNITS)]
                if L == 0:
                    act.wait_ge(cols_ready, 1)
                    for h in range(2):
                        split_hi(0, 0, range(4 * h, 4 * h + 4))
                        round_unit(act, units[h])
                    for h in range(2):
                        square_x(0, 0, h)
                    round_unit(act, units[2])
                act.wait_ge(x_rstd, 2 * L + 1)
                for c in range(5):
                    for n in (2 * c + 3, 2 * c + 4):
                        if n < W_IN_UNITS:
                            round_unit(act, units[n], in_words(n))
                    act.wait_ge(used, WIN[L] + min(2 * c + 2, W_IN_UNITS))
                    n = min(FB, D_IN - c * FB)
                    for t in range(NT):
                        nc.scalar.activation(pr[:, t, c * FB:c * FB + n], bank[2 * (c % 2) + t][:, 0:n], ACT.Copy,
                                             scale=rsx[:, t:t + 1]).then_inc(pr_ready, 1)
                act.wait_ge(sguT_psum, L + 1)
                act.wait_ge(pr_ready, 10 * (L + 1))
                nc.scalar.activation(gates[:].rearrange("p t h b -> p t (h b)"), pr[:, :, GT:GT + 12], ACT.Exp,
                                     scale=-1.0).then_inc(gate_e, 1)
                for t in range(NT):
                    nc.scalar.activation(junk[:, :], pr[:, t, V0:V0 + GW], ACT.Square,
                                         accum_out=ss[:, t, 6:7]).then_inc(v_ss, 1)
                    act.wait_ge(v_ss, 2 * L + t + 1)
                wout = [Unit(WOUT[L] + n) for n in range(W_OUT_UNITS)]
                for n in range(SPL):
                    round_unit(act, wout[n])
                act.wait_ge(z_ready, 3 * (L + 1))
                for j in range(2):
                    act.wait_ge(dlt_psum, 2 * L + j + 1)
                    nc.scalar.copy(dlt[:, j], bank[j][0:HD, :].rearrange("p (g s) -> p g s", g=2)).then_inc(dlt_ready, 1)
                act.wait_ge(gelu_in, L + 1)
                nc.scalar.activation(hz[:], hy[:], ACT.Exp, scale=-2.0 * GELU_C).then_inc(gelu_e, 1)
                for j in range(3):
                    act.wait_ge(qkT_psum, 3 * L + j + 1)
                    nc.scalar.copy(qT[:, j] if j < 2 else kT[:],
                                   bank[[6, 7, 4][j]][0:HD, :].rearrange("p (h s) -> p h s", h=2)).then_inc(qkT_ready, 1)
                def probs(i):
                    act.wait_ge(a_max, 4 * L + i + 1)
                    for h in range(NH):
                        n = P * (i % 2 + 1)
                        nc.scalar.activation(sc[:, i % 2, h, 0:n], sc[:, i % 2, h, 0:n], ACT.Exp,
                                             bias=mx[:, i, h:h + 1], accum_out=sm[:, i, h:h + 1]).then_inc(a_exp, 1)

                probs(0)
                act.wait_ge(cs_in, L + 1)
                nc.scalar.activation(scc[:], scc[:], ACT.Exp).then_inc(cs_exp, 1)
                act.wait_ge(cT_psum, L + 1)
                nc.scalar.copy(pcT[:].rearrange("p t q -> p (t q)"), bank[7][:, 0:NT * P]).then_inc(cT_ready, 1)
                for i in range(4):
                    t, k = i % 2, 4 * L + i
                    if i:
                        probs(i)
                    for kt in range(t + 1):
                        act.wait_ge(a_T, 6 * L + [0, 1, 3, 4][i] + kt + 1)
                        if k:
                            act.wait_ge(a_o, k)
                        nc.scalar.copy(pT[:, kt], bank[4 + kt][:, :].rearrange("p (h q) -> p h q", h=NH)).then_inc(a_Tr, 1)
                act.wait_ge(mix_done, 6 * (L + 1))
                act.wait_ge(a_done, 4 * (L + 1))
                for t in range(NT):
                    for m in range(4):
                        nc.scalar.activation(junk[:, :], xn[:, t, m * GW:(m + 1) * GW], ACT.Square,
                                             accum_out=ssy[:, t, m:m + 1]).then_inc(y_sq, 1)
                        act.wait_ge(y_sq, 8 * L + 4 * t + m + 1)
                split_hi(3 * L + 1, 3 * L + 1)
                round_unit(act, wout[3])

            def silu(value, k, tiles, normed=True):
                act.wait_ge(used, value)
                act.wait_ge(gT_psum, k * tiles)
                for t in range(tiles):
                    nc.scalar.activation(sg[:, t, :], bank[t][:, :], ACT.Silu,
                                         scale=1.0 if normed else rsx[:, t:t + 1]).then_inc(silu_done, 1)

            def split_g(k, tiles, at=0):
                for t in range(tiles):
                    act.wait_ge(gT_psum, k * tiles + t + 1)
                    nc.scalar.copy(gTh[:, at + t], bank[4 + t][:, :].rearrange("p (c s) -> p c s", c=4)).then_inc(gTh_ready, 1)

            def step(base, rounds, turns, k, tiles, at=0, normed=True):
                for n in range(4):
                    round_unit(act, Unit(base + n, rounds, turns))
                silu(base + rounds + 2, k, tiles, normed)
                split_g(k - 1, tiles, at)
                for n in range(4, 6):
                    round_unit(act, Unit(base + n, rounds, turns))

            def dense():
                round_unit(act, Unit(DENSE + 3))
                act.wait_ge(x_rstd, 2)
                silu(DENSE + 2, 0, NT, False)
                with act.Fori(1, NFB) as f:
                    step(DENSE + 4, (f - 1) * 6, f - 1, f, NT, normed=False)
                for n in range(FFN_UNITS - 2, FFN_UNITS):
                    round_unit(act, Unit(DENSE + n))
                split_g(NFB - 1, NT)

            mixer(0)
            next_operand(1, 2, DENSE, 1)
            dense()
            next_operand(2, 3, WIN[1], 2)
            mixer(1)
            next_operand(3, 5, MOE, 1)
            act.wait_ge(lg_ready, 1)
            nc.scalar.activation(ra[:], ra[:], ACT.Exp).then_inc(lg_exp, 1)

            def split_gathered(k):
                for j in range(2):
                    act.wait_ge(xg_psum, 2 * k + j + 1)
                    nc.scalar.copy(xgh[:, 4 * j:4 * j + 4, :],
                                   bank[1 + 2 * j][:, :].rearrange("p (c s) -> p c s", c=4)).then_inc(xgh_ready, 1)

            def copy_onehot(k):
                act.wait_ge(ohT_psum, k + 1)
                nc.scalar.copy(onehotT[:, :], bank[5][:, 0:NT * P]).then_inc(ohT_ready, 1)

            def blocks(base, rounds, turns, k, follows):
                kb = k * NFB + NT * NFB
                with act.Fori(1, NFB) as f:
                    step(base + 4, rounds + (f - 1) * 6, turns + (f - 1), kb + f, 1)
                copy_onehot(k)
                round_unit(act, Unit(base + FFN_UNITS - 2, rounds, turns))
                if follows:
                    split_gathered(k + 1)
                round_unit(act, Unit(base + FFN_UNITS - 1, rounds, turns))
                split_g(kb + NFB - 1, 1, 1)
                if follows:
                    for n in range(3):
                        round_unit(act, Unit(base + FFN_UNITS + n, rounds, turns))
                act.wait_ge(used, base + rounds + FFN_UNITS)
                for j in range(2):
                    nc.scalar.copy(ygh[:, 4 * j:4 * j + 4, :],
                                   bank[6 + j][:, :].rearrange("p (c n) -> p c n", c=4)).then_inc(ygh_ready, 1)
                if follows:
                    round_unit(act, Unit(base + FFN_UNITS + 3, rounds, turns))
                    silu(base + rounds + FFN_UNITS + 2, kb + NFB, 1)

            def experts(base, k0):
                split_gathered(k0)
                for n in range(0 if k0 else SPL, 4):
                    round_unit(act, Unit(base + n))
                silu(base + 2, k0 * NFB + NT * NFB, 1)
                with act.Fori(0, NE - 1) as e:
                    blocks(base, e * FFN_UNITS, e * (FFN_UNITS // RAW), k0 + e, True)
                last = (NE - 1) * FFN_UNITS
                blocks(base + last, 0, 0, k0 + NE - 1, False)

            experts(MOE, 0)
            act.wait_ge(route_ready, 1)
            more = act.value_load(flag[0:1, 0:1], min_val=0, max_val=1)
            with act.If(more > 0):
                experts(MOE2, NE)

        @block.vector
        def _(dve):
            V = nc.vector
            count = [0]

            def link(ins):
                count[0] += 1
                ins.then_inc(dve_order, 1)
                dve.wait_ge(dve_order, count[0])

            def settle(*ins):
                for i in ins:
                    count[0] += 1
                    i.then_inc(dve_order, 1)
                dve.wait_ge(dve_order, count[0])

            def tt(o, a, b, op):
                return V.tensor_tensor(o, a, b, op)

            def split_lo(k, gain, chunks=range(KC)):
                for c in chunks:
                    dve.wait_ge(xTh_ready, 8 * k + c // 2 * 2 + 2)
                    V.scalar_tensor_tensor(xTl[:, c, :], xT_bank(k, c), gain_col(gain, c), xTh[:, c, :].bitcast(F32), ALU.mult,
                                           ALU.subtract).then_inc(xTl_ready, 1)

            def rope(q, cos, sin, scr):
                a, b = q[..., 0:8] if len(q.shape) == 2 else q[:, :, :, 0:8], q[..., 8:16] if len(q.shape) == 2 else q[:, :, :, 8:16]
                settle(tt(scr[0], a, cos, ALU.mult), tt(scr[1], b, sin, ALU.mult),
                       tt(scr[2], a, sin, ALU.mult), tt(scr[3], b, cos, ALU.mult))
                return tt(a, scr[0], scr[1], ALU.subtract), tt(b, scr[2], scr[3], ALU.add)

            def mixer(L):
                units = [Unit(WIN[L] + n) for n in range(W_IN_UNITS)]
                if L == 0:
                    dve.wait_ge(rowsT_psum, 1)
                    V.tensor_copy(cols[:, :], bank[1][:, 0:N_ROWS]).then_inc(cols_ready, 1)
                    dve.wait_ge(cols_ready, 1)
                    for h in range(2):
                        split_lo(0, 0, range(4 * h, 4 * h + 4))
                        rest_unit(dve, units[h])
                    rest_unit(dve, units[2])
                for n in range(SPL, W_IN_UNITS):
                    rest_unit(dve, units[n], in_words(n))
                    if n == 5:
                        dve.wait_ge(sguT_psum, L + 1)
                        tt(sgT[:], bank[4][:, :].rearrange("p (g t) -> p g t", g=NH), bc(C("triu"), 1, NH),
                           ALU.mult).then_inc(sguT_ready, 1)
                wout = [Unit(WOUT[L] + n) for n in range(W_OUT_UNITS)]
                if L == 0:
                    dve.wait_ge(s_tables, 16)
                def scores(i):
                    t = i % 2
                    dve.wait_ge(a_s, 4 * L + i + 1)
                    if 4 * L + i >= 2:
                        dve.wait_ge(a_T, 6 * (L if i >= 2 else L - 1) + [4, 6, 1, 3][i])
                    b0 = 2 * (i % 2)
                    if t == 0:
                        link(tt(sc[:, 0, :, 0:P], bank[b0][:, :].rearrange("p (h k) -> p h k", h=NH), bc(C("causal"), 1, NH), ALU.add))
                    else:
                        done = []
                        for j in range(2):
                            src = bank[b0 + j][:, :].rearrange("p (h k) -> p h k", h=2)
                            done.append(V.tensor_copy(sc[:, 1, 2 * j:2 * j + 2, 0:P], src[:, :, 0:P]))
                            done.append(tt(sc[:, 1, 2 * j:2 * j + 2, P:S], src[:, :, P:S], bc(C("causal"), 1, 2), ALU.add))
                        settle(*done)
                    V.tensor_reduce(mx[:, i, :], sc[:, i % 2, :, 0:P * (t + 1)], AX_X, ALU.max, negate=True).then_inc(a_max, 1)

                dve.wait_ge(pr_ready, 10 * (L + 1))
                for t in range(NT):
                    V.tensor_copy(kd[:, t], bc(pr[:, t, KCM:KCM + 2 * HD].rearrange("p (j d) -> p j d", j=2), 2, 2)).then_inc(kd_ready, 1)
                a = tt(tmp[:, :, 0:4, :].rearrange("p t h d -> p t (h d)"), pr[:, :, 0:GW], pr[:, :, 0:GW], ALU.mult)
                b = tt(tmp[:, :, 4, :], pr[:, :, KS:KS + HD], pr[:, :, KS:KS + HD], ALU.mult)
                c = tt(tmp[:, :, 5, :], pr[:, :, KW:KW + HD], pr[:, :, KW:KW + HD], ALU.mult)
                settle(a, b, c)
                V.tensor_reduce(ss[:, :, 0:6], tmp[:], AX_X, ALU.add).then_inc(qk_ss, 1)
                dve.wait_ge(s_lay[L], LAY_LOADED)
                link(V.tensor_scalar(g6[:, 0:NH, :], g6[:, 0:NH, :], HD ** -0.5, None, ALU.mult))
                z = tmp[:, :, :, :].rearrange("p t h d -> p t (h d)")[:, :, 0:GW]
                dve.wait_ge(qk_ss, L + 1)
                link(tt(z, pr[:, :, CG:CG + GW], pr[:, :, HIN:HIN + GW], ALU.mult))
                for k in range(3):
                    tt(zk[k], z, bc(cw[:, k, :], 1, NT), ALU.mult).then_inc(z_ready, 1)
                dve.wait_ge(kdT_psum, L + 1)
                peT = cols[:, PE_ROW + L * 32:PE_ROW + (L + 1) * 32].rearrange("p (k a) -> p k a", k=2)
                for s in range(2):
                    half = slice(s * HD, (s + 1) * HD)
                    for hi in range(2):
                        src = bank[4][half, :].rearrange("p (j n a two) -> p j n a two", j=2, n=16, two=2)[:, :, hi:hi + NCMP, :, s]
                        dst = kvb[half, :, 8 * hi:8 * hi + 8, 0:NCMP].rearrange("p j a n -> p j n a")
                        for j in range(2):
                            tt(dst[:, j], src[:, j], bc(peT[half, j, 8 * hi:8 * hi + 8], 1, NCMP), ALU.add).then_inc(kvb_ready, 1)
                dve.wait_ge(qk_rstd, 2 * (L + 1))
                a = tt(qk[:, :, 0:4, :], pr[:, :, 0:GW].rearrange("p t (h d) -> p t h d", h=NH), bc(rs[:, :, 0:4], 3, HD), ALU.mult)
                b = tt(qk[:, :, 4, :], pr[:, :, KS:KS + HD], bc(rs[:, :, 4], 2, HD), ALU.mult)
                c = tt(qk[:, :, 5, :], pr[:, :, KW:KW + HD], bc(rs[:, :, 5], 2, HD), ALU.mult)
                settle(a, b, c)
                qf = qk[:].rearrange("p t h d -> p t (h d)")
                link(tt(qf, qf, bc(g6[:].rearrange("p h d -> p (h d)"), 1, NT), ALU.mult))
                cos = bc(C("cos").rearrange("p (t f) -> p t f", t=NT), 2, 6)
                sin = bc(C("sin").rearrange("p (t f) -> p t f", t=NT), 2, 6)
                for i in rope(qk, cos, sin, rp):
                    i.then_inc(qk_ready, 1)
                for t in range(NT):
                    V.scalar_tensor_tensor(vn[:, t, :], pr[:, t, V0:V0 + GW], rs[:, t, 6:7], gsgu[:, :], ALU.mult,
                                           ALU.mult).then_inc(vn_ready, 1)
                dve.wait_ge(gate_e, L + 1)
                gf = gates[:].rearrange("p t h b -> p (t h b)")
                link(V.tensor_scalar(gf, gf, 1.0, None, ALU.add))
                link(V.reciprocal(gf, gf))
                for n in range(SPL):
                    rest_unit(dve, wout[n])
                dve.wait_ge(hid_psum, L + 1)
                link(V.tensor_copy(hx[:], bank[5][:, 0:2 * CP].rearrange("p (j n) -> p j n", j=2)[:, :, 0:NCMP]))
                link(tt(hy[:], hx[:], hx[:], ALU.mult))
                link(V.tensor_scalar(hy[:], hy[:], 0.044715, 1.0, ALU.mult, ALU.add))
                link(tt(hz[:], hy[:], hx[:], ALU.mult))
                V.tensor_copy(hy[:], hz[:]).then_inc(gelu_in, 1)
                dve.wait_ge(conv_psum, L + 1)
                tt(xn[:, :, 3 * GW:4 * GW], bank[3][:, :].rearrange("p (t d) -> p t d", t=NT), pr[:, :, BG:BG + GW],
                   ALU.mult).then_inc(mix_done, 1)
                dve.wait_ge(gelu_e, L + 1)
                link(V.tensor_scalar(hy[:], hz[:], 1.0, None, ALU.add))
                link(V.reciprocal(hz[:], hy[:]))
                for j in range(2):
                    tt(hidp[:, j, :, 0:NCMP], bc(hx[:, j], 1, NH), bc(hz[:, j], 1, NH), ALU.mult).then_inc(hid_ready, 1)
                dve.wait_ge(kcvc_psum, L + 1)
                link(V.tensor_copy(kcs[:, 0, :], bank[5][0:CP, 128:192]))
                link(tt(kcs[:, 1, :], kcs[:, 0, :], kcs[:, 0, :], ALU.mult))
                V.tensor_reduce(ssc[:], kcs[:, 1, :], AX_X, ALU.add).then_inc(kc_ss, 1)
                tt(vbd[:], bc(bank[5][:, 192:256], 1, NH), bc(C("blk"), 2, HD), ALU.mult).then_inc(vbd_ready, 1)
                scores(0)
                dve.wait_ge(poolY_psum, L + 1)
                tt(xn[:, :, 2 * GW:3 * GW], bank[2][:, :].rearrange("p (t d) -> p t d", t=NT), bc(psc[:, :], 1, NT),
                   ALU.mult).then_inc(mix_done, 1)
                dve.wait_ge(kc_rstd, L + 1)
                link(V.scalar_tensor_tensor(kcs[:, 2, :], kcs[:, 0, :], rsc[:, 0:1], gkc[0:CP, :], ALU.mult, ALU.mult))
                for i in rope(kcs[:, 2, :], C("ccos", CP), C("csin", CP), [krp[:, i, :] for i in range(4)]):
                    i.then_inc(kc_ready, 1)
                dve.wait_ge(kcT_psum, L + 1)
                V.tensor_copy(kcT[:], bank[5][0:HD, 256:256 + CP]).then_inc(kcT_ready, 1)
                dve.wait_ge(cs_psum, L + 1)
                for t in range(NT):
                    i = tt(scc[:, t], bank[6][:, t * P:(t + 1) * P].rearrange("p (h n) -> p h n", h=NH),
                           bc(C("cmask")[:, t * CP:(t + 1) * CP], 1, NH), ALU.add)
                    count[0] += 1
                    i.then_inc(dve_order, 1)
                dve.wait_ge(dve_order, count[0])
                link(V.tensor_reduce(mxc[:], scc[:], AX_X, ALU.max))
                tt(scc[:], scc[:], bc(mxc[:], 3, CP), ALU.subtract).then_inc(cs_in, 1)

                dve.wait_ge(sgu_psum, L + 1)
                for g in range(NH):
                    V.scalar_tensor_tensor(xn[:, :, GW + g * HD:GW + (g + 1) * HD],
                                           bank[1][:, :].rearrange("p (t d) -> p t d", t=NT)[:, :, g * HD:(g + 1) * HD],
                                           cols[:, SGB_ROW + L * NH + g:SGB_ROW + L * NH + g + 1], pr[:, :, U0 + g * HD:U0 + (g + 1) * HD], ALU.add,
                                           ALU.mult).then_inc(mix_done, 1)
                dve.wait_ge(cs_exp, L + 1)
                link(V.tensor_reduce(smc[:], scc[:], AX_X, ALU.add))
                a = V.reciprocal(smc[:], smc[:])
                b = tt(scc[:], scc[:], bc(C("cvalid").rearrange("p (t n) -> p t n", t=NT), 2, NH), ALU.mult)
                b.then_inc(cs_ready, 1)
                link(a)
                link(tt(smc[:], smc[:], gates[:, :, :, 0], ALU.mult))
                scores(1)
                dve.wait_ge(co_psum, L + 1)
                for t in range(NT):
                    tt(xn[:, t, 0:GW].rearrange("p (h d) -> p h d", h=NH),
                       bank[7][:, t * GW:(t + 1) * GW].rearrange("p (h d) -> p h d", h=NH), bc(smc[:, t, :], 2, HD),
                       ALU.mult).then_inc(co_done, 1)
                for i in range(4):
                    t, br = i % 2, i // 2
                    if i + 2 < 4:
                        nxt = i + 2
                    else:
                        nxt = None
                    dve.wait_ge(a_exp, 4 * (4 * L + i + 1))
                    link(V.reciprocal(cf[:, i, :], sm[:, i, :]))
                    link(tt(cf[:, i, :], cf[:, i, :], gates[:, t, :, 1 + br], ALU.mult))
                    if nxt is not None:
                        scores(nxt)
                    dve.wait_ge(a_o, 4 * L + i + 1)
                    dve.wait_ge(co_done, 2 * L + 2)
                    o = bank[6 + i % 2][:, 0:GW]
                    link(tt(ot[:, :].rearrange("p (h d) -> p h d", h=NH), o.rearrange("p (h d) -> p h d", h=NH),
                            bc(cf[:, i, :], 2, HD), ALU.mult))
                    if i >= 1:
                        dve.wait_ge(a_done, 4 * L + i)
                    tt(xn[:, t, 0:GW], xn[:, t, 0:GW], ot[:, :], ALU.add).then_inc(a_done, 1)
                for t in range(NT):
                    dve.wait_ge(y_rstd, 2 * L + t + 1)
                    y = xn[:, t, :].rearrange("p (m d) -> p m d", m=4)
                    tt(y, y, bc(rsy[:, t, :], 2, GW), ALU.mult).then_inc(yn_ready, 1)
                split_lo(3 * L + 1, 3 * L + 1)
                rest_unit(dve, wout[3])

                def add_mixed(b):
                    dve.wait_ge(used, WOUT[L] + 2 * b + 2)
                    for t in range(NT):
                        tt(x[:, t, b * FB:(b + 1) * FB], x[:, t, b * FB:(b + 1) * FB], bank[2 * b + t][:, :], ALU.add).then_inc(x_mid, 1)

                nxt, k = (DENSE, MOE)[L], 3 * L + 2
                add_mixed(0)
                rest_unit(dve, Unit(nxt))
                split_lo(k, k, range(0, 4))
                rest_unit(dve, Unit(nxt + 1))
                add_mixed(1)
                rest_unit(dve, Unit(nxt + 2))
                split_lo(k, k, range(4, 8))

            def times_h3(value, k, tiles, normed=True):
                dve.wait_ge(used, value)
                for t in range(tiles):
                    dve.wait_ge(silu_done, k * tiles + t + 1)
                    if normed:
                        tt(sg[:, t, :], sg[:, t, :], bank[2 + t][:, :], ALU.mult).then_inc(g_ready, 1)
                    else:
                        V.scalar_tensor_tensor(sg[:, t, :], bank[2 + t][:, :], rsx[:, t:t + 1], sg[:, t, :], ALU.mult,
                                               ALU.mult).then_inc(g_ready, 1)

            def split_g(k, tiles, at=0):
                for t in range(tiles):
                    dve.wait_ge(gTh_ready, k * tiles + t + 1)
                    tt(gTl[:, at + t], bank[4 + t][:, :].rearrange("p (c s) -> p c s", c=4), gTh[:, at + t].bitcast(F32),
                       ALU.subtract).then_inc(gTl_ready, 1)

            def add_y(value, half):
                dve.wait_ge(used, value)
                for t in range(NT):
                    xs = x[:, t, half * FB:(half + 1) * FB]
                    tt(xs, xs, bank[(6 if half == 0 else 4) + t][:, :], ALU.add).then_inc(y_added, 1)

            def dense_step(f, add):
                base, r = DENSE + 4, (f - 1) * 6
                rest_unit(dve, Unit(base, r))
                times_h3(base + r - (2 if add else 0), f - 1, NT, False)
                rest_unit(dve, Unit(base + 1, r))
                if add:
                    add_y(base + r - 1, 0)
                rest_unit(dve, Unit(base + 2, r))
                if add:
                    add_y(base + r, 1)
                rest_unit(dve, Unit(base + 3, r))
                split_g(f - 1, NT)
                rest_unit(dve, Unit(base + 4, r))
                rest_unit(dve, Unit(base + 5, r))

            def dense():
                rest_unit(dve, Unit(DENSE + 3))
                dense_step(1, False)
                with dve.Fori(2, NFB) as f:
                    dense_step(f, True)
                end = DENSE + FFN_UNITS
                rest_unit(dve, Unit(end - 2))
                times_h3(end - 4, NFB - 1, NT, False)
                rest_unit(dve, Unit(end - 1))
                add_y(end - 3, 0)
                add_y(end - 2, 1)
                split_g(NFB - 1, NT)
                add_y(end - 1, 0)
                rest_unit(dve, Unit(WIN[1]))
                split_lo(3, 3, range(0, 4))
                rest_unit(dve, Unit(WIN[1] + 1))
                add_y(end, 1)
                rest_unit(dve, Unit(WIN[1] + 2))
                split_lo(3, 3, range(4, 8))

            V.memset(hidp[:].rearrange("p j h n -> p (j h n)"), 0.0).then_inc(hp_ready, 1)
            V.memset(zero[:].bitcast(F32), 0.0).then_inc(zero_ready, 1)
            dve.wait_ge(hp_ready, 1)
            dve.wait_ge(s_const, 16)
            mixer(0)
            dense()
            mixer(1)
            dve.wait_ge(x_rstd, 4)
            dve.wait_ge(s_gbc, 16)
            for t in range(NT):
                V.scalar_tensor_tensor(xn[:, t, :], x[:, t, :], rsx[:, t:t + 1], gbc, ALU.mult, ALU.mult).then_inc(xn_ready, 1)
            dve.wait_ge(lg_psum, 1)
            settle(*[V.tensor_scalar(lg[:, t, :], bank[0][:, t * NE:(t + 1) * NE], rsx[:, t:t + 1], None, ALU.mult) for t in range(NT)])
            settle(*[V.max(top[:, t, :], lg[:, t, :]) for t in range(NT)])
            m1, m2 = bc(top[:, :, 0], 2, NE), bc(top[:, :, 1], 2, NE)
            tt(ra[:], lg[:], m1, ALU.subtract).then_inc(lg_ready, 1)
            settle(tt(sel[:], lg[:], m2, ALU.is_gt), tt(rb[:], lg[:], m2, ALU.is_equal))
            link(V.tensor_reduce(rsc1[:], sel[:], AX_X, ALU.add))
            link(tt(posm[:, :, 0], rsc1[:], rb[:, :, 0], ALU.add))
            for e in range(1, NE):
                link(tt(posm[:, :, e], posm[:, :, e - 1], rb[:, :, e], ALU.add))
            link(V.tensor_scalar(posm[:], posm[:], 2.0, None, ALU.is_le))
            link(tt(rb[:], rb[:], posm[:], ALU.mult))
            tt(sel[:], sel[:], rb[:], ALU.add).then_inc(sel_ready, 1)
            dve.wait_ge(sel_ready, 1)
            dve.wait_ge(lg_exp, 1)
            link(tt(ra[:], ra[:], sel[:], ALU.mult))
            link(V.tensor_reduce(rsc1[:], ra[:], AX_X, ALU.add))
            link(V.reciprocal(rsc1[:], rsc1[:]))
            link(tt(gate[:], ra[:], bc(rsc1[:], 2, NE), ALU.mult))
            dve.wait_ge(pos_psum, 1)
            link(V.scalar_tensor_tensor(posm[:], bank[1][:, 0:NT * NE].rearrange("p (t e) -> p t e", t=NT), 1.0, sel[:],
                                        ALU.add, ALU.mult))
            link(V.tensor_scalar(posm[:], posm[:], -1.0, None, ALU.add))
            link(V.tensor_reduce(cnt[:, 0:1], bank[1][:, NT * NE:(NT + 1) * NE], AX_X, ALU.max))
            V.tensor_scalar(flag[:], cnt[:, 0:1], float(SLOTS), None, ALU.is_gt).then_inc(route_ready, 1)

            def make_onehot(k, e, first_slot):
                for t in range(NT):
                    V.tensor_scalar(onehot[:, t, :], C("iota"), float(first_slot), posm[:, t, ds(e, 1)], ALU.add,
                                    ALU.is_equal).then_inc(oh_ready, 1)

            def split_gathered(k):
                for j in range(2):
                    dve.wait_ge(xgh_ready, 2 * k + j + 1)
                    tt(xgl[:, 4 * j:4 * j + 4, :], bank[1 + 2 * j][:, :].rearrange("p (c s) -> p c s", c=4),
                       xgh[:, 4 * j:4 * j + 4, :].bitcast(F32), ALU.subtract).then_inc(xgl_ready, 1)

            def blocks(base, rounds, k, e, first_slot, follows):
                kb = k * NFB + NT * NFB
                rest_unit(dve, Unit(base + 4, rounds))
                times_h3(base + rounds + 4, kb, 1)
                for n in (5, 6, 7):
                    rest_unit(dve, Unit(base + n, rounds))
                split_g(kb, 1)
                rest_unit(dve, Unit(base + 8, rounds))
                if follows:
                    dve.wait_ge(ohT_psum, k + 1)
                    make_onehot(k + 1, e + 1, first_slot)
                rest_unit(dve, Unit(base + 9, rounds))
                with dve.Fori(2, NFB) as f:
                    r = rounds + (f - 1) * 6
                    rest_unit(dve, Unit(base + 4, r))
                    times_h3(base + r + 2, kb + f - 1, 1)
                    for n in (5, 6, 7):
                        rest_unit(dve, Unit(base + n, r))
                    split_g(kb + f - 1, 1)
                    for n in (8, 9):
                        rest_unit(dve, Unit(base + n, r))
                rest_unit(dve, Unit(base + FFN_UNITS - 2, rounds))
                times_h3(base + rounds + FFN_UNITS - 4, kb + NFB - 1, 1)
                if follows:
                    split_gathered(k + 1)
                rest_unit(dve, Unit(base + FFN_UNITS - 1, rounds))
                split_g(kb + NFB - 1, 1, 1)
                if follows:
                    for n in range(3):
                        rest_unit(dve, Unit(base + FFN_UNITS + n, rounds))
                for j in range(2):
                    dve.wait_ge(ygh_ready, 2 * k + j + 1)
                    tt(ygl[:, 4 * j:4 * j + 4, :], bank[6 + j][:, :].rearrange("p (c n) -> p c n", c=4),
                       ygh[:, 4 * j:4 * j + 4, :].bitcast(F32), ALU.subtract).then_inc(ygl_ready, 1)
                if follows:
                    rest_unit(dve, Unit(base + FFN_UNITS + 3, rounds))
                for t in range(NT):
                    for j in range(2):
                        dve.wait_ge(sc_psum, 4 * k + 2 * t + j + 1)
                        xs = x[:, t, j * FB:(j + 1) * FB]
                        b = bank[[1, 3, 4, 5][2 * t + j]]
                        V.scalar_tensor_tensor(xs, b[:, :], gate[:, t, ds(e, 1)], xs, ALU.mult, ALU.add).then_inc(sc_done, 1)

            def experts(base, k0, first_slot):
                make_onehot(k0, 0, first_slot)
                split_gathered(k0)
                for n in range(0 if k0 else SPL, 4):
                    rest_unit(dve, Unit(base + n))
                with dve.Fori(0, NE - 1) as e:
                    blocks(base, e * FFN_UNITS, k0 + e, e, first_slot, True)
                blocks(base + (NE - 1) * FFN_UNITS, 0, k0 + NE - 1, NE - 1, first_slot, False)

            dve.wait_ge(route_ready, 1)
            experts(MOE, 0, 0)
            more = dve.value_load(flag[0:1, 0:1], min_val=0, max_val=1)
            with dve.If(more > 0):
                experts(MOE2, NE, SLOTS)
            V.tensor_copy(cnt[:, 1:2], rsx[:, 0:1]).then_inc(s_done, 1)

        @block.tensor
        def _(pe):
            T = nc.tensor

            def turn_y(k, value):
                for c in range(KC):
                    for t in range(NT):
                        if c == 0:
                            pe.wait_ge(yn_ready, value - NT + t + 1)
                        i = T.transpose(xT_bank(k, c)[:, t * P:(t + 1) * P], xn[:, t, c * P:(c + 1) * P], ident)
                    i.then_inc(xT_psum, 1)

            def turn_x(k, h):
                pe.wait_ge(*x_half(k, h))
                for c in range(4 * h, 4 * h + 4):
                    for t in range(NT):
                        i = T.transpose(xT_bank(k, c)[:, t * P:(t + 1) * P], x[:, t, c * P:(c + 1) * P], ident)
                    i.then_inc(xT_psum, 1)

            def product(L0, n_units, k, bank_of, width_of):
                for n in range(n_units):
                    u = Unit(L0 + n)
                    whole = width_of(n) != FB
                    w = width_of(n)
                    chunks = range(KC) if whole else range(4 * (n % 2), 4 * (n % 2) + 4)
                    pe.wait_ge(s_lo, u.n + 1)
                    wh = u.hi[:, 0:len(chunks) * w].rearrange("p (c n) -> p c n", n=w)
                    wl = u.lo[:, 0:len(chunks) * w].rearrange("p (c n) -> p c n", n=w)
                    for j, c in enumerate(chunks):
                        if n < 2 or whole:
                            pe.wait_ge(xTl_ready, 8 * k + c + 1)
                        for t in range(NT):
                            i = three_passes(bank_of(n, t)[:, 0:w], xTh[:, c, t * P:(t + 1) * P], xTl[:, c, t * P:(t + 1) * P],
                                             wh[:, j, :], wl[:, j, :], c == 0, c == KC - 1)
                    i.then_inc(used, 1)
                    yield n

            def mixer(L):
                if L == 0:
                    pe.wait_ge(s_const, 16)
                    pe.wait_ge(s_rows, 16 * 5)
                    T.transpose(bank[1][:, 0:N_ROWS], rows, ident[0:N_ROWS, 0:N_ROWS]).then_inc(rowsT_psum, 1)
                    for h in range(2):
                        turn_x(0, h)
                    pe.wait_ge(cols_ready, 1)
                for n in product(WIN[L], W_IN_UNITS, 3 * L, lambda n, t: bank[2 * ((n // 2) % 2) + t],
                                 lambda n: FB if n < W_IN_UNITS - 1 else D_IN - 4 * FB):
                    if n == 0 and L:
                        turn_x(3, 1)
                    if n % 2 and n >= 3:
                        pe.wait_ge(pr_ready, 10 * L + n - 1)
                    if n == 3:
                        pe.wait_ge(s_sgw, 16 * (L + 1))
                        for g in range(NH):
                            i = T.transpose(bank[4][:, g * P:(g + 1) * P], sgw[:, g, :], ident)
                        i.then_inc(sguT_psum, 1)
                pe.wait_ge(sguT_ready, L + 1)
                for t in range(NT):
                    pe.wait_ge(kd_ready, 2 * L + t + 1)
                    for j in range(2):
                        i = T.transpose(bank[4][:, j * S + t * P:j * S + (t + 1) * P], kd[:, t, j].rearrange("p a d -> p (a d)"), ident)
                i.then_inc(kdT_psum, 1)
                pe.wait_ge(pr_ready, 10 * (L + 1))
                if L == 0:
                    pe.wait_ge(s_tables, 16)
                band = C("band").rearrange("p (m g t) -> p m g t", m=3, g=4)
                for g in range(4):
                    o = bank[g // 2][0:HD, (g % 2) * S:(g % 2 + 1) * S]
                    w = [pr[:, t, PIN + g * HD:PIN + (g + 1) * HD] for t in range(NT)]
                    T.matmul(o[:, 0:P], w[0], band[:, 0, g, :], start=True, stop=True)
                    T.matmul(o[:, P:S], w[0], band[:, 1, g, :], start=True, stop=False)
                    i = T.matmul(o[:, P:S], w[1], band[:, 2, g, :], start=False, stop=True)
                    if g % 2:
                        i.then_inc(dlt_psum, 1)
                pe.wait_ge(z_ready, 3 * (L + 1))
                sh = C("shift").rearrange("p (k t) -> p k t", k=4)
                for t in range(NT):
                    o = bank[3][:, t * GW:(t + 1) * GW]
                    T.matmul(o, ident, zk[2][:, t, :], start=True, stop=False)
                    T.matmul(o, sh[:, 0, :], zk[1][:, t, :], start=False, stop=False)
                    i = T.matmul(o, sh[:, 1, :], zk[0][:, t, :], start=False, stop=(t == 0))
                    if t:
                        T.matmul(o, sh[:, 2, :], zk[1][:, 0, :], start=False, stop=False)
                        i = T.matmul(o, sh[:, 3, :], zk[0][:, 0, :], start=False, stop=True)
                i.then_inc(conv_psum, 1)
                pe.wait_ge(s_lay[L], LAY_LOADED)
                pe.wait_ge(kvb_ready, 8 * (L + 1))
                for j in range(2):
                    for a in range(16):
                        i = T.matmul(bank[5][:, j * CP:j * CP + NCMP], w1c[:, j, a, :], kvb[:, j, a, 0:NCMP],
                                     start=(a == 0), stop=(a == 15))
                i.then_inc(hid_psum, 1)
                pe.wait_ge(qk_ready, 2 * (L + 1))
                for h in range(6):
                    for t in range(NT):
                        i = T.transpose(bank[[6, 7, 4][h // 2]][0:HD, (h % 2) * S + t * P:(h % 2) * S + (t + 1) * P],
                                        qk[:, t, h, :], ident)
                    if h % 2:
                        i.then_inc(qkT_psum, 1)
                pe.wait_ge(hid_ready, 2 * (L + 1))
                T.matmul(bank[5][0:CP, 128:192], hidp[:, 0, 0, :], w2c[:, 0, :], start=True, stop=True)
                T.matmul(bank[5][:, 192:256], hidp[:, 1].rearrange("p h n -> p (h n)"), w2c[:, 1, :], start=True,
                         stop=True).then_inc(kcvc_psum, 1)

                def scores(i):
                    t, b0 = i % 2, 2 * (i % 2)
                    if i >= 2:
                        pe.wait_ge(a_max, 4 * L + i - 1)
                    for h in range(NH):
                        n = P * (t + 1)
                        b = bank[b0 + h * n // 512]
                        mm = T.matmul(b[:, h * n % 512:h * n % 512 + n], qT[:, h // 2, h % 2, t * P:(t + 1) * P],
                                      kT[:, i // 2, 0:n], start=True, stop=True)
                    mm.then_inc(a_s, 1)

                def turn_probs(i):
                    pe.wait_ge(a_exp, 4 * (4 * L + i + 1))
                    if i:
                        pe.wait_ge(a_Tr, 6 * L + [0, 1, 3, 4][i])
                    for kt in range(i % 2 + 1):
                        for h in range(NH):
                            mm = T.transpose(bank[4 + kt][:, h * P:(h + 1) * P], sc[:, i % 2, h, kt * P:(kt + 1) * P], ident)
                        mm.then_inc(a_T, 1)

                pe.wait_ge(qkT_ready, 3 * (L + 1))
                scores(0)
                pe.wait_ge(dlt_ready, 2 * (L + 1))
                for t in range(NT):
                    for g in range(4):
                        i = T.matmul(bank[2][:, t * GW + g * HD:t * GW + (g + 1) * HD], dlt[:, g // 2, g % 2, t * P:(t + 1) * P], pw[HD:P, g, :],
                                     start=True, stop=True)
                i.then_inc(poolY_psum, 1)
                pe.wait_ge(kc_ready, 2 * (L + 1))
                T.transpose(bank[5][0:HD, 256:256 + CP], kcs[:, 2, :], ident[0:CP, 0:CP]).then_inc(kcT_psum, 1)
                pe.wait_ge(kcT_ready, L + 1)
                for t in range(NT):
                    for h in range(NH):
                        i = T.matmul(bank[6][:, (t * NH + h) * CP:(t * NH + h + 1) * CP], qT[:, h // 2, h % 2, t * P:(t + 1) * P], kcT[:, :],
                                     start=True, stop=True)
                i.then_inc(cs_psum, 1)
                pe.wait_ge(vn_ready, 2 * (L + 1))
                for t in range(NT):
                    for g in range(NH):
                        i = T.matmul(bank[1][:, t * GW + g * HD:t * GW + (g + 1) * HD], sgT[:, g, :], vn[:, t, g * HD:(g + 1) * HD],
                                     start=True, stop=True)
                i.then_inc(sgu_psum, 1)
                pe.wait_ge(mix_done, 6 * L + 2)
                scores(1)
                pe.wait_ge(cs_ready, L + 1)
                for t in range(NT):
                    i = T.transpose(bank[7][:, t * P:(t + 1) * P], scc[:, t].rearrange("p h n -> p (h n)"), ident)
                i.then_inc(cT_psum, 1)
                turn_probs(0)
                pe.wait_ge(cT_ready, L + 1)
                pe.wait_ge(vbd_ready, L + 1)
                for t in range(NT):
                    i = T.matmul(bank[7][:, t * GW:(t + 1) * GW], pcT[:, t, :], vbd[:].rearrange("p h d -> p (h d)"),
                                 start=True, stop=True)
                i.then_inc(co_psum, 1)
                for i in range(4):
                    t, v0 = i % 2, (VS, VW)[i // 2]
                    if i:
                        turn_probs(i)
                    if i + 2 < 4:
                        scores(i + 2)
                    pe.wait_ge(a_Tr, 6 * L + [0, 1, 3, 4][i] + t + 1)
                    if i >= 2:
                        pe.wait_ge(a_done, 4 * L + i - 1)
                    elif i == 1:
                        pe.wait_ge(co_done, 2 * L + 2)
                    for h in range(NH):
                        for kt in range(t + 1):
                            mm = T.matmul(bank[6 + i % 2][:, h * HD:(h + 1) * HD], pT[:, kt, h, :],
                                          pr[:, kt, v0:v0 + HD], start=(kt == 0), stop=(kt == t))
                    mm.then_inc(a_o, 1)
                turn_y(3 * L + 1, 2 * L + 2)
                for n in product(WOUT[L], W_OUT_UNITS, 3 * L + 1, lambda n, t: bank[2 * (n // 2) + t], lambda n: FB):
                    if n == 2:
                        turn_x(3 * L + 2, 0)

            def up(base, rounds, w, tiles, xh, xl, halves=range(2)):
                for h in halves:
                    u = Unit(base + 2 * w + h, rounds)
                    pe.wait_ge(s_lo, u.n + 1)
                    wh = u.hi[:, :].rearrange("p (c n) -> p c n", c=4)
                    wl = u.lo[:, :].rearrange("p (c n) -> p c n", c=4)
                    for j in range(4):
                        c = 4 * h + j
                        for t in range(tiles):
                            i = three_passes(bank[2 * w + t][:, :], xh[:, c, t * P:(t + 1) * P], xl[:, c, t * P:(t + 1) * P],
                                             wh[:, j, :], wl[:, j, :], c == 0, c == KC - 1)
                    i.then_inc(used, 1)

            def turn(k, tiles):
                for t in range(tiles):
                    pe.wait_ge(g_ready, k * tiles + t + 1)
                    for c in range(4):
                        i = T.transpose(bank[4 + t][:, c * P:(c + 1) * P], sg[:, t, c * P:(c + 1) * P], ident)
                    i.then_inc(gT_psum, 1)

            def down(base, rounds, h, value, tiles, dense, last=True, at=0, midway=None):
                u = Unit(base + h, rounds)
                pe.wait_ge(s_lo, u.n + 1)
                if h == 0:
                    pe.wait_ge(gTl_ready, value)
                wh = u.hi[:, :].rearrange("p (c n) -> p c n", c=4)
                wl = u.lo[:, :].rearrange("p (c n) -> p c n", c=4)
                for j in range(4):
                    for t in range(tiles):
                        o = bank[(6 if h == 0 else 4) + t] if dense else bank[6 + h]
                        i = three_passes(o[:, :], gTh[:, at + t, j, :], gTl[:, at + t, j, :], wh[:, j, :], wl[:, j, :],
                                         dense and j == 0, last and j == 3)
                    if midway is not None and j == 1:
                        midway()
                i.then_inc(used, 1)

            mixer(0)
            pe.wait_ge(xTl_ready, 8 * 2 + 4)
            up(DENSE, 0, 0, NT, xTh, xTl, (0,))
            turn_x(2, 1)
            pe.wait_ge(xTl_ready, 8 * 3)
            up(DENSE, 0, 0, NT, xTh, xTl, (1,))
            up(DENSE, 0, 1, NT, xTh, xTl)

            def dense_step(f, r, peeled):
                pe.wait_ge(silu_done, NT * f)
                up(DENSE + 4, r, 0, NT, xTh, xTl)
                if not peeled:
                    pe.wait_ge(y_added, 4 * (f - 1))
                turn(f - 1, NT)
                up(DENSE + 4, r, 1, NT, xTh, xTl)
                for h in range(2):
                    down(DENSE + 8, r, h, f * NT, NT, True)

            dense_step(1, 0, True)
            with pe.Fori(2, NFB) as f:
                dense_step(f, (f - 1) * 6, False)
            pe.wait_ge(y_added, 4 * (NFB - 1))
            turn(NFB - 1, NT)
            down(DENSE + FFN_UNITS - 2, 0, 0, NFB * NT, NT, True)
            down(DENSE + FFN_UNITS - 2, 0, 1, NFB * NT, NT, True, midway=lambda: turn_x(3, 0))
            mixer(1)
            turn_x(5, 1)
            pe.wait_ge(s_rt, 16)
            pe.wait_ge(xTl_ready, 48)
            for t in range(NT):
                for c in range(KC):
                    for n, a in enumerate((xTh, xTl)):
                        i = T.matmul(bank[0][:, t * NE:(t + 1) * NE], a[:, c, t * P:(t + 1) * P].bitcast(F32), rt[:, c, :],
                                     start=(c == 0 and n == 0), stop=(c == KC - 1 and n == 1))
            i.then_inc(lg_psum, 1)
            pe.wait_ge(sel_ready, 1)
            T.matmul(bank[1][:, 0:NE], C("before"), sel[:, 0, :], start=True, stop=True)
            T.matmul(bank[1][:, NE:2 * NE], C("ones"), sel[:, 0, :], start=True, stop=False)
            T.matmul(bank[1][:, NE:2 * NE], C("before"), sel[:, 1, :], start=False, stop=True)
            T.matmul(bank[1][:, 2 * NE:3 * NE], C("ones"), sel[:, 0, :], start=True, stop=False)
            T.matmul(bank[1][:, 2 * NE:3 * NE], C("ones"), sel[:, 1, :], start=False, stop=True).then_inc(pos_psum, 1)
            pe.wait_ge(route_ready, 1)
            pe.wait_ge(zero_ready, 1)

            def gather(k):
                pe.wait_ge(oh_ready, 2 * (k + 1))
                for c in range(KC):
                    for t in range(NT):
                        i = T.matmul(bank[1 + 2 * (c // 4)][:, (c % 4) * P:(c % 4 + 1) * P], xn[:, t, c * P:(c + 1) * P],
                                     onehot[:, t, :], start=(t == 0), stop=(t == NT - 1))
                    if c % 4 == 3:
                        i.then_inc(xg_psum, 1)

            def scatter(k):
                for t in range(NT):
                    for j in range(2):
                        pe.wait_ge(ygl_ready, 2 * k + j + 1)
                        o = bank[[1, 3, 4, 5][2 * t + j]][:, :]
                        w = onehotT[:, t * P:(t + 1) * P]
                        T.matmul(o, w, ygh[:, 4 * j:4 * j + 4, :], start=True, stop=False)
                        T.matmul(o, w, ygl[:, 4 * j:4 * j + 4, :], start=False, stop=True).then_inc(sc_psum, 1)

            def turn_onehot(k):
                for t in range(NT):
                    i = T.transpose(bank[5][:, t * P:(t + 1) * P], onehot[:, t, :], ident)
                i.then_inc(ohT_psum, 1)

            def open_y():
                for h in range(2):
                    T.matmul(bank[6 + h][:, :], zero[:, :], bc(zero[:, :], 1, 4), start=True, stop=False)

            def blocks(base, rounds, k, follows):
                kb = k * NFB + NT * NFB
                with pe.Fori(1, NFB - 1) as f:
                    r = rounds + (f - 1) * 6
                    pe.wait_ge(silu_done, kb + f)
                    up(base + 4, r, 0, 1, xgh, xgl)
                    turn(kb + f - 1, 1)
                    up(base + 4, r, 1, 1, xgh, xgl)
                    for h in range(2):
                        down(base + 8, r, h, kb + f, 1, False, last=False)
                last = base + 4 + 6 * (NFB - 2)
                pe.wait_ge(silu_done, kb + NFB - 1)
                up(last, rounds, 0, 1, xgh, xgl)
                turn(kb + NFB - 2, 1)
                up(last, rounds, 1, 1, xgh, xgl)
                if follows:
                    gather(k + 1)
                down(last + 4, rounds, 0, kb + NFB - 1, 1, False, last=False)
                turn(kb + NFB - 1, 1)
                down(last + 4, rounds, 1, kb + NFB - 1, 1, False, last=False)
                for h in range(2):
                    down(last + 6, rounds, h, kb + NFB, 1, False, at=1)
                if follows:
                    pe.wait_ge(xgl_ready, 2 * (k + 2))
                    pe.wait_ge(silu_done, kb + NFB)
                    up(base + FFN_UNITS, rounds, 0, 1, xgh, xgl)
                pe.wait_ge(ohT_ready, k + 1)
                scatter(k)
                if follows:
                    open_y()
                    up(base + FFN_UNITS, rounds, 1, 1, xgh, xgl)
                    pe.wait_ge(sc_done, 4 * (k + 1))
                    turn_onehot(k + 1)

            def experts(base, k0):
                gather(k0)
                pe.wait_ge(xgl_ready, 2 * (k0 + 1))
                if k0:
                    pe.wait_ge(silu_done, k0 * NFB + NT * NFB)
                up(base, 0, 0, 1, xgh, xgl)
                open_y()
                up(base, 0, 1, 1, xgh, xgl)
                turn_onehot(k0)
                with pe.Fori(0, NE - 1) as e:
                    blocks(base, e * FFN_UNITS, k0 + e, True)
                blocks(base + (NE - 1) * FFN_UNITS, 0, k0 + NE - 1, False)

            experts(MOE, 0)
            more = pe.value_load(flag[0:1, 0:1], min_val=0, max_val=1)
            with pe.If(more > 0):
                experts(MOE2, NE)


_INS = ["x", "attn_norm_g", "w_in", "q_norm_g", "k_norm_g", "cmp_pe", "cmp_w1", "cmp_w2", "sgu_norm_g", "sgu_w",
        "sgu_b", "pool_w", "pool_scale", "conv_w", "mix_out_norm_g", "w_out", "ffn_norm_g", "ffn_w1", "ffn_w3",
        "ffn_w2", "router_w", "expert_w1", "expert_w3", "expert_w2"]


def kernel(**inputs):
    import concourse.bacc as bacc
    from concourse.bass_utils import run_bass_kernel_spmd

    nc = bacc.Bacc("TRN2", target_bir_lowering=False, num_devices=1)
    arrays, args = {}, []
    for name in _INS:
        a = np.ascontiguousarray(inputs[name])
        arrays[f"in_{name}"] = a
        args.append(nc.dram_tensor(f"in_{name}", a.shape, mybir.dt.from_np(a.dtype), kind="ExternalInput").ap())
    args[0] = args[0].rearrange("b s d -> (b s) d")
    arrays["in_consts"] = const_table()
    args.append(nc.dram_tensor("in_consts", arrays["in_consts"].shape, F32, kind="ExternalInput").ap())
    o = nc.dram_tensor("out_0", (1, S, D), F32, kind="ExternalOutput").ap()
    build(nc, *args, o.rearrange("b s d -> (b s) d"))
    r = run_bass_kernel_spmd(nc, [arrays], core_ids=[0])
    return r.results[0]["out_0"]
```

```python
from contextlib import ExitStack

import numpy as np

import concourse.bass as bass
from concourse import mybir

F32 = mybir.dt.float32
F32R = mybir.dt.float32r
I32 = mybir.dt.int32
ALU = mybir.AluOpType
ACT = mybir.ActivationFunctionType
AX_X = mybir.AxisListType.X
ds = bass.ds

P = 128
D = 1024
KC = D // P
S = 256
NT = S // P
HD = 64
NH = 4
GW = 256
DEPTH = 2
D_IN = 2188
FF = 3584
NE = 8
EPS = 1e-6
NEG = -1e30
NCMP = S // 16 - 1
CP = 32
THETA = 500000.0
POOLS = (2, 4, 8, 16)
Q0, KCM, KS, VS, KW, VW, GT, U0, V0, PIN, BG, CG, HIN = 0, 256, 384, 448, 512, 576, 640, 652, 908, 1164, 1420, 1676, 1932
FB = 512
NFB = FF // FB
UW = 2048
RAW = 6
SPL = 3
W_IN_UNITS = 9
W_OUT_UNITS = 4
FFN_UNITS = 6 * NFB
SLOTS = 128
PE_ROW = 3 * DEPTH * KC
SGB_ROW = PE_ROW + DEPTH * 2 * 16
N_ROWS = SGB_ROW + DEPTH * NH
Y_ORDER = (4, 5, 2, 3, 6, 7, 0, 1)
ROUTER = 5
OUT_HALF = (1, 0, 0, 1)
GELU_C = 0.7978845608028654


def const_layout():
    at, out = 0, {}
    for name, n in (("ident", P), ("triu", P), ("mhalf", 8),
                    ("band", 12 * P), ("shift", 4 * P), ("causal", P),
                    ("before", P), ("ones", P), ("iota", P), ("cos", NT * 8), ("sin", NT * 8),
                    ("ccos", 8), ("csin", 8), ("cmask", NT * CP), ("cvalid", NT * CP), ("blk", NH)):
        out[name] = (at, n)
        at += n
    return out, at


def const_table():
    lay, width = const_layout()
    c = np.zeros((P, width), np.float32)

    def put(name, a):
        at, n = lay[name]
        a = np.asarray(a, np.float32).reshape(a.shape[0], -1)
        c[:a.shape[0], at:at + n] = a

    r = np.arange(P)
    put("ident", np.eye(P))
    t = np.arange(S)
    bands = []
    for win in POOLS:
        b = ((t[:, None] <= t[None, :]) & (t[:, None] > t[None, :] - win)) / np.minimum(t + 1, win)[None, :].astype(np.float32)
        bands.append(b.astype(np.float32) - np.eye(S, dtype=np.float32))
    bands = np.stack(bands, 1)
    put("band", np.stack([bands[:P, :, :P], bands[:P, :, P:], bands[P:, :, P:]], 1))
    put("shift", np.stack([r[None, :] == r[:, None] + 1, r[None, :] == r[:, None] + 2,
                           r[None, :] + P == r[:, None] + 1, r[None, :] + P == r[:, None] + 2], 1))
    put("causal", np.where(r[None, :] <= r[:, None], 0.0, NEG))
    put("triu", r[:, None] <= r[None, :])
    put("before", r[:, None] < r[None, :])
    put("ones", np.ones((P, P)))
    put("iota", np.tile(r[None, :], (P, 1)))
    inv = (THETA ** (-np.arange(8, dtype=np.float32) / 8)).astype(np.float32)
    ang = (t.astype(np.float32)[:, None] * inv).reshape(NT, P, 8).transpose(1, 0, 2)
    put("cos", np.cos(ang))
    put("sin", np.sin(ang))
    end = (np.arange(CP) * 16 + 31).astype(np.float32)
    put("ccos", np.cos(end[:, None] * inv))
    put("csin", np.sin(end[:, None] * inv))
    ok = (end[None, :] <= t[:, None]) & (np.arange(CP) < NCMP)[None, :]
    ok = ok.reshape(NT, P, CP).transpose(1, 0, 2)
    put("cmask", np.where(ok, 0.0, NEG))
    put("cvalid", ok)
    put("blk", r[:, None] // CP == np.arange(NH)[None, :])
    put("mhalf", np.full((P, 8), -0.5))
    return c


def spread(ap, axis, n):
    shape = list(ap.shape)
    shape[axis] = n
    return ap.broadcast_to(shape)


def bc(ap, axis, n):
    return spread(ap.unsqueeze(axis), axis, n)


def build(nc, x_in, attn_norm_g, w_in, q_norm_g, k_norm_g, cmp_pe, cmp_w1, cmp_w2, sgu_norm_g, sgu_w, sgu_b,
          pool_w, pool_scale, conv_w, mix_out_norm_g, w_out, ffn_norm_g, ffn_w1, ffn_w3, ffn_w2,
          router_w, expert_w1, expert_w3, expert_w2, consts, out):
    lay, cwidth = const_layout()
    ctx = ExitStack()
    with ctx:
        def sb(name, shape, dt=F32):
            return ctx.enter_context(nc.sbuf_tensor(name, shape, dt))

        def sem(name):
            return ctx.enter_context(nc.semaphore(name))

        raw = [sb(f"raw{i}", [P, UW]) for i in range(RAW)]
        whi = [sb(f"whi{i}", [P, UW], F32R) for i in range(SPL)]
        wlo = [sb(f"wlo{i}", [P, UW], F32R) for i in range(SPL)]
        ct = sb("ct", [P, cwidth])
        x = sb("x", [P, NT, D])
        xn = sb("xn", [P, NT, D])
        xTh = sb("xTh", [P, KC, S], F32R)
        xTl = sb("xTl", [P, KC, S], F32R)
        pr = sb("pr", [P, NT, D_IN])
        rows = pr[0:N_ROWS, 1, 0:P]
        cols = sb("cols", [P, N_ROWS])
        g6 = sb("g6", [P, 6, HD])
        gkc = sb("gkc", [P, HD])
        gsgu = sb("gsgu", [P, GW])
        psc = sb("psc", [P, GW])
        cw = sb("cw", [P, 3, GW])
        sgT = sb("sgT", [P, NH, P])
        pw = sb("pw", [P, NH, HD])
        big = sb("big", [P, 4096])
        w1c = big[:, :].rearrange("p (k a n) -> p k a n", k=2, a=16)
        w2c = sb("w2c", [P, 2, HD])
        rt = sb("rt", [P, KC, NE])
        ssx = sb("ssx", [P, NT, 2])
        rsx = sb("rsx", [P, NT])
        ss = sb("ss", [P, NT, 8])
        rs = sb("rs", [P, NT, 8])
        ssc = sb("ssc", [CP, 1])
        rsc = sb("rsc", [CP, 1])
        ssy = sb("ssy", [P, NT, NH])
        rsy = sb("rsy", [P, NT, NH])
        kd = xn[:, :, 2 * GW:3 * GW].rearrange("p t (j a d) -> p t j a d", j=2, a=2)
        zk = [xn[:, :, 0:GW], xn[:, :, GW:2 * GW], xn[:, :, 3 * GW:4 * GW]]
        tmp = sb("tmp", [P, NT, 6, HD])
        qk = sb("qk", [P, NT, 6, HD])
        rp = [xn[:, :, 2 * GW + 48 * i:2 * GW + 48 * (i + 1)].rearrange("p t (h f) -> p t h f", h=6) for i in range(4)]
        qT = pr[0:HD, :, CG:CG + 2 * GW].rearrange("p t (i s) -> p t i s", i=2)
        dlt = pr[HD:P, :, CG:CG + 2 * GW].rearrange("p t (i s) -> p t i s", i=2)
        sgw = qk[:].rearrange("p t h d -> p (t h d)")[:, 0:NH * P].rearrange("p (g s) -> p g s", g=NH)
        kT = sb("kT", [HD, 2, S])
        vn = tmp[:].rearrange("p t h d -> p t (h d)")[:, :, 0:GW]
        kvb = sb("kvb", [P, 2, 16, 16])
        hx = big[:, 3840:3840 + 2 * NCMP].rearrange("p (j n) -> p j n", j=2)
        hy = big[:, 3872:3872 + 2 * NCMP].rearrange("p (j n) -> p j n", j=2)
        hz = big[:, 3904:3904 + 2 * NCMP].rearrange("p (j n) -> p j n", j=2)
        hraw = big[0:NCMP, 3584:3840]
        hidp = sb("hidp", [P, 2, NH, CP])
        kcs = sb("kcs", [CP, 3, HD])
        krp = sb("krp", [CP, 4, 8])
        kcT = sb("kcT", [HD, CP])
        vbd = sb("vbd", [P, NH, HD])
        gates = sb("gates", [P, NT, NH, 3])
        sc = big[:, 0:2048].rearrange("p (i h s) -> p i h s", i=2, h=NH)
        scc = big[:, 3072:3328].rearrange("p (t h n) -> p t h n", t=NT, h=NH)
        mx = sb("mx", [P, 4, NH])
        sm = sb("sm", [P, 4, NH])
        cf = sb("cf", [P, 4, NH])
        mxc = sb("mxc", [P, NT, NH])
        smc = sb("smc", [P, NT, NH])
        pT = big[:, 2048:3072].rearrange("p (k h q) -> p k h q", k=2, h=NH)
        pcT = big[:, 3328:3584].rearrange("p (t q) -> p t q", t=NT)
        ot = big[:, 3584:3840]
        junk_v = xn[:, 0, 0:GW]
        junk = qk[:, 0].rearrange("p h d -> p (h d)")[:, 0:GW]
        gTh_last, gTl_last = xTh[:, KC // 2:KC, :], xTl[:, KC // 2:KC, :]
        sg = pr[:, 1, 1024:2048].rearrange("p (t n) -> p t n", t=NT)
        gTh = sb("gTh", [P, NT, 4, P], F32R)
        gTl = sb("gTl", [P, NT, 4, P], F32R)
        gbc = pr[:, 0, 0:D]
        lg = sb("lg", [P, NT, NE])
        top = sb("top", [P, NT, 8])
        sel = sb("sel", [P, NT, NE])
        ra = sb("ra", [P, NT, NE])
        rb = sb("rb", [P, NT, NE])
        rsc1 = sb("rsc1", [P, NT])
        gate = sb("gate", [P, NT, NE])
        posm = sb("posm", [P, NT, NE])
        cnt = sb("cnt", [P, 2])
        flag = sb("flag", [P, 1], I32)
        ygh = xTh[:, :, SLOTS:2 * SLOTS]
        ygl = xTl[:, :, SLOTS:2 * SLOTS]
        onehot = pr[:, 1, 0:NT * SLOTS].rearrange("p (t s) -> p t s", t=NT)
        onehotT = sb("onehotT", [P, S], F32R)
        xTf = big[:, 0:KC * S].rearrange("p (c s) -> p c s", c=KC)
        lgT = big[0:NE, KC * S:KC * S + S]
        xgh = xTh[:, :, 0:SLOTS]
        xgl = xTl[:, :, 0:SLOTS]
        zero = sb("zero", [P, P], F32R)

        bank = [ctx.enter_context(nc.psum_tensor(f"bank{i}", [P, 512], F32)) for i in range(8)]

        def C(name, rows=P):
            at, n = lay[name]
            return ct[0:rows, at:at + n]

        ident = C("ident")

        def gain_col(gain, c):
            i = (gain % 3) * DEPTH * KC + gain // 3 * KC + c
            return cols[:, i:i + 1]

        s_const, s_tables, s_x, s_rows = sem("const_in"), sem("tables_in"), sem("x_in"), sem("rows_in")
        s_sgw, s_lay = sem("sgu_w_in"), [sem("layer_in0"), sem("layer_in1")]
        s_gbc, s_rt = sem("ffn_gain_in"), sem("router_in")
        landed = [sem(f"landed{i}") for i in range(RAW)]
        s_hi, s_lo, used = sem("unit_hi"), sem("unit_lo"), sem("unit_used")
        x_sq, x_rstd, xn_ready = sem("x_sq"), sem("x_rstd"), sem("xn_ready")
        xT_psum, xTh_ready, xTl_ready = sem("xT_psum"), sem("xTh_ready"), sem("xTl_ready")
        pr_ready = sem("proj_ready")
        rowsT_psum, cols_ready = sem("rowsT_psum"), sem("cols_ready")
        sguT_psum, sguT_ready = sem("sguT_psum"), sem("sguT_ready")
        kd_ready, kdT_psum, kvb_ready = sem("kd_ready"), sem("kdT_psum"), sem("kvb_ready")
        hraw_ready, hidT_psum = sem("hid_copied"), sem("hidT_psum")
        hid_psum, gelu_in, gelu_e, hid_ready = sem("hid_psum"), sem("gelu_in"), sem("gelu_exp"), sem("hid_ready")
        kcvc_psum, kc_ss, kc_rstd, kc_ready = sem("kcvc_psum"), sem("kc_ss"), sem("kc_rstd"), sem("kc_ready")
        kcT_psum, kcT_ready, vbd_ready = sem("kcT_psum"), sem("kcT_ready"), sem("vbd_ready")
        z_ready, qk_ss, v_ss, qk_rstd = sem("z_ready"), sem("qk_ss"), sem("v_ss"), sem("qk_rstd")
        qk_ready, vn_ready = sem("qk_ready"), sem("vn_ready")
        qkT_psum, qkT_ready = sem("qkT_psum"), sem("qkT_ready")
        dlt_psum, dlt_ready, poolY_psum = sem("dlt_psum"), sem("dlt_ready"), sem("poolY_psum")
        conv_psum, sgu_psum, mix_done = sem("conv_psum"), sem("sgu_psum"), sem("mix_evacuated")
        gate_e = sem("gate_exp")
        cs_psum, cs_in, cs_exp, cs_ready = sem("cmp_scores"), sem("cmp_masked"), sem("cmp_exp"), sem("cmp_probs")
        cT_psum, cT_ready, co_psum, co_done = sem("cmpT_psum"), sem("cmpT_ready"), sem("cmp_out"), sem("cmp_out_used")
        a_s, a_max, a_exp = sem("scores"), sem("score_max"), sem("probs")
        a_T, a_Tr, a_o, a_done = sem("probsT"), sem("probsT_copied"), sem("attn_out"), sem("attn_out_used")
        y_sq, y_rstd, yn_ready = sem("y_sq"), sem("y_rstd"), sem("yn_ready")
        x_mid = sem("x_plus_mixer")
        silu_done, g_ready, gT_psum, gTh_ready, gTl_ready = (sem("silu_done"), sem("g_ready"), sem("gT_psum"),
                                                             sem("gTh_ready"), sem("gTl_ready"))
        y_added = sem("dense_y_added")
        xTf_act, xTf_dve = sem("xTf_by_scalar"), sem("xTf_by_vector")
        lgT_psum, lgT_ready = sem("logitsT_psum"), sem("logitsT")
        lg_psum, lg_ready, lg_exp = sem("logits_psum"), sem("top2_in"), sem("top2_exp")
        sel_ready, pos_psum, route_ready = sem("sel_ready"), sem("pos_psum"), sem("route_ready")
        zero_ready, hp_ready = sem("zero_ready"), sem("hidp_zeroed")
        oh_ready, xg_psum, xgh_ready, xgl_ready = sem("onehot"), sem("gathered"), sem("xgh_ready"), sem("xgl_ready")
        ohT_psum, ohT_ready, ygh_ready, ygl_ready, sc_psum, sc_done = (sem("onehotT_psum"), sem("onehotT"), sem("ygh_ready"), sem("ygl_ready"),
                                                           sem("scattered"), sem("scatter_added"))
        dve_order, pool_order = sem("dve_order"), sem("pool_order")
        s_done, s_out = sem("x_final"), sem("out_stored")

        WIN = [0, W_IN_UNITS + W_OUT_UNITS + FFN_UNITS]
        WOUT = [n + W_IN_UNITS for n in WIN]
        DENSE = WOUT[0] + W_OUT_UNITS
        MOE = WOUT[1] + W_OUT_UNITS
        MOE2 = MOE + NE * FFN_UNITS
        HEAD = lay["band"][0]
        LAY_LOADED = 16 * 11

        class Unit:

            def __init__(self, base, rounds=0, slots_ahead=0):
                self.base, self.rounds, self.ahead = base, rounds, slots_ahead
                self.raw = raw[base % RAW]
                self.landed = landed[base % RAW]
                self.hi, self.lo = whi[base % SPL], wlo[base % SPL]
                self.n = base + rounds
                self.turn = base // RAW + slots_ahead

        def load_unit(sp, u, src, words):
            if u.base >= RAW:
                sp.wait_ge(s_lo, u.n - RAW + 1)
            sp.dma_start(words(u.raw), src).then_inc(u.landed, 16)

        def round_unit(act, u, n=UW):
            act.wait_ge(u.landed, 16 * (u.turn + 1))
            if u.base >= SPL:
                act.wait_ge(used, u.n - SPL + 1)
            nc.scalar.activation(u.hi[:, 0:n], u.raw[:, 0:n], ACT.Copy).then_inc(s_hi, 1)

        def rest_unit(dve, u, n=UW):
            dve.wait_ge(s_hi, u.n + 1)
            nc.vector.tensor_tensor(u.lo[:, 0:n], u.raw[:, 0:n], u.hi[:, 0:n].bitcast(F32), ALU.subtract).then_inc(s_lo, 1)

        def in_words(n):
            return (4 * FB) if n < W_IN_UNITS - 1 else KC * (D_IN - 4 * FB)

        def is_y(k):
            return k % 3 == 1

        def xT_bank(k, c):
            return bank[(3, 0, 1, 2)[c // 2] if is_y(k) else 2 + c // 2][:, (c % 2) * S:(c % 2 + 1) * S]

        def turned(k, c):
            return 8 * k + (Y_ORDER.index(c) if is_y(k) else c) + 1

        def bank_turned(k, c):
            return turned(k, c // 2 * 2 + 1)

        def x_half(k, h):
            if k == 0:
                return s_x, 16
            if k == 3:
                return y_added, 4 * NFB - 2 + 2 * h
            return x_mid, 4 * (k // 3) + 2 * (h + 1)

        def three_passes(o, xh, xl, wh, wl, start, stop):
            nc.tensor.matmul(o, xh, wh, start=start, stop=False)
            nc.tensor.matmul(o, xh, wl, start=False, stop=False)
            return nc.tensor.matmul(o, xl, wh, start=False, stop=stop)

        block = ctx.enter_context(nc.Block())

        @block.sync
        def _(sp):
            sp.dma_start(x[:], x_in.rearrange("(t p) d -> p t d", p=P)).then_inc(s_x, 16)
            sp.dma_start(ct[:, 0:HEAD], consts[:, 0:HEAD]).then_inc(s_const, 16)
            for j, g in enumerate((attn_norm_g, mix_out_norm_g, ffn_norm_g)):
                sp.dma_start(rows[j * DEPTH * KC:(j + 1) * DEPTH * KC, :], g.rearrange("l (c p) -> (l c) p", p=P)).then_inc(s_rows, 16)
            sp.dma_start(rows[PE_ROW:SGB_ROW, :], cmp_pe.rearrange("l k (a two) d -> (l k a) (two d)", two=2)).then_inc(s_rows, 16)
            sp.dma_start(rows[SGB_ROW:N_ROWS, :], sgu_b.rearrange("l g t -> (l g) t")).then_inc(s_rows, 16)

            def mixer_weights(L):
                for n in range(W_IN_UNITS):
                    if L == 0 and n == RAW:
                        sp.dma_start(ct[:, HEAD:], consts[:, HEAD:]).then_inc(s_tables, 16)
                    src = w_in[L].rearrange("(c p) n -> p c n", p=P)
                    if n < W_IN_UNITS - 1:
                        b, h = n // 2, n % 2
                        src = src[:, 4 * h:4 * h + 4, b * FB:(b + 1) * FB]
                        load_unit(sp, Unit(WIN[L] + n), src, lambda r: r[:, :].rearrange("p (c n) -> p c n", c=4))
                    else:
                        src = src[:, :, 4 * FB:D_IN]
                        load_unit(sp, Unit(WIN[L] + n), src,
                                  lambda r: r[:, 0:in_words(8)].rearrange("p (c n) -> p c n", c=KC))
                for n in range(W_OUT_UNITS):
                    b, h = n // 2, OUT_HALF[n]
                    src = w_out[L].rearrange("(c p) n -> p c n", p=P)[:, 4 * h:4 * h + 4, b * FB:(b + 1) * FB]
                    load_unit(sp, Unit(WOUT[L] + n), src, lambda r: r[:, :].rearrange("p (c n) -> p c n", c=4))

            def in_block(u0, rounds, turns, w1, w3, f):
                j = 0
                for w in (w1, w3):
                    for h in range(2):
                        src = w.rearrange("(c p) n -> p c n", p=P)[:, 4 * h:4 * h + 4, ds(f * FB, FB)]
                        load_unit(sp, Unit(u0 + j, rounds, turns), src,
                                  lambda r: r[:, :].rearrange("p (c n) -> p c n", c=4))
                        j += 1

            def out_block(u0, rounds, turns, w2, f):
                for h in range(2):
                    src = w2[ds(f * FB, FB), h * FB:(h + 1) * FB].rearrange("(c p) n -> p c n", p=P)
                    load_unit(sp, Unit(u0 + h, rounds, turns), src,
                              lambda r: r[:, :].rearrange("p (c n) -> p c n", c=4))

            def ffn_weights(base, rounds, turns, w1, w3, w2):
                in_block(base, rounds, turns, w1, w3, 0)
                with sp.Fori(1, NFB) as f:
                    in_block(base + 4, rounds + (f - 1) * 6, turns + (f - 1), w1, w3, f)
                    out_block(base + 8, rounds + (f - 1) * 6, turns + (f - 1), w2, f - 1)
                out_block(base + FFN_UNITS - 2, rounds, turns, w2, NFB - 1)

            def expert(w, e):
                return w[0, ds(e, 1)].rearrange("a k n -> (a k) n")

            mixer_weights(0)
            ffn_weights(DENSE, 0, 0, ffn_w1[0], ffn_w3[0], ffn_w2[0])
            mixer_weights(1)

            def experts(base):
                with sp.Fori(0, NE) as e:
                    ffn_weights(base, e * FFN_UNITS, e * (FFN_UNITS // RAW),
                                expert(expert_w1, e), expert(expert_w3, e), expert(expert_w2, e))

            experts(MOE)
            sp.wait_ge(route_ready, 1)
            more = sp.value_load(flag[0:1, 0:1], min_val=0, max_val=1)
            with sp.If(more > 0):
                experts(MOE2)
            sp.wait_ge(s_done, 1)
            sp.dma_start(out.rearrange("(t p) d -> p t d", p=P), x[:]).then_inc(s_out, 16)
            sp.wait_ge(s_out, 16)

        @block.gpsimd
        def _(pool):
            count = [0]

            def small(dst, src, s):
                pool.dma_start(dst, src, allow_slow_non_contiguous=True).then_inc(s, 16)

            def layer_weights(L):
                small(sgw[:], sgu_w[L].rearrange("g t s -> t g s"), s_sgw)
                for k in range(2):
                    small(w1c[:, k], cmp_w1[L, k].rearrange("(a p) n -> p a n", p=P), s_lay[L])
                    small(w2c[:, k], cmp_w2[L, k], s_lay[L])
                small(cw[:], spread(conv_w[L:L + 1], 0, P), s_lay[L])
                small(g6[:, 0:NH, :], spread(bc(q_norm_g[L:L + 1], 1, NH), 0, P), s_lay[L])
                small(g6[:, NH:NH + 2, :], spread(k_norm_g[L:L + 1, 1:3], 0, P), s_lay[L])
                small(gkc[:], spread(k_norm_g[L, 0:1], 0, P), s_lay[L])
                small(gsgu[:], spread(sgu_norm_g[L:L + 1], 0, P), s_lay[L])
                small(psc[:], spread(pool_scale[L:L + 1], 0, P), s_lay[L])
                small(pw[HD:P], pool_w[L].rearrange("g c d -> c g d"), s_lay[L])

            def rsqrt(outp, inp, n, wait, value, done):
                pool.wait_ge(wait, value)
                nc.gpsimd.tensor_scalar(inp, inp, 1.0 / n, EPS, ALU.mult, ALU.add).then_inc(pool_order, 1)
                count[0] += 1
                pool.wait_ge(pool_order, count[0])
                w = inp.shape[-1]
                nc.gpsimd.tensor_tensor(outp, inp, C("mhalf", inp.shape[0])[:, 0:w], ALU.pow).then_inc(done, 1)

            def x_statistics(n):
                pool.wait_ge(x_sq, 4 * (n + 1))
                nc.gpsimd.tensor_tensor(ssx[:, :, 0], ssx[:, :, 0], ssx[:, :, 1], ALU.add).then_inc(pool_order, 1)
                count[0] += 1
                rsqrt(rsx[:], ssx[:, :, 0], D, pool_order, count[0], x_rstd)

            pool.wait_ge(s_const, 16)
            for L in range(DEPTH):
                x_statistics(2 * L)
                if L == 0:
                    layer_weights(0)
                    small(rt[:], router_w[0].rearrange("(c p) e -> p c e", p=P), s_rt)
                pool.wait_ge(v_ss, 2 * (L + 1))
                pool.wait_ge(qk_ss, L + 1)
                nc.gpsimd.tensor_scalar(ss[:, :, 0:6], ss[:, :, 0:6], 1.0 / HD, EPS, ALU.mult, ALU.add).then_inc(pool_order, 1)
                nc.gpsimd.tensor_scalar(ss[:, :, 6:7], ss[:, :, 6:7], 1.0 / GW, EPS, ALU.mult, ALU.add).then_inc(pool_order, 1)
                count[0] += 2
                pool.wait_ge(pool_order, count[0])
                for t in range(NT):
                    nc.gpsimd.tensor_tensor(rs[:, t, 0:7], ss[:, t, 0:7], C("mhalf")[:, 0:7], ALU.pow).then_inc(qk_rstd, 1)
                rsqrt(rsc[:], ssc[:], HD, kc_ss, L + 1, kc_rstd)
                for t in range(NT):
                    rsqrt(rsy[:, t, 1:4], ssy[:, t, 1:4], GW, y_sq, 8 * L + 6, y_rstd)
                for t in range(NT):
                    rsqrt(rsy[:, t, 0:1], ssy[:, t, 0:1], GW, y_sq, 8 * L + 7 + t, y_rstd)
                if L == 0:
                    pool.wait_ge(yn_ready, 4)
                    layer_weights(1)
                x_statistics(2 * L + 1)
            pool.wait_ge(y_sq, 16)
            small(gbc, spread(ffn_norm_g[1:2], 0, P), s_gbc)

        @block.scalar
        def _(act):
            def square_x(n, k, h):
                act.wait_ge(*x_half(k, h))
                if n:
                    act.wait_ge(x_rstd, n)
                for t in range(NT):
                    nc.scalar.activation(xn[:, t, h * FB:(h + 1) * FB], x[:, t, h * FB:(h + 1) * FB], ACT.Square,
                                         accum_out=ssx[:, t, h:h + 1]).then_inc(x_sq, 1)

            def split_hi(k, gain, chunks=range(KC)):
                for c in chunks:
                    act.wait_ge(xT_psum, bank_turned(k, c))
                    nc.scalar.activation(xTh[:, c, :], xT_bank(k, c), ACT.Copy, scale=gain_col(gain, c)).then_inc(xTh_ready, 1)

            def take(k, chunks):
                if k != ROUTER:
                    split_hi(k, k, chunks)
                    return
                act.wait_ge(xT_psum, bank_turned(k, chunks[0]))
                for c in chunks[0:2]:
                    nc.scalar.activation(xTf[:, c, :], xT_bank(k, c), ACT.Copy, scale=gain_col(k, c)).then_inc(xTf_act, 1)

            def next_operand(n, k, base, ahead):
                for i in range(ahead):
                    round_unit(act, Unit(base + i))
                square_x(n, k, 0)
                take(k, range(0, 4))
                for i in range(ahead, SPL):
                    if k == ROUTER and i == SPL - 1:
                        square_x(n, k, 1)
                        take(k, range(4, 8))
                    round_unit(act, Unit(base + i))
                if k != ROUTER:
                    take(k, range(4, 8))
                    square_x(n, k, 1)

            def mixer(L):
                units = [Unit(WIN[L] + n) for n in range(W_IN_UNITS)]
                if L == 0:
                    act.wait_ge(cols_ready, 1)
                    for h in range(2):
                        split_hi(0, 0, range(4 * h, 4 * h + 4))
                        round_unit(act, units[h])
                    for h in range(2):
                        square_x(0, 0, h)
                    round_unit(act, units[2])
                act.wait_ge(x_rstd, 2 * L + 1)
                for c in range(5):
                    for n in (2 * c + 3, 2 * c + 4):
                        if n < W_IN_UNITS:
                            round_unit(act, units[n], in_words(n))
                    act.wait_ge(used, WIN[L] + min(2 * c + 2, W_IN_UNITS))
                    n = min(FB, D_IN - c * FB)
                    for t in range(NT):
                        nc.scalar.activation(pr[:, t, c * FB:c * FB + n], bank[2 * (c % 2) + t][:, 0:n], ACT.Copy,
                                             scale=rsx[:, t:t + 1]).then_inc(pr_ready, 1)
                    if c == 2:
                        act.wait_ge(pr_ready, 10 * L + 6)
                        nc.scalar.activation(gates[:].rearrange("p t h b -> p t (h b)"), pr[:, :, GT:GT + 12], ACT.Exp,
                                             scale=-1.0).then_inc(gate_e, 1)
                        for t in range(NT):
                            nc.scalar.activation(junk_v, pr[:, t, V0:V0 + GW], ACT.Square,
                                                 accum_out=ss[:, t, 6:7]).then_inc(v_ss, 1)
                            act.wait_ge(v_ss, 2 * L + t + 1)
                wout = [Unit(WOUT[L] + n) for n in range(W_OUT_UNITS)]
                for n in range(SPL):
                    round_unit(act, wout[n])
                act.wait_ge(gelu_in, L + 1)
                nc.scalar.activation(hz[:], hy[:], ACT.Exp, scale=-2.0 * GELU_C).then_inc(gelu_e, 1)
                act.wait_ge(z_ready, 3 * L + 1)
                for j in range(3):
                    act.wait_ge(qkT_psum, 3 * L + j + 1)
                    nc.scalar.copy(qT[:, j] if j < 2 else kT[:],
                                   bank[[6, 7, 5][j]][0:HD, :].rearrange("p (h s) -> p h s", h=2)).then_inc(qkT_ready, 1)
                for j in range(2):
                    act.wait_ge(dlt_psum, 2 * L + j + 1)
                    nc.scalar.copy(dlt[:, j], bank[j][0:HD, :].rearrange("p (g s) -> p g s", g=2)).then_inc(dlt_ready, 1)
                def probs(i):
                    act.wait_ge(a_max, 4 * L + i + 1)
                    for h in range(NH):
                        n = P * (i % 2 + 1)
                        nc.scalar.activation(sc[:, i % 2, h, 0:n], sc[:, i % 2, h, 0:n], ACT.Exp,
                                             bias=mx[:, i, h:h + 1], accum_out=sm[:, i, h:h + 1]).then_inc(a_exp, 1)

                act.wait_ge(cs_in, L + 1)
                nc.scalar.activation(scc[:], scc[:], ACT.Exp).then_inc(cs_exp, 1)
                probs(0)
                act.wait_ge(mix_done, 6 * (L + 1))

                def square_y(t, m):
                    nc.scalar.activation(junk[:, :], xn[:, t, m * GW:(m + 1) * GW], ACT.Square,
                                         accum_out=ssy[:, t, m:m + 1]).then_inc(y_sq, 1)

                for n in range(6):
                    square_y(n // 3, n % 3 + 1)
                    act.wait_ge(y_sq, 8 * L + n + 1)
                act.wait_ge(cT_psum, L + 1)
                nc.scalar.copy(pcT[:].rearrange("p t q -> p (t q)"), bank[7][:, 0:NT * P]).then_inc(cT_ready, 1)
                def copy_probs(i):
                    k = 4 * L + i
                    for kt in range(i % 2 + 1):
                        act.wait_ge(a_T, 6 * L + [0, 1, 3, 4][i] + kt + 1)
                        if k:
                            act.wait_ge(a_o, k)
                        nc.scalar.copy(pT[:, kt], bank[4 + kt][:, :].rearrange("p (h q) -> p h q", h=NH)).then_inc(a_Tr, 1)

                k = 3 * L + 1
                copy_probs(0)
                for i in (1, 2):
                    probs(i)
                    copy_probs(i)
                probs(3)
                copy_probs(3)
                split_hi(k, k, Y_ORDER[0:6])
                for t in range(NT):
                    act.wait_ge(a_done, 4 * L + 3 + t)
                    square_y(t, 0)
                    act.wait_ge(y_sq, 8 * L + 7 + t)
                split_hi(k, k, Y_ORDER[6:8])
                round_unit(act, wout[3])

            def silu(value, k, tiles, normed=True):
                act.wait_ge(used, value)
                act.wait_ge(gT_psum, k * tiles)
                for t in range(tiles):
                    nc.scalar.activation(sg[:, t, :], bank[t][:, :], ACT.Silu,
                                         scale=1.0 if normed else rsx[:, t:t + 1]).then_inc(silu_done, 1)

            def split_g(k, tiles, at=0, last_dense=False):
                for t in range(tiles):
                    act.wait_ge(gT_psum, k * tiles + t + 1)
                    o, b = (gTh_last[:, :, t * P:(t + 1) * P], bank[t]) if last_dense else (gTh[:, at + t], bank[4 + t])
                    nc.scalar.copy(o, b[:, :].rearrange("p (c s) -> p c s", c=4)).then_inc(gTh_ready, 1)

            def step(base, rounds, turns, k, tiles, at=0, normed=True):
                for n in range(5):
                    round_unit(act, Unit(base + n, rounds, turns))
                silu(base + rounds + 2, k, tiles, normed)
                split_g(k - 1, tiles, at)
                round_unit(act, Unit(base + 5, rounds, turns))

            def dense():
                round_unit(act, Unit(DENSE + 3))
                act.wait_ge(x_rstd, 2)
                silu(DENSE + 2, 0, NT, False)
                with act.Fori(1, NFB) as f:
                    step(DENSE + 4, (f - 1) * 6, f - 1, f, NT, normed=False)
                round_unit(act, Unit(DENSE + FFN_UNITS - 2))
                split_g(NFB - 1, NT, last_dense=True)
                round_unit(act, Unit(DENSE + FFN_UNITS - 1))

            act.wait_ge(zero_ready, 1)
            nc.scalar.activation(top[:, 0, 0:1], zero[:, 0:1].bitcast(F32), ACT.Exp)
            mixer(0)
            next_operand(1, 2, DENSE, 1)
            dense()
            next_operand(2, 3, WIN[1], 2)
            mixer(1)
            next_operand(3, ROUTER, MOE, 1)
            act.wait_ge(lg_ready, 1)
            act.wait_ge(x_rstd, 4)
            for t in range(NT):
                nc.scalar.activation(ra[:, t], ra[:, t], ACT.Exp, scale=rsx[:, t:t + 1]).then_inc(lg_exp, 1)

            def split_gathered(k):
                for j in range(2):
                    act.wait_ge(xg_psum, 2 * k + j + 1)
                    nc.scalar.copy(xgh[:, 4 * j:4 * j + 4, :],
                                   bank[1 + 2 * j][:, :].rearrange("p (c s) -> p c s", c=4)).then_inc(xgh_ready, 1)

            def copy_onehot(k):
                act.wait_ge(ohT_psum, k + 1)
                nc.scalar.copy(onehotT[:, :], bank[5][:, 0:NT * P]).then_inc(ohT_ready, 1)

            def blocks(base, rounds, turns, k, follows):
                kb = k * NFB + NT * NFB
                with act.Fori(1, NFB) as f:
                    step(base + 4, rounds + (f - 1) * 6, turns + (f - 1), kb + f, 1)
                copy_onehot(k)
                round_unit(act, Unit(base + FFN_UNITS - 2, rounds, turns))
                if follows:
                    split_gathered(k + 1)
                split_g(kb + NFB - 1, 1, 1)
                round_unit(act, Unit(base + FFN_UNITS - 1, rounds, turns))
                if follows:
                    for n in range(3):
                        round_unit(act, Unit(base + FFN_UNITS + n, rounds, turns))
                for j in range(2):
                    act.wait_ge(used, base + rounds + FFN_UNITS - 1 + j)
                    nc.scalar.copy(ygh[:, 4 * j:4 * j + 4, :],
                                   bank[6 + j][:, :].rearrange("p (c n) -> p c n", c=4)).then_inc(ygh_ready, 1)
                if follows:
                    round_unit(act, Unit(base + FFN_UNITS + 3, rounds, turns))
                    silu(base + rounds + FFN_UNITS + 2, kb + NFB, 1)

            def experts(base, k0):
                split_gathered(k0)
                for n in range(0 if k0 else SPL, 4):
                    round_unit(act, Unit(base + n))
                silu(base + 2, k0 * NFB + NT * NFB, 1)
                with act.Fori(0, NE - 1) as e:
                    blocks(base, e * FFN_UNITS, e * (FFN_UNITS // RAW), k0 + e, True)
                last = (NE - 1) * FFN_UNITS
                blocks(base + last, 0, 0, k0 + NE - 1, False)

            experts(MOE, 0)
            act.wait_ge(route_ready, 1)
            more = act.value_load(flag[0:1, 0:1], min_val=0, max_val=1)
            with act.If(more > 0):
                experts(MOE2, NE)

        @block.vector
        def _(dve):
            V = nc.vector
            count = [0]

            def link(ins):
                count[0] += 1
                ins.then_inc(dve_order, 1)
                dve.wait_ge(dve_order, count[0])

            def settle(*ins):
                for i in ins:
                    count[0] += 1
                    i.then_inc(dve_order, 1)
                dve.wait_ge(dve_order, count[0])

            def tt(o, a, b, op):
                return V.tensor_tensor(o, a, b, op)

            def split_lo(k, gain, chunks=range(KC)):
                for c in chunks:
                    dve.wait_ge(xTh_ready, bank_turned(k, c))
                    V.scalar_tensor_tensor(xTl[:, c, :], xT_bank(k, c), gain_col(gain, c), xTh[:, c, :].bitcast(F32), ALU.mult,
                                           ALU.subtract).then_inc(xTl_ready, 1)

            def take(k, chunks):
                if k != ROUTER:
                    split_lo(k, k, chunks)
                    return
                dve.wait_ge(xT_psum, bank_turned(k, chunks[2]))
                for c in chunks[2:4]:
                    V.tensor_scalar(xTf[:, c, :], xT_bank(k, c), gain_col(k, c), None, ALU.mult).then_inc(xTf_dve, 1)

            def rope(q, cos, sin, scr):
                a, b = q[..., 0:8] if len(q.shape) == 2 else q[:, :, :, 0:8], q[..., 8:16] if len(q.shape) == 2 else q[:, :, :, 8:16]
                settle(tt(scr[0], a, cos, ALU.mult), tt(scr[1], b, sin, ALU.mult),
                       tt(scr[2], a, sin, ALU.mult), tt(scr[3], b, cos, ALU.mult))
                return tt(a, scr[0], scr[1], ALU.subtract), tt(b, scr[2], scr[3], ALU.add)

            def mixer(L):
                units = [Unit(WIN[L] + n) for n in range(W_IN_UNITS)]
                if L == 0:
                    dve.wait_ge(rowsT_psum, 1)
                    V.tensor_copy(cols[:, :], bank[1][:, 0:N_ROWS]).then_inc(cols_ready, 1)
                    dve.wait_ge(cols_ready, 1)
                    for h in range(2):
                        split_lo(0, 0, range(4 * h, 4 * h + 4))
                        rest_unit(dve, units[h])
                    rest_unit(dve, units[2])
                for n in range(SPL, W_IN_UNITS):
                    rest_unit(dve, units[n], in_words(n))
                    if n == 5:
                        dve.wait_ge(sguT_psum, L + 1)
                        tt(sgT[:], bank[4][:, :].rearrange("p (g t) -> p g t", g=NH), bc(C("triu"), 1, NH),
                           ALU.mult).then_inc(sguT_ready, 1)
                wout = [Unit(WOUT[L] + n) for n in range(W_OUT_UNITS)]
                if L == 0:
                    dve.wait_ge(s_tables, 16)
                def scores(i):
                    t = i % 2
                    dve.wait_ge(a_s, 4 * L + i + 1)
                    if 4 * L + i >= 2:
                        dve.wait_ge(a_T, 6 * (L if i >= 2 else L - 1) + [4, 6, 1, 3][i])
                    b0 = 2 * (i % 2)
                    if t == 0:
                        link(tt(sc[:, 0, :, 0:P], bank[b0][:, :].rearrange("p (h k) -> p h k", h=NH), bc(C("causal"), 1, NH), ALU.add))
                    else:
                        done = []
                        for j in range(2):
                            src = bank[b0 + j][:, :].rearrange("p (h k) -> p h k", h=2)
                            done.append(V.tensor_copy(sc[:, 1, 2 * j:2 * j + 2, 0:P], src[:, :, 0:P]))
                            done.append(tt(sc[:, 1, 2 * j:2 * j + 2, P:S], src[:, :, P:S], bc(C("causal"), 1, 2), ALU.add))
                        settle(*done)
                    V.tensor_reduce(mx[:, i, :], sc[:, i % 2, :, 0:P * (t + 1)], AX_X, ALU.max, negate=True).then_inc(a_max, 1)

                dve.wait_ge(pr_ready, 10 * L + 4)
                for t in range(NT):
                    V.tensor_copy(kd[:, t], bc(pr[:, t, KCM:KCM + 2 * HD].rearrange("p (j d) -> p j d", j=2), 2, 2)).then_inc(kd_ready, 1)
                a = tt(tmp[:, :, 0:4, :].rearrange("p t h d -> p t (h d)"), pr[:, :, 0:GW], pr[:, :, 0:GW], ALU.mult)
                b = tt(tmp[:, :, 4, :], pr[:, :, KS:KS + HD], pr[:, :, KS:KS + HD], ALU.mult)
                c = tt(tmp[:, :, 5, :], pr[:, :, KW:KW + HD], pr[:, :, KW:KW + HD], ALU.mult)
                settle(a, b, c)
                V.tensor_reduce(ss[:, :, 0:6], tmp[:], AX_X, ALU.add).then_inc(qk_ss, 1)
                dve.wait_ge(s_lay[L], LAY_LOADED)
                link(V.tensor_scalar(g6[:, 0:NH, :], g6[:, 0:NH, :], HD ** -0.5, None, ALU.mult))
                dve.wait_ge(kdT_psum, L + 1)
                peT = cols[:, PE_ROW + L * 32:PE_ROW + (L + 1) * 32].rearrange("p (k a) -> p k a", k=2)
                for s in range(2):
                    half = slice(s * HD, (s + 1) * HD)
                    for hi in range(2):
                        src = bank[4][half, :].rearrange("p (j n a two) -> p j n a two", j=2, n=16, two=2)[:, :, hi:hi + NCMP, :, s]
                        dst = kvb[half, :, 8 * hi:8 * hi + 8, 0:NCMP].rearrange("p j a n -> p j n a")
                        for j in range(2):
                            tt(dst[:, j], src[:, j], bc(peT[half, j, 8 * hi:8 * hi + 8], 1, NCMP), ALU.add).then_inc(kvb_ready, 1)
                dve.wait_ge(qk_rstd, 2 * (L + 1))
                a = tt(qk[:, :, 0:4, :], pr[:, :, 0:GW].rearrange("p t (h d) -> p t h d", h=NH), bc(rs[:, :, 0:4], 3, HD), ALU.mult)
                b = tt(qk[:, :, 4, :], pr[:, :, KS:KS + HD], bc(rs[:, :, 4], 2, HD), ALU.mult)
                c = tt(qk[:, :, 5, :], pr[:, :, KW:KW + HD], bc(rs[:, :, 5], 2, HD), ALU.mult)
                settle(a, b, c)
                qf = qk[:].rearrange("p t h d -> p t (h d)")
                link(tt(qf, qf, bc(g6[:].rearrange("p h d -> p (h d)"), 1, NT), ALU.mult))
                cos = bc(C("cos").rearrange("p (t f) -> p t f", t=NT), 2, 6)
                sin = bc(C("sin").rearrange("p (t f) -> p t f", t=NT), 2, 6)
                for i in rope(qk, cos, sin, rp):
                    i.then_inc(qk_ready, 1)
                for t in range(NT):
                    V.scalar_tensor_tensor(vn[:, t, :], pr[:, t, V0:V0 + GW], rs[:, t, 6:7], gsgu[:, :], ALU.mult,
                                           ALU.mult).then_inc(vn_ready, 1)
                z = xn[:, :, 2 * GW:3 * GW]
                dve.wait_ge(qk_ready, 2 * (L + 1))
                dve.wait_ge(pr_ready, 10 * (L + 1))
                link(tt(z, pr[:, :, CG:CG + GW], pr[:, :, HIN:HIN + GW], ALU.mult))
                for k in range(3):
                    tt(zk[k], z, bc(cw[:, k, :], 1, NT), ALU.mult).then_inc(z_ready, 1)
                dve.wait_ge(gate_e, L + 1)
                gf = gates[:].rearrange("p t h b -> p (t h b)")
                link(V.tensor_scalar(gf, gf, 1.0, None, ALU.add))
                link(V.reciprocal(gf, gf))
                rest_unit(dve, wout[0])
                dve.wait_ge(hid_psum, L + 1)
                V.tensor_copy(hraw, bank[4][0:NCMP, 0:2 * P]).then_inc(hraw_ready, 1)
                dve.wait_ge(hidT_psum, L + 1)
                link(V.tensor_copy(hx[:], bank[4][:, 2 * P:2 * P + 2 * CP].rearrange("p (j n) -> p j n", j=2)[:, :, 0:NCMP]))
                link(tt(hy[:], hx[:], hx[:], ALU.mult))
                link(V.tensor_scalar(hy[:], hy[:], 0.044715, 1.0, ALU.mult, ALU.add))
                link(tt(hz[:], hy[:], hx[:], ALU.mult))
                V.tensor_copy(hy[:], hz[:]).then_inc(gelu_in, 1)
                dve.wait_ge(gelu_e, L + 1)
                link(V.tensor_scalar(hy[:], hz[:], 1.0, None, ALU.add))
                link(V.reciprocal(hz[:], hy[:]))
                for j in range(2):
                    tt(hidp[:, j, :, 0:NCMP], bc(hx[:, j], 1, NH), bc(hz[:, j], 1, NH), ALU.mult).then_inc(hid_ready, 1)
                rest_unit(dve, wout[1])
                dve.wait_ge(kcvc_psum, L + 1)
                link(V.tensor_copy(kcs[:, 0, :], bank[4][0:CP, 128:192]))
                link(tt(kcs[:, 1, :], kcs[:, 0, :], kcs[:, 0, :], ALU.mult))
                V.tensor_reduce(ssc[:], kcs[:, 1, :], AX_X, ALU.add).then_inc(kc_ss, 1)
                tt(vbd[:], bc(bank[4][:, 192:256], 1, NH), bc(C("blk"), 2, HD), ALU.mult).then_inc(vbd_ready, 1)
                dve.wait_ge(kc_rstd, L + 1)
                link(V.scalar_tensor_tensor(kcs[:, 2, :], kcs[:, 0, :], rsc[:, 0:1], gkc[0:CP, :], ALU.mult, ALU.mult))
                for i in rope(kcs[:, 2, :], C("ccos", CP), C("csin", CP), [krp[:, i, :] for i in range(4)]):
                    i.then_inc(kc_ready, 1)
                dve.wait_ge(kcT_psum, L + 1)
                V.tensor_copy(kcT[:], bank[4][0:HD, 256:256 + CP]).then_inc(kcT_ready, 1)
                dve.wait_ge(conv_psum, L + 1)
                tt(xn[:, :, 3 * GW:4 * GW], bank[3][:, :].rearrange("p (t d) -> p t d", t=NT), pr[:, :, BG:BG + GW],
                   ALU.mult).then_inc(mix_done, 1)
                dve.wait_ge(cs_psum, L + 1)
                for t in range(NT):
                    i = tt(scc[:, t], bank[6][:, t * P:(t + 1) * P].rearrange("p (h n) -> p h n", h=NH),
                           bc(C("cmask")[:, t * CP:(t + 1) * CP], 1, NH), ALU.add)
                    count[0] += 1
                    i.then_inc(dve_order, 1)
                dve.wait_ge(dve_order, count[0])
                link(V.tensor_reduce(mxc[:], scc[:], AX_X, ALU.max))
                tt(scc[:], scc[:], bc(mxc[:], 3, CP), ALU.subtract).then_inc(cs_in, 1)
                scores(0)
                dve.wait_ge(cs_exp, L + 1)
                link(V.tensor_reduce(smc[:], scc[:], AX_X, ALU.add))
                a = V.reciprocal(smc[:], smc[:])
                b = tt(scc[:], scc[:], bc(C("cvalid").rearrange("p (t n) -> p t n", t=NT), 2, NH), ALU.mult)
                b.then_inc(cs_ready, 1)
                link(a)
                link(tt(smc[:], smc[:], gates[:, :, :, 0], ALU.mult))
                dve.wait_ge(poolY_psum, L + 1)
                tt(xn[:, :, 2 * GW:3 * GW], bank[2][:, :].rearrange("p (t d) -> p t d", t=NT), bc(psc[:, :], 1, NT),
                   ALU.mult).then_inc(mix_done, 1)
                dve.wait_ge(sgu_psum, L + 1)
                for g in range(NH):
                    V.scalar_tensor_tensor(xn[:, :, GW + g * HD:GW + (g + 1) * HD],
                                           bank[1][:, :].rearrange("p (t d) -> p t d", t=NT)[:, :, g * HD:(g + 1) * HD],
                                           cols[:, SGB_ROW + L * NH + g:SGB_ROW + L * NH + g + 1], pr[:, :, U0 + g * HD:U0 + (g + 1) * HD], ALU.add,
                                           ALU.mult).then_inc(mix_done, 1)
                rest_unit(dve, wout[2])
                scores(1)
                dve.wait_ge(co_psum, L + 1)
                for t in range(NT):
                    tt(xn[:, t, 0:GW].rearrange("p (h d) -> p h d", h=NH),
                       bank[7][:, t * GW:(t + 1) * GW].rearrange("p (h d) -> p h d", h=NH), bc(smc[:, t, :], 2, HD),
                       ALU.mult).then_inc(co_done, 1)
                def attend(i, meanwhile=None):
                    t, br = i % 2, i // 2
                    dve.wait_ge(a_exp, 4 * (4 * L + i + 1))
                    link(V.reciprocal(cf[:, i, :], sm[:, i, :]))
                    link(tt(cf[:, i, :], cf[:, i, :], gates[:, t, :, 1 + br], ALU.mult))
                    if i + 2 < 4:
                        scores(i + 2)
                    if meanwhile is not None:
                        meanwhile()
                    dve.wait_ge(a_o, 4 * L + i + 1)
                    dve.wait_ge(co_done, 2 * L + 2)
                    o = bank[6 + i % 2][:, 0:GW]
                    link(tt(ot[:, :].rearrange("p (h d) -> p h d", h=NH), o.rearrange("p (h d) -> p h d", h=NH),
                            bc(cf[:, i, :], 2, HD), ALU.mult))
                    if i >= 1:
                        dve.wait_ge(a_done, 4 * L + i)
                    tt(xn[:, t, 0:GW], xn[:, t, 0:GW], ot[:, :], ALU.add).then_inc(a_done, 1)

                k = 3 * L + 1
                def normalise_others():
                    for t in range(NT):
                        dve.wait_ge(y_rstd, 4 * L + t + 1)
                        y = xn[:, t, GW:4 * GW].rearrange("p (m d) -> p m d", m=3)
                        tt(y, y, bc(rsy[:, t, 1:4], 2, GW), ALU.mult).then_inc(yn_ready, 1)

                attend(0)
                attend(1, normalise_others)
                attend(2)
                split_lo(k, k, Y_ORDER[0:6])
                attend(3)
                for t in range(NT):
                    dve.wait_ge(y_rstd, 4 * L + 2 + t + 1)
                    V.tensor_scalar(xn[:, t, 0:GW], xn[:, t, 0:GW], rsy[:, t, 0:1], None, ALU.mult).then_inc(yn_ready, 1)
                split_lo(k, k, Y_ORDER[6:8])
                rest_unit(dve, wout[3])

                def add_mixed(b):
                    dve.wait_ge(used, WOUT[L] + 2 * b + 2)
                    for t in range(NT):
                        tt(x[:, t, b * FB:(b + 1) * FB], x[:, t, b * FB:(b + 1) * FB], bank[4 + 2 * b + t][:, :], ALU.add).then_inc(x_mid, 1)

                nxt, k = (DENSE, MOE)[L], 3 * L + 2
                add_mixed(0)
                rest_unit(dve, Unit(nxt))
                take(k, range(0, 4))
                rest_unit(dve, Unit(nxt + 1))
                add_mixed(1)
                if k != ROUTER:
                    rest_unit(dve, Unit(nxt + 2))
                take(k, range(4, 8))

            def times_h3(value, k, tiles, normed=True):
                dve.wait_ge(used, value)
                for t in range(tiles):
                    dve.wait_ge(silu_done, k * tiles + t + 1)
                    if normed:
                        tt(sg[:, t, :], sg[:, t, :], bank[2 + t][:, :], ALU.mult).then_inc(g_ready, 1)
                    else:
                        V.scalar_tensor_tensor(sg[:, t, :], bank[2 + t][:, :], rsx[:, t:t + 1], sg[:, t, :], ALU.mult,
                                               ALU.mult).then_inc(g_ready, 1)

            def split_g(k, tiles, at=0, last_dense=False):
                for t in range(tiles):
                    dve.wait_ge(gTh_ready, k * tiles + t + 1)
                    if last_dense:
                        lo, hi, b = gTl_last[:, :, t * P:(t + 1) * P], gTh_last[:, :, t * P:(t + 1) * P], bank[t]
                    else:
                        lo, hi, b = gTl[:, at + t], gTh[:, at + t], bank[4 + t]
                    tt(lo, b[:, :].rearrange("p (c s) -> p c s", c=4), hi.bitcast(F32), ALU.subtract).then_inc(gTl_ready, 1)

            def add_y(value, half):
                dve.wait_ge(used, value)
                for t in range(NT):
                    xs = x[:, t, half * FB:(half + 1) * FB]
                    tt(xs, xs, bank[(6 if half == 0 else 4) + t][:, :], ALU.add).then_inc(y_added, 1)

            def dense_step(f, add):
                base, r = DENSE + 4, (f - 1) * 6
                rest_unit(dve, Unit(base, r))
                times_h3(base + r - (2 if add else 0), f - 1, NT, False)
                rest_unit(dve, Unit(base + 1, r))
                if add:
                    add_y(base + r - 1, 0)
                rest_unit(dve, Unit(base + 2, r))
                if add:
                    add_y(base + r, 1)
                rest_unit(dve, Unit(base + 3, r))
                split_g(f - 1, NT)
                rest_unit(dve, Unit(base + 4, r))
                rest_unit(dve, Unit(base + 5, r))

            def dense():
                rest_unit(dve, Unit(DENSE + 3))
                dense_step(1, False)
                with dve.Fori(2, NFB) as f:
                    dense_step(f, True)
                end = DENSE + FFN_UNITS
                rest_unit(dve, Unit(end - 2))
                times_h3(end - 4, NFB - 1, NT, False)
                add_y(end - 3, 0)
                split_g(NFB - 1, NT, last_dense=True)
                rest_unit(dve, Unit(end - 1))
                add_y(end - 2, 1)
                add_y(end - 1, 0)
                rest_unit(dve, Unit(WIN[1]))
                split_lo(3, 3, range(0, 4))
                add_y(end, 1)
                rest_unit(dve, Unit(WIN[1] + 1))
                rest_unit(dve, Unit(WIN[1] + 2))
                split_lo(3, 3, range(4, 8))

            V.memset(hidp[:].rearrange("p j h n -> p (j h n)"), 0.0).then_inc(hp_ready, 1)
            V.memset(zero[:].bitcast(F32), 0.0).then_inc(zero_ready, 1)
            dve.wait_ge(hp_ready, 1)
            dve.wait_ge(s_const, 16)
            mixer(0)
            dense()
            mixer(1)
            dve.wait_ge(lgT_psum, 1)
            V.tensor_copy(lgT, bank[0][0:NE, 0:S]).then_inc(lgT_ready, 1)
            dve.wait_ge(lg_psum, 1)
            link(V.tensor_copy(lg[:], bank[0][:, S:S + NT * NE].rearrange("p (t e) -> p t e", t=NT)))
            settle(*[V.max(top[:, t, :], lg[:, t, :]) for t in range(NT)])
            m1, m2 = bc(top[:, :, 0], 2, NE), bc(top[:, :, 1], 2, NE)
            settle(tt(sel[:], lg[:], m2, ALU.is_gt), tt(rb[:], lg[:], m2, ALU.is_equal))
            tt(ra[:], lg[:], m1, ALU.subtract).then_inc(lg_ready, 1)
            link(V.tensor_reduce(rsc1[:], sel[:], AX_X, ALU.add))
            link(tt(posm[:, :, 0], rsc1[:], rb[:, :, 0], ALU.add))
            for e in range(1, NE):
                link(tt(posm[:, :, e], posm[:, :, e - 1], rb[:, :, e], ALU.add))
            link(V.scalar_tensor_tensor(rb[:], posm[:], 2.0, rb[:], ALU.is_le, ALU.mult))
            tt(sel[:], sel[:], rb[:], ALU.add).then_inc(sel_ready, 1)
            dve.wait_ge(x_rstd, 4)
            dve.wait_ge(s_gbc, 16)
            for t in range(NT):
                V.scalar_tensor_tensor(xn[:, t, :], x[:, t, :], rsx[:, t:t + 1], gbc, ALU.mult, ALU.mult).then_inc(xn_ready, 1)
            dve.wait_ge(pos_psum, 1)
            dve.wait_ge(sel_ready, 1)
            link(V.scalar_tensor_tensor(posm[:], bank[0][:, 0:NT * NE].rearrange("p (t e) -> p t e", t=NT), 1.0, sel[:],
                                        ALU.add, ALU.mult))

            def gates_and_flag():
                link(V.tensor_reduce(cnt[:, 0:1], bank[0][:, NT * NE:(NT + 1) * NE], AX_X, ALU.max))
                V.tensor_scalar(flag[:], cnt[:, 0:1], float(SLOTS), None, ALU.is_gt).then_inc(route_ready, 1)
                dve.wait_ge(lg_exp, NT)
                link(tt(ra[:], ra[:], sel[:], ALU.mult))
                link(V.tensor_reduce(rsc1[:], ra[:], AX_X, ALU.add))
                link(V.reciprocal(rsc1[:], rsc1[:]))
                link(tt(gate[:], ra[:], bc(rsc1[:], 2, NE), ALU.mult))

            def make_onehot(k, e, first_slot):
                for t in range(NT):
                    V.tensor_scalar(onehot[:, t, :], C("iota"), float(first_slot + 1), posm[:, t, ds(e, 1)], ALU.add,
                                    ALU.is_equal).then_inc(oh_ready, 1)

            def split_gathered(k):
                for j in range(2):
                    dve.wait_ge(xgh_ready, 2 * k + j + 1)
                    tt(xgl[:, 4 * j:4 * j + 4, :], bank[1 + 2 * j][:, :].rearrange("p (c s) -> p c s", c=4),
                       xgh[:, 4 * j:4 * j + 4, :].bitcast(F32), ALU.subtract).then_inc(xgl_ready, 1)

            def blocks(base, rounds, k, e, first_slot, follows):
                kb = k * NFB + NT * NFB
                rest_unit(dve, Unit(base + 4, rounds))
                times_h3(base + rounds + 4, kb, 1)
                for n in (5, 6, 7, 8):
                    rest_unit(dve, Unit(base + n, rounds))
                split_g(kb, 1)
                if follows:
                    dve.wait_ge(ohT_psum, k + 1)
                    make_onehot(k + 1, e + 1, first_slot)
                rest_unit(dve, Unit(base + 9, rounds))
                with dve.Fori(2, NFB) as f:
                    r = rounds + (f - 1) * 6
                    rest_unit(dve, Unit(base + 4, r))
                    times_h3(base + r + 2, kb + f - 1, 1)
                    for n in (5, 6, 7, 8):
                        rest_unit(dve, Unit(base + n, r))
                    split_g(kb + f - 1, 1)
                    rest_unit(dve, Unit(base + 9, r))
                times_h3(base + rounds + FFN_UNITS - 4, kb + NFB - 1, 1)
                rest_unit(dve, Unit(base + FFN_UNITS - 2, rounds))
                if follows:
                    split_gathered(k + 1)
                split_g(kb + NFB - 1, 1, 1)
                rest_unit(dve, Unit(base + FFN_UNITS - 1, rounds))
                if follows:
                    for n in range(3):
                        rest_unit(dve, Unit(base + FFN_UNITS + n, rounds))
                for j in range(2):
                    dve.wait_ge(ygh_ready, 2 * k + j + 1)
                    tt(ygl[:, 4 * j:4 * j + 4, :], bank[6 + j][:, :].rearrange("p (c n) -> p c n", c=4),
                       ygh[:, 4 * j:4 * j + 4, :].bitcast(F32), ALU.subtract).then_inc(ygl_ready, 1)
                if follows:
                    rest_unit(dve, Unit(base + FFN_UNITS + 3, rounds))
                for j in range(2):
                    for t in range(NT):
                        dve.wait_ge(sc_psum, 4 * k + 2 * j + t + 1)
                        xs = x[:, t, j * FB:(j + 1) * FB]
                        b = bank[[1, 3, 4, 5][2 * j + t]]
                        V.scalar_tensor_tensor(xs, b[:, :], gate[:, t, ds(e, 1)], xs, ALU.mult, ALU.add).then_inc(sc_done, 1)

            def experts(base, k0, first_slot):
                make_onehot(k0, 0, first_slot)
                if k0 == 0:
                    gates_and_flag()
                    rest_unit(dve, Unit(base + 2))
                split_gathered(k0)
                for n in range(0 if k0 else SPL, 4):
                    rest_unit(dve, Unit(base + n))
                with dve.Fori(0, NE - 1) as e:
                    blocks(base, e * FFN_UNITS, k0 + e, e, first_slot, True)
                blocks(base + (NE - 1) * FFN_UNITS, 0, k0 + NE - 1, NE - 1, first_slot, False)

            experts(MOE, 0, 0)
            dve.wait_ge(route_ready, 1)
            more = dve.value_load(flag[0:1, 0:1], min_val=0, max_val=1)
            with dve.If(more > 0):
                experts(MOE2, NE, SLOTS)
            V.tensor_copy(cnt[:, 1:2], rsx[:, 0:1]).then_inc(s_done, 1)

        @block.tensor
        def _(pe):
            T = nc.tensor

            def turn_y(k, chunks, value):
                pe.wait_ge(yn_ready, value)
                for c in chunks:
                    for t in range(NT):
                        i = T.transpose(xT_bank(k, c)[:, t * P:(t + 1) * P], xn[:, t, c * P:(c + 1) * P], ident)
                    i.then_inc(xT_psum, 1)

            def turn_x(k, h):
                pe.wait_ge(*x_half(k, h))
                for c in range(4 * h, 4 * h + 4):
                    for t in range(NT):
                        i = T.transpose(xT_bank(k, c)[:, t * P:(t + 1) * P], x[:, t, c * P:(c + 1) * P], ident)
                    i.then_inc(xT_psum, 1)

            def product(L0, n_units, k, bank_of, width_of, half_of=lambda n: n % 2, midway=None):
                for n in range(n_units):
                    u = Unit(L0 + n)
                    whole = width_of(n) != FB
                    w = width_of(n)
                    chunks = list(range(KC)) if whole else list(range(4 * half_of(n), 4 * half_of(n) + 4))
                    pe.wait_ge(s_lo, u.n + 1)
                    wh = u.hi[:, 0:len(chunks) * w].rearrange("p (c n) -> p c n", n=w)
                    wl = u.lo[:, 0:len(chunks) * w].rearrange("p (c n) -> p c n", n=w)
                    for i, c in enumerate(sorted(chunks, key=lambda c: turned(k, c))):
                        j = chunks.index(c)
                        first, last = (n % 2 == 0 or whole) and i == 0, (n % 2 == 1 or whole) and i == len(chunks) - 1
                        if n < 2 or whole:
                            pe.wait_ge(xTl_ready, turned(k, c))
                        for t in range(NT):
                            mm = three_passes(bank_of(n, t)[:, 0:w], xTh[:, c, t * P:(t + 1) * P], xTl[:, c, t * P:(t + 1) * P],
                                              wh[:, j, :], wl[:, j, :], first, last)
                        if midway is not None and n == 0 and i == 1:
                            midway()
                    mm.then_inc(used, 1)
                    yield n

            def keep_warm(n, b=3):
                for _ in range(n):
                    T.matmul(bank[b][:, :], zero[:, :], bc(zero[:, :], 1, 4), start=True, stop=True)

            def mixer(L):
                if L == 0:
                    pe.wait_ge(s_const, 16)
                    pe.wait_ge(s_rows, 16 * 5)
                    T.transpose(bank[1][:, 0:N_ROWS], rows, ident[0:N_ROWS, 0:N_ROWS]).then_inc(rowsT_psum, 1)
                    for h in range(2):
                        turn_x(0, h)
                    pe.wait_ge(cols_ready, 1)
                for n in product(WIN[L], W_IN_UNITS, 3 * L, lambda n, t: bank[2 * ((n // 2) % 2) + t],
                                 lambda n: FB if n < W_IN_UNITS - 1 else D_IN - 4 * FB,
                                 midway=(lambda: turn_x(3, 1)) if L else None):
                    if n % 2 and n >= 3:
                        pe.wait_ge(pr_ready, 10 * L + n - 1)
                    if n == 3:
                        pe.wait_ge(s_sgw, 16 * (L + 1))
                        for g in range(NH):
                            i = T.transpose(bank[4][:, g * P:(g + 1) * P], sgw[:, g, :], ident)
                        i.then_inc(sguT_psum, 1)
                    if n == W_IN_UNITS - 2:
                        pe.wait_ge(sguT_ready, L + 1)
                        for t in range(NT):
                            pe.wait_ge(kd_ready, 2 * L + t + 1)
                            for j in range(2):
                                i = T.transpose(bank[4][:, j * S + t * P:j * S + (t + 1) * P], kd[:, t, j].rearrange("p a d -> p (a d)"), ident)
                        i.then_inc(kdT_psum, 1)
                pe.wait_ge(s_lay[L], LAY_LOADED)
                pe.wait_ge(kvb_ready, 8 * (L + 1))
                for j in range(2):
                    for a in range(16):
                        i = T.matmul(bank[4][0:NCMP, j * P:(j + 1) * P], kvb[:, j, a, 0:NCMP], w1c[:, j, a, :],
                                     start=(a == 0), stop=(a == 15))
                i.then_inc(hid_psum, 1)
                pe.wait_ge(qk_ready, 2 * (L + 1))
                for h in range(6):
                    for t in range(NT):
                        i = T.transpose(bank[[6, 7, 5][h // 2]][0:HD, (h % 2) * S + t * P:(h % 2) * S + (t + 1) * P],
                                        qk[:, t, h, :], ident)
                    if h % 2:
                        i.then_inc(qkT_psum, 1)
                    if h == 1:
                        pe.wait_ge(hraw_ready, L + 1)
                        for j in range(2):
                            i = T.transpose(bank[4][:, 2 * P + j * CP:2 * P + j * CP + NCMP], hraw[:, j * P:(j + 1) * P],
                                            ident[0:NCMP, 0:NCMP])
                        i.then_inc(hidT_psum, 1)
                pe.wait_ge(pr_ready, 10 * (L + 1))
                if L == 0:
                    pe.wait_ge(s_tables, 16)
                band = C("band").rearrange("p (m g t) -> p m g t", m=3, g=4)
                for g in range(4):
                    o = bank[g // 2][0:HD, (g % 2) * S:(g % 2 + 1) * S]
                    w = [pr[:, t, PIN + g * HD:PIN + (g + 1) * HD] for t in range(NT)]
                    T.matmul(o[:, 0:P], w[0], band[:, 0, g, :], start=True, stop=True)
                    T.matmul(o[:, P:S], w[0], band[:, 1, g, :], start=True, stop=False)
                    i = T.matmul(o[:, P:S], w[1], band[:, 2, g, :], start=False, stop=True)
                    if g % 2:
                        i.then_inc(dlt_psum, 1)
                pe.wait_ge(hid_ready, 2 * (L + 1))
                T.matmul(bank[4][0:CP, 128:192], hidp[:, 0, 0, :], w2c[:, 0, :], start=True, stop=True)
                T.matmul(bank[4][:, 192:256], hidp[:, 1].rearrange("p h n -> p (h n)"), w2c[:, 1, :], start=True,
                         stop=True).then_inc(kcvc_psum, 1)
                pe.wait_ge(z_ready, 3 * (L + 1))
                sh = C("shift").rearrange("p (k t) -> p k t", k=4)
                for t in range(NT):
                    o = bank[3][:, t * GW:(t + 1) * GW]
                    T.matmul(o, ident, zk[2][:, t, :], start=True, stop=False)
                    T.matmul(o, sh[:, 0, :], zk[1][:, t, :], start=False, stop=False)
                    i = T.matmul(o, sh[:, 1, :], zk[0][:, t, :], start=False, stop=(t == 0))
                    if t:
                        T.matmul(o, sh[:, 2, :], zk[1][:, 0, :], start=False, stop=False)
                        i = T.matmul(o, sh[:, 3, :], zk[0][:, 0, :], start=False, stop=True)
                i.then_inc(conv_psum, 1)

                def scores(i):
                    t, b0 = i % 2, 2 * (i % 2)
                    if i >= 2:
                        pe.wait_ge(a_max, 4 * L + i - 1)
                    for h in range(NH):
                        n = P * (t + 1)
                        b = bank[b0 + h * n // 512]
                        mm = T.matmul(b[:, h * n % 512:h * n % 512 + n], qT[:, h // 2, h % 2, t * P:(t + 1) * P],
                                      kT[:, i // 2, 0:n], start=True, stop=True)
                    mm.then_inc(a_s, 1)

                def turn_probs(i):
                    pe.wait_ge(a_exp, 4 * (4 * L + i + 1))
                    if i:
                        pe.wait_ge(a_Tr, 6 * L + [0, 1, 3, 4][i])
                    for kt in range(i % 2 + 1):
                        for h in range(NH):
                            mm = T.transpose(bank[4 + kt][:, h * P:(h + 1) * P], sc[:, i % 2, h, kt * P:(kt + 1) * P], ident)
                        mm.then_inc(a_T, 1)

                pe.wait_ge(qkT_ready, 3 * (L + 1))
                pe.wait_ge(dlt_ready, 2 * (L + 1))
                pe.wait_ge(kc_ready, 2 * (L + 1))
                T.transpose(bank[4][0:HD, 256:256 + CP], kcs[:, 2, :], ident[0:CP, 0:CP]).then_inc(kcT_psum, 1)
                scores(0)
                pe.wait_ge(kcT_ready, L + 1)
                for t in range(NT):
                    for h in range(NH):
                        i = T.matmul(bank[6][:, (t * NH + h) * CP:(t * NH + h + 1) * CP], qT[:, h // 2, h % 2, t * P:(t + 1) * P], kcT[:, :],
                                     start=True, stop=True)
                i.then_inc(cs_psum, 1)
                for t in range(NT):
                    for g in range(4):
                        i = T.matmul(bank[2][:, t * GW + g * HD:t * GW + (g + 1) * HD], dlt[:, g // 2, g % 2, t * P:(t + 1) * P], pw[HD:P, g, :],
                                     start=True, stop=True)
                i.then_inc(poolY_psum, 1)
                pe.wait_ge(vn_ready, 2 * (L + 1))
                for t in range(NT):
                    for g in range(NH):
                        i = T.matmul(bank[1][:, t * GW + g * HD:t * GW + (g + 1) * HD], sgT[:, g, :], vn[:, t, g * HD:(g + 1) * HD],
                                     start=True, stop=True)
                i.then_inc(sgu_psum, 1)
                pe.wait_ge(mix_done, 6 * L + 2)
                scores(1)
                pe.wait_ge(cs_ready, L + 1)
                for t in range(NT):
                    i = T.transpose(bank[7][:, t * P:(t + 1) * P], scc[:, t].rearrange("p h n -> p (h n)"), ident)
                i.then_inc(cT_psum, 1)
                pe.wait_ge(vbd_ready, L + 1)
                turn_probs(0)
                pe.wait_ge(cT_ready, L + 1)
                for t in range(NT):
                    i = T.matmul(bank[7][:, t * GW:(t + 1) * GW], pcT[:, t, :], vbd[:].rearrange("p h d -> p (h d)"),
                                 start=True, stop=True)
                i.then_inc(co_psum, 1)
                def attend(i, meanwhile):
                    t, v0 = i % 2, (VS, VW)[i // 2]
                    if i:
                        turn_probs(i)
                    meanwhile()
                    pe.wait_ge(a_Tr, 6 * L + [0, 1, 3, 4][i] + t + 1)
                    if i >= 2:
                        pe.wait_ge(a_done, 4 * L + i - 1)
                    elif i == 1:
                        pe.wait_ge(co_done, 2 * L + 2)
                    for h in range(NH):
                        for kt in range(t + 1):
                            mm = T.matmul(bank[6 + i % 2][:, h * HD:(h + 1) * HD], pT[:, kt, h, :],
                                          pr[:, kt, v0:v0 + HD], start=(kt == 0), stop=(kt == t))
                    mm.then_inc(a_o, 1)

                k = 3 * L + 1

                def turn_others():
                    pe.wait_ge(a_max, 4 * L + 4)
                    turn_y(k, Y_ORDER[0:6], 4 * L + 2)

                attend(0, lambda: scores(2))
                attend(1, lambda: scores(3))
                pe.wait_ge(zero_ready, 1)
                pe.wait_ge(mix_done, 6 * (L + 1))
                attend(2, lambda: keep_warm(3, 1))
                keep_warm(4, 1)
                attend(3, turn_others)
                for n in product(WOUT[L], W_OUT_UNITS, k, lambda n, t: bank[4 + 2 * (n // 2) + t], lambda n: FB,
                                 lambda n: OUT_HALF[n]):
                    if n == 0:
                        turn_y(k, Y_ORDER[6:8], 4 * L + 4)
                    if n == 2:
                        turn_x(3 * L + 2, 0)

            def up(base, rounds, w, tiles, xh, xl, halves=range(2), midway=None):
                for h in halves:
                    u = Unit(base + 2 * w + h, rounds)
                    pe.wait_ge(s_lo, u.n + 1)
                    wh = u.hi[:, :].rearrange("p (c n) -> p c n", c=4)
                    wl = u.lo[:, :].rearrange("p (c n) -> p c n", c=4)
                    for j in range(4):
                        c = 4 * h + j
                        for t in range(tiles):
                            i = three_passes(bank[2 * w + t][:, :], xh[:, c, t * P:(t + 1) * P], xl[:, c, t * P:(t + 1) * P],
                                             wh[:, j, :], wl[:, j, :], c == 0, c == KC - 1)
                        if midway is not None and j == 1:
                            midway()
                    i.then_inc(used, 1)

            def turn(k, tiles, b0=4):
                for t in range(tiles):
                    pe.wait_ge(g_ready, k * tiles + t + 1)
                    for c in range(4):
                        i = T.transpose(bank[b0 + t][:, c * P:(c + 1) * P], sg[:, t, c * P:(c + 1) * P], ident)
                    i.then_inc(gT_psum, 1)

            def down(base, rounds, h, value, tiles, dense, last=True, at=0, midway=None, last_dense=False):
                u = Unit(base + h, rounds)
                pe.wait_ge(s_lo, u.n + 1)
                if h == 0:
                    pe.wait_ge(gTl_ready, value)
                wh = u.hi[:, :].rearrange("p (c n) -> p c n", c=4)
                wl = u.lo[:, :].rearrange("p (c n) -> p c n", c=4)
                for j in range(4):
                    for t in range(tiles):
                        o = bank[(6 if h == 0 else 4) + t] if dense else bank[6 + h]
                        if last_dense:
                            gh, gl = gTh_last[:, j, t * P:(t + 1) * P], gTl_last[:, j, t * P:(t + 1) * P]
                        else:
                            gh, gl = gTh[:, at + t, j, :], gTl[:, at + t, j, :]
                        i = three_passes(o[:, :], gh, gl, wh[:, j, :], wl[:, j, :],
                                         dense and j == 0, last and j == 3)
                    if midway is not None and j == 1:
                        midway()
                i.then_inc(used, 1)

            mixer(0)
            pe.wait_ge(xTl_ready, 8 * 2 + 4)
            up(DENSE, 0, 0, NT, xTh, xTl, (0,), lambda: turn_x(2, 1))
            pe.wait_ge(xTl_ready, 8 * 3)
            up(DENSE, 0, 0, NT, xTh, xTl, (1,))
            up(DENSE, 0, 1, NT, xTh, xTl)

            def dense_step(f, r, first=False, last=False):
                pe.wait_ge(silu_done, NT * f)
                up(DENSE + 4, r, 0, NT, xTh, xTl)
                if not first:
                    pe.wait_ge(y_added, 4 * (f - 1))
                turn(f - 1, NT)
                up(DENSE + 4, r, 1, NT, xTh, xTl)
                down(DENSE + 8, r, 0, f * NT, NT, True)
                if last:
                    turn(NFB - 1, NT, 0)
                down(DENSE + 8, r, 1, f * NT, NT, True)

            dense_step(1, 0, first=True)
            with pe.Fori(2, NFB - 1) as f:
                dense_step(f, (f - 1) * 6)
            dense_step(NFB - 1, (NFB - 2) * 6, last=True)
            end = DENSE + FFN_UNITS - 2
            pe.wait_ge(y_added, 4 * (NFB - 1) - 2)
            down(end, 0, 0, NFB * NT, NT, True, last_dense=True)
            pe.wait_ge(y_added, 4 * (NFB - 1))
            down(end, 0, 1, NFB * NT, NT, True, midway=lambda: turn_x(3, 0), last_dense=True)
            mixer(1)
            pe.wait_ge(zero_ready, 1)
            pe.wait_ge(s_rt, 16)
            for h in range(2):
                if h:
                    turn_x(ROUTER, 1)
                pe.wait_ge(xTf_act, 2 * (h + 1))
                pe.wait_ge(xTf_dve, 2 * (h + 1))
                for c in range(4 * h, 4 * h + 4):
                    i = T.matmul(bank[0][0:NE, 0:S], rt[:, c, :], xTf[:, c, :], start=(c == 0), stop=(c == KC - 1))
            i.then_inc(lgT_psum, 1)
            pe.wait_ge(lgT_ready, 1)
            for t in range(NT):
                i = T.transpose(bank[0][:, S + t * NE:S + (t + 1) * NE], lgT[:, t * P:(t + 1) * P], ident[0:NE, 0:NE])
            i.then_inc(lg_psum, 1)
            keep_warm(14)
            pe.wait_ge(sel_ready, 1)
            T.matmul(bank[0][:, 0:NE], C("before"), sel[:, 0, :], start=True, stop=True)
            T.matmul(bank[0][:, NE:2 * NE], C("ones"), sel[:, 0, :], start=True, stop=False)
            T.matmul(bank[0][:, NE:2 * NE], C("before"), sel[:, 1, :], start=False, stop=True)
            T.matmul(bank[0][:, 2 * NE:3 * NE], C("ones"), sel[:, 0, :], start=True, stop=False)
            T.matmul(bank[0][:, 2 * NE:3 * NE], C("ones"), sel[:, 1, :], start=False, stop=True).then_inc(pos_psum, 1)
            pe.wait_ge(zero_ready, 1)

            keep_warm(5)
            pe.wait_ge(xn_ready, NT)

            def gather(k):
                pe.wait_ge(oh_ready, 2 * (k + 1))
                for c in range(KC):
                    for t in range(NT):
                        i = T.matmul(bank[1 + 2 * (c // 4)][:, (c % 4) * P:(c % 4 + 1) * P], xn[:, t, c * P:(c + 1) * P],
                                     onehot[:, t, :], start=(t == 0), stop=(t == NT - 1))
                    if c % 4 == 3:
                        i.then_inc(xg_psum, 1)

            def scatter(k):
                for j in range(2):
                    for t in range(NT):
                        pe.wait_ge(ygl_ready, 2 * k + j + 1)
                        o = bank[[1, 3, 4, 5][2 * j + t]][:, :]
                        w = onehotT[:, t * P:(t + 1) * P]
                        T.matmul(o, w, ygh[:, 4 * j:4 * j + 4, :], start=True, stop=False)
                        T.matmul(o, w, ygl[:, 4 * j:4 * j + 4, :], start=False, stop=True).then_inc(sc_psum, 1)

            def turn_onehot(k):
                for t in range(NT):
                    i = T.transpose(bank[5][:, t * P:(t + 1) * P], onehot[:, t, :], ident)
                i.then_inc(ohT_psum, 1)

            def open_y():
                for h in range(2):
                    T.matmul(bank[6 + h][:, :], zero[:, :], bc(zero[:, :], 1, 4), start=True, stop=False)

            def blocks(base, rounds, k, follows):
                kb = k * NFB + NT * NFB
                with pe.Fori(1, NFB - 1) as f:
                    r = rounds + (f - 1) * 6
                    pe.wait_ge(silu_done, kb + f)
                    up(base + 4, r, 0, 1, xgh, xgl)
                    turn(kb + f - 1, 1)
                    up(base + 4, r, 1, 1, xgh, xgl)
                    for h in range(2):
                        down(base + 8, r, h, kb + f, 1, False, last=False)
                last = base + 4 + 6 * (NFB - 2)
                pe.wait_ge(silu_done, kb + NFB - 1)
                up(last, rounds, 0, 1, xgh, xgl)
                turn(kb + NFB - 2, 1)
                up(last, rounds, 1, 1, xgh, xgl)
                if follows:
                    gather(k + 1)
                down(last + 4, rounds, 0, kb + NFB - 1, 1, False, last=False)
                turn(kb + NFB - 1, 1)
                down(last + 4, rounds, 1, kb + NFB - 1, 1, False, last=False)
                for h in range(2):
                    down(last + 6, rounds, h, kb + NFB, 1, False, at=1)
                if follows:
                    pe.wait_ge(xgl_ready, 2 * (k + 2))
                    pe.wait_ge(silu_done, kb + NFB)
                    up(base + FFN_UNITS, rounds, 0, 1, xgh, xgl)
                pe.wait_ge(ohT_ready, k + 1)
                scatter(k)
                if follows:
                    open_y()
                    up(base + FFN_UNITS, rounds, 1, 1, xgh, xgl)
                    pe.wait_ge(sc_done, 4 * (k + 1))
                    turn_onehot(k + 1)

            def experts(base, k0):
                gather(k0)
                pe.wait_ge(xgl_ready, 2 * k0 + 1)
                if k0:
                    pe.wait_ge(silu_done, k0 * NFB + NT * NFB)
                else:
                    pe.wait_ge(route_ready, 1)
                up(base, 0, 0, 1, xgh, xgl, (0,))
                pe.wait_ge(xgl_ready, 2 * (k0 + 1))
                up(base, 0, 0, 1, xgh, xgl, (1,))
                open_y()
                up(base, 0, 1, 1, xgh, xgl)
                turn_onehot(k0)
                with pe.Fori(0, NE - 1) as e:
                    blocks(base, e * FFN_UNITS, k0 + e, True)
                blocks(base + (NE - 1) * FFN_UNITS, 0, k0 + NE - 1, False)

            experts(MOE, 0)
            more = pe.value_load(flag[0:1, 0:1], min_val=0, max_val=1)
            with pe.If(more > 0):
                experts(MOE2, NE)


_INS = ["x", "attn_norm_g", "w_in", "q_norm_g", "k_norm_g", "cmp_pe", "cmp_w1", "cmp_w2", "sgu_norm_g", "sgu_w",
        "sgu_b", "pool_w", "pool_scale", "conv_w", "mix_out_norm_g", "w_out", "ffn_norm_g", "ffn_w1", "ffn_w3",
        "ffn_w2", "router_w", "expert_w1", "expert_w3", "expert_w2"]


def kernel(**inputs):
    import concourse.bacc as bacc
    from concourse.bass_utils import run_bass_kernel_spmd

    nc = bacc.Bacc("TRN2", target_bir_lowering=False, num_devices=1)
    arrays, args = {}, []
    for name in _INS:
        a = np.ascontiguousarray(inputs[name])
        arrays[f"in_{name}"] = a
        args.append(nc.dram_tensor(f"in_{name}", a.shape, mybir.dt.from_np(a.dtype), kind="ExternalInput").ap())
    args[0] = args[0].rearrange("b s d -> (b s) d")
    arrays["in_consts"] = const_table()
    args.append(nc.dram_tensor("in_consts", arrays["in_consts"].shape, F32, kind="ExternalInput").ap())
    o = nc.dram_tensor("out_0", (1, S, D), F32, kind="ExternalOutput").ap()
    build(nc, *args, o.rearrange("b s d -> (b s) d"))
    r = run_bass_kernel_spmd(nc, [arrays], core_ids=[0])
    return r.results[0]["out_0"]
```
